# Optimizing a Trainium2 kernel written in Bass

```python
import jax
import jax.numpy as jnp
from jax import lax
import numpy as np

D_MODEL = 1024
BATCH = 1
SEQ = 256
DEPTH = 1

HEAD_DIM = 64
N_Q_HEADS = D_MODEL // HEAD_DIM
N_KV_HEADS = N_Q_HEADS // 8
WINDOW = 128
ROPE_THETA = 10000.0
ATTN_WIDTH = N_Q_HEADS * HEAD_DIM
KV_WIDTH = N_KV_HEADS * HEAD_DIM
POOL_WINDOWS = (2, 4, 8, 16)
POOL_WIDTH = D_MODEL // 2
POOL_GROUP = POOL_WIDTH // len(POOL_WINDOWS)
N_BRANCHES = 2
IN_WIDTH = ATTN_WIDTH + 2 * KV_WIDTH + POOL_WIDTH + N_BRANCHES * D_MODEL
IN_SPLITS = (ATTN_WIDTH, ATTN_WIDTH + KV_WIDTH, ATTN_WIDTH + 2 * KV_WIDTH,
             ATTN_WIDTH + 2 * KV_WIDTH + POOL_WIDTH)
N_EXPERTS = 32
TOP_K = 4
D_FF = D_MODEL
SWIGLU_LIMIT = 7.0
SWIGLU_ALPHA = 1.702
MOE_BLOCK = 256
RMS_EPS = 1e-5
MAX_POS_OFFSET = 1024

kernel_name = 'hybrid_swa_sink_pool_moe_block'

def rms_norm(x, g):
    xf = x.astype(jnp.float32)
    y = xf * lax.rsqrt(jnp.mean(xf * xf, axis=-1, keepdims=True) + RMS_EPS)
    return (y * g.astype(jnp.float32)).astype(x.dtype)

def apply_rope(t, positions):
    inv_freq = ROPE_THETA ** (-jnp.arange(0, HEAD_DIM, 2, dtype=jnp.float32) / HEAD_DIM)
    ang = positions.astype(jnp.float32)[..., None] * inv_freq
    cos = jnp.cos(ang)[:, :, None, :]
    sin = jnp.sin(ang)[:, :, None, :]
    tf = t.astype(jnp.float32)
    t1, t2 = tf[..., :HEAD_DIM // 2], tf[..., HEAD_DIM // 2:]
    out = jnp.concatenate([t1 * cos - t2 * sin, t2 * cos + t1 * sin], axis=-1)
    return out.astype(t.dtype)

def sliding_window_attention(q, k, v, sinks):
    B, S = q.shape[0], q.shape[1]
    nb = S // WINDOW
    grp = N_Q_HEADS // N_KV_HEADS
    qb = q.reshape(B, nb, WINDOW, N_KV_HEADS, grp, HEAD_DIM)

    def band(t):
        tb = t.reshape(B, nb, WINDOW, N_KV_HEADS, HEAD_DIM)
        prev = jnp.concatenate([jnp.zeros_like(tb[:, :1]), tb[:, :-1]], axis=1)
        return jnp.concatenate([prev, tb], axis=2)

    kk, vv = band(k), band(v)
    scale = HEAD_DIM ** -0.5
    s = jnp.einsum('bnqhgd,bnkhd->bnhgqk', qb, kk,
                   preferred_element_type=jnp.float32) * scale
    qi = jnp.arange(WINDOW)[:, None]
    kj = jnp.arange(2 * WINDOW)[None, :]
    dist = qi + WINDOW - kj
    band_mask = (dist >= 0) & (dist < WINDOW)
    key_valid = (jnp.arange(nb)[:, None] * WINDOW - WINDOW + jnp.arange(2 * WINDOW)[None, :]) >= 0
    mask = band_mask[None] & key_valid[:, None, :]
    s = jnp.where(mask[None, :, None, None], s, -jnp.inf)
    sink = sinks.astype(jnp.float32).reshape(1, 1, N_KV_HEADS, grp, 1, 1)
    m = jnp.maximum(jnp.max(s, axis=-1, keepdims=True), sink)
    p = jnp.exp(s - m)
    denom = jnp.sum(p, axis=-1, keepdims=True) + jnp.exp(sink - m)
    probs = (p / denom).astype(v.dtype)
    o = jnp.einsum('bnhgqk,bnkhd->bnqhgd', probs, vv)
    return o.reshape(B, S, N_Q_HEADS * HEAD_DIM)

def multiscale_pool(u):
    B, S, _ = u.shape
    uf = u.astype(jnp.float32)
    c = jnp.cumsum(uf, axis=1)
    t = jnp.arange(S)
    outs = []
    for gi, w in enumerate(POOL_WINDOWS):
        sl = slice(gi * POOL_GROUP, (gi + 1) * POOL_GROUP)
        cg = c[..., sl]
        lower = jnp.concatenate([jnp.zeros((B, w, POOL_GROUP), jnp.float32), cg[:, :S - w]], axis=1)
        cnt = jnp.minimum(t + 1, w).astype(jnp.float32)[None, :, None]
        outs.append((cg - lower) / cnt - uf[..., sl])
    return jnp.stack(outs, axis=2).astype(u.dtype)

def token_mixer(h, positions, w_in, b_in, attn_sinks, w_o_attn, b_o_attn,
                w_pool_mix, pool_scale, w_pool_up, w_out):
    B, S, _ = h.shape
    z = h @ w_in + b_in
    q, k, v, u, gate_logits = jnp.split(z, IN_SPLITS, axis=-1)
    q = apply_rope(q.reshape(B, S, N_Q_HEADS, HEAD_DIM), positions)
    k = apply_rope(k.reshape(B, S, N_KV_HEADS, HEAD_DIM), positions)
    v = v.reshape(B, S, N_KV_HEADS, HEAD_DIM)
    y_attn = sliding_window_attention(q, k, v, attn_sinks) @ w_o_attn + b_o_attn
    pooled = multiscale_pool(u)
    mixed = jnp.einsum('bsgc,gcd->bsgd', pooled, w_pool_mix).reshape(B, S, POOL_WIDTH)
    y_pool = (mixed * pool_scale) @ w_pool_up
    gates = jax.nn.sigmoid(gate_logits.astype(jnp.float32)).astype(h.dtype)
    gates = gates.reshape(B, S, N_BRANCHES, D_MODEL)
    merged = gates[:, :, 0] * y_attn + gates[:, :, 1] * y_pool
    return merged @ w_out

def moe_ffn(h, w_router, b_router, w_gate, b_gate, w_up, b_up, w_down, b_down):
    B, S, D = h.shape
    N = B * S
    hf = h.reshape(N, D)
    logits = (hf @ w_router + b_router).astype(jnp.float32)
    top_v, top_e = lax.top_k(logits, TOP_K)
    comb = jax.nn.softmax(top_v, axis=-1)
    M = N * TOP_K
    flat_e = top_e.reshape(M).astype(jnp.int32)
    flat_w = comb.reshape(M)
    flat_tok = jnp.arange(M, dtype=jnp.int32) // TOP_K
    order = jnp.argsort(flat_e)
    s_e, s_tok, s_w = flat_e[order], flat_tok[order], flat_w[order]
    sizes = jnp.bincount(flat_e, length=N_EXPERTS).astype(jnp.int32)
    starts = jnp.cumsum(sizes) - sizes
    padded = (sizes + MOE_BLOCK - 1) // MOE_BLOCK * MOE_BLOCK
    pends = jnp.cumsum(padded)
    pstarts = pends - padded
    dest = pstarts[s_e] + jnp.arange(M, dtype=jnp.int32) - starts[s_e]
    n_blocks = (M + N_EXPERTS * (MOE_BLOCK - 1) + MOE_BLOCK - 1) // MOE_BLOCK
    P = n_blocks * MOE_BLOCK
    row_tok = jnp.full((P,), N, jnp.int32).at[dest].set(s_tok)
    row_w = jnp.zeros((P,), jnp.float32).at[dest].set(s_w)
    block_e = jnp.searchsorted(pends, jnp.arange(n_blocks, dtype=jnp.int32) * MOE_BLOCK, side='right')
    block_e = jnp.minimum(block_e, N_EXPERTS - 1).astype(jnp.int32)
    h_pad = jnp.concatenate([hf, jnp.zeros((1, D), hf.dtype)], axis=0)
    xs = h_pad[row_tok].reshape(n_blocks, MOE_BLOCK, D)

    def expert_block(args):
        xb, e = args
        g = xb @ w_gate[e] + b_gate[e]
        u = xb @ w_up[e] + b_up[e]
        g = jnp.minimum(g, SWIGLU_LIMIT)
        u = jnp.clip(u, -SWIGLU_LIMIT, SWIGLU_LIMIT)
        a = g * jax.nn.sigmoid(SWIGLU_ALPHA * g) * (u + 1.0)
        return a @ w_down[e] + b_down[e]

    ys = lax.map(expert_block, (xs, block_e)).reshape(P, D)
    ys = ys * row_w.astype(ys.dtype)[:, None]
    out = jax.ops.segment_sum(ys, row_tok, num_segments=N + 1)[:N]
    return out.reshape(B, S, D)

def setup_inputs(seed: int = 0) -> dict:
    key = jax.random.key(seed)
    ks = jax.random.split(key, 24)
    f32 = jnp.float32
    L = DEPTH

    def nrm(k, shape, scale):
        return jax.random.normal(k, shape, f32) * scale

    x = nrm(ks[0], (BATCH, SEQ, D_MODEL), 1.0)
    offsets = jax.random.randint(ks[1], (BATCH, 1), 0, MAX_POS_OFFSET, dtype=jnp.int32)
    positions = offsets + jnp.arange(SEQ, dtype=jnp.int32)[None, :]
    return {
        'x': x,
        'positions': positions,
        'norm_mix_g': 1.0 + nrm(ks[2], (L, D_MODEL), 0.02),
        'w_in': nrm(ks[3], (L, D_MODEL, IN_WIDTH), D_MODEL ** -0.5),
        'b_in': nrm(ks[4], (L, IN_WIDTH), 0.02),
        'attn_sinks': nrm(ks[5], (L, N_Q_HEADS), 0.5),
        'w_o_attn': nrm(ks[6], (L, ATTN_WIDTH, D_MODEL), ATTN_WIDTH ** -0.5),
        'b_o_attn': nrm(ks[7], (L, D_MODEL), 0.02),
        'w_pool_mix': nrm(ks[8], (L, len(POOL_WINDOWS), POOL_GROUP, POOL_GROUP), POOL_GROUP ** -0.5),
        'pool_scale': 1.0 + nrm(ks[9], (L, POOL_WIDTH), 0.02),
        'w_pool_up': nrm(ks[10], (L, POOL_WIDTH, D_MODEL), POOL_WIDTH ** -0.5),
        'w_out': nrm(ks[11], (L, D_MODEL, D_MODEL), D_MODEL ** -0.5),
        'norm_ffn_g': 1.0 + nrm(ks[12], (L, D_MODEL), 0.02),
        'w_router': nrm(ks[13], (L, D_MODEL, N_EXPERTS), D_MODEL ** -0.5),
        'b_router': nrm(ks[14], (L, N_EXPERTS), 0.01),
        'w_gate': nrm(ks[15], (L, N_EXPERTS, D_MODEL, D_FF), D_MODEL ** -0.5),
        'b_gate': nrm(ks[16], (L, N_EXPERTS, D_FF), 0.02),
        'w_up': nrm(ks[17], (L, N_EXPERTS, D_MODEL, D_FF), D_MODEL ** -0.5),
        'b_up': nrm(ks[18], (L, N_EXPERTS, D_FF), 0.02),
        'w_down': nrm(ks[19], (L, N_EXPERTS, D_FF, D_MODEL), D_FF ** -0.5),
        'b_down': nrm(ks[20], (L, N_EXPERTS, D_MODEL), 0.02),
        'norm_final_g': 1.0 + nrm(ks[21], (D_MODEL,), 0.02),
    }

def reference(x, positions, norm_mix_g, w_in, b_in, attn_sinks, w_o_attn, b_o_attn,
              w_pool_mix, pool_scale, w_pool_up, w_out, norm_ffn_g, w_router, b_router,
              w_gate, b_gate, w_up, b_up, w_down, b_down, norm_final_g):
    for l in range(DEPTH):
        h = rms_norm(x, norm_mix_g[l])
        x = x + token_mixer(h, positions, w_in[l], b_in[l], attn_sinks[l], w_o_attn[l], b_o_attn[l],
                            w_pool_mix[l], pool_scale[l], w_pool_up[l], w_out[l])
        h = rms_norm(x, norm_ffn_g[l])
        x = x + moe_ffn(h, w_router[l], b_router[l], w_gate[l], b_gate[l], w_up[l], b_up[l],
                        w_down[l], b_down[l])
    return rms_norm(x, norm_final_g)


_drawn_inputs = setup_inputs


def setup_inputs(seed=0):
    import zlib

    import numpy as np

    out = dict(_drawn_inputs(seed))
    spreads = {}
    factors = {'attn_sinks': 3.992, 'b_gate': 6.766, 'b_up': 8.0, 'b_down': 6.384, 'norm_final_g': 2.747}
    for name, (base, spread) in spreads.items():
        noise = np.random.default_rng([zlib.crc32(name.encode()), seed]).standard_normal(out[name].shape)
        drawn = base * np.exp(spread * noise) if base else spread * noise
        out[name] = jnp.asarray(drawn.astype(out[name].dtype))
    for name, factor in factors.items():
        out[name] = (out[name] * factor).astype(out[name].dtype)
    return out
```

```python
from contextlib import ExitStack

import concourse.bass as bass
from concourse import mybir

D = 1024
S = 256
P = 128
NT = S // P
KT = D // P
HALF = 512
NH = D // HALF
DH = 64
NQ = D // DH
NKV = NQ // 8
NPAIR = NQ // 2
ROT = DH // 2
KVW = NKV * DH
POOLW = D // 2
NG = 4
WINDOWS = (2, 4, 8, 16)
IN_W = D + 2 * KVW + POOLW + 2 * D
EPS = 1e-5
LIMIT = 7.0
ALPHA = 1.702
NE = 32
TOPK = 4
CAP = 64
LEVELS = S // CAP - 1
OVER = 16
PAIRS = NE // 2
ENTRIES = NE + OVER + 2
CHUNKS = 24
RING = 12
BONUS = 5
CH_KT = 2
BPARTS = 3

CONST_COLS = {}
_at = 0
for _name, _width in (("ident", P), ("mask", 2 * P), ("band", NG * 3 * P), ("upper", P), ("slot_no", CAP),
                      ("bias_sel", NE), ("entry_no", OVER), ("upper32", NE), ("expert_no", 2),
                      ("inv_freq", ROT)):
    CONST_COLS[_name] = (_at, _at + _width)
    _at += _width
CONST_W = _at


def hybrid_block(nc, x, positions, norm_mix_g, w_in, b_in, attn_sinks, w_o_attn, b_o_attn, w_pool_mix,
                 pool_scale, w_pool_up, w_out, norm_ffn_g, w_router, b_router, w_gate, b_gate, w_up,
                 b_up, w_down, b_down, norm_final_g, consts, out):
    f32 = mybir.dt.float32
    bf16 = mybir.dt.bfloat16
    i32 = mybir.dt.int32
    ALU = mybir.AluOpType
    ACT = mybir.ActivationFunctionType
    AX = mybir.AxisListType

    ctx = ExitStack()
    with ctx:
        def sb(name, shape, dt=f32):
            return ctx.enter_context(nc.sbuf_tensor(name, shape, dt))

        def sem(name):
            return ctx.enter_context(nc.semaphore(name))

        ring = sb("ring", [P, RING * CH_KT * D])
        resid = sb("resid", [P, NT, D])
        gvec = sb("gvec", [P, D])
        const = sb("const", [P, CONST_W])
        hT = sb("hT", [P, KT, S])
        h = sb("h", [P, NT, D])
        zq = sb("zq", [P, NT, D])
        zu = sb("zu", [P, NT, POOLW])
        zg = sb("zg", [P, 2, NT, D])
        qT = sb("qT", [P, NPAIR, S])
        kpad = sb("kpad", [P, NT, 2 * NKV, P])
        kT = sb("kT", [P, NKV, 2, S])
        bias_zkv = sb("bias_zkv", [P, 3 * HALF + NT * 2 * KVW])
        bias_in = bias_zkv[:, 0:3 * HALF].rearrange("p (m n) -> p m n", m=3)
        zkv = bias_zkv[:, 3 * HALF:].rearrange("p (t n) -> p t n", t=NT)
        tmp = sb("tmp", [P, D + 2 * KVW])
        soft = sb("soft", [P, 5 * HALF])
        probs = soft[:, 0:3 * HALF].rearrange("p (m n) -> p m n", m=3)
        pT = soft[:, 3 * HALF:].rearrange("p (m n) -> p m n", m=2)
        wmix = sb("wmix", [P, NG, P])
        w_rt = sb("w_rt", [P, KT, NE])
        small = sb("small", [P, 672])
        pos_i = sb("pos_i", [P, NT], i32)
        sel_bf = sb("sel_bf", [P, NT, NE], bf16)
        upper_bf = sb("upper_bf", [P, P], bf16)
        ones_bf = sb("ones_bf", [P, P], bf16)
        ones_f = sb("ones_f", [NE, P])
        rank_tab = sb("rank_tab", [P, NT, ENTRIES])
        comb_tab = sb("comb_tab", [P, NT, ENTRIES])
        bsel_tab = sb("bsel_tab", [BPARTS * NE, ENTRIES], bf16)
        bsel = sb("bsel", [BPARTS * NE, 2, CAP], bf16)
        over_i = sb("over_i", [1, OVER + 2], i32)

        def cst(name, rows=P):
            a, b = CONST_COLS[name]
            return const[0:rows, a:b]

        xgT = qT[:, 0:4, :].rearrange("p a (b c) -> p (a b) c", c=P)
        gm = zg[:, 0, 0, :]
        sg = zg[:, 0, 1, :]
        um = zg[:, 1, 0, :]
        act_a = zg[:, 1, 1, :]
        aT = zq[:, 0, :].rearrange("p (k s) -> p k s", s=P)
        y_sb = zq[:, 1, :]
        pick = tmp[:, 0:2 * NT * CAP].rearrange("p (t x s) -> p t x s", t=NT, x=2)
        pickw = tmp[:, 256:512].rearrange("p (t x s) -> p t x s", t=NT, x=2)
        back = tmp[:, 512:768]
        bias3 = kT[:, :, :, :].rearrange("p a b s -> p (a b s)").bitcast(bf16)[0:BPARTS * NE, :]
        b_dn = kpad[0:NE, :, :, :].rearrange("p a b s -> p (a b s)")
        stage = probs[0:BPARTS * NE, 0:2, :].rearrange("p a n -> p (a n)")
        stage_r = pT[0:BPARTS * NE, :, :].rearrange("p a n -> p (a n)")
        stage_h = probs[0:BPARTS * NE, 2, :].bitcast(bf16)
        attnT = zq[:, :, :].rearrange("p t (k s) -> p (t k) s", s=S)
        pooledT = h[:, 0, :].rearrange("p (g s) -> p g s", s=S)
        mixedT = h[:, 1, :].rearrange("p (g s) -> p g s", s=S)
        pool_g = qT[:, :, :].rearrange("p (t k) s -> p t (k s)", t=NT)
        b_oa = tmp[:, 0:D]

        def piece(at, width):
            return small[:, at:at + width]

        ssq, ms, rms, rstd = piece(0, 2), piece(2, 2), piece(4, 2), piece(6, 2)
        pscale, sinks = piece(8, 4), piece(16, NQ)
        posf = piece(32, 2)
        ang = piece(64, 64).rearrange("p (t r) -> p t r", t=NT)
        rk = piece(128, 64).rearrange("p (t r) -> p t r", t=NT)
        cos_t = piece(192, 64).rearrange("p (t r) -> p t r", t=NT)
        sin_t = piece(256, 64).rearrange("p (t r) -> p t r", t=NT)
        mx, mneg, sume, esink, dens, rden = (piece(320 + 2 * n, 2) for n in range(6))
        b_rt = piece(336, NE)
        lg = piece(64, 64).rearrange("p (t e) -> p t e", t=NT)
        ex = piece(128, 64).rearrange("p (t e) -> p t e", t=NT)
        gt = piece(192, 64).rearrange("p (t e) -> p t e", t=NT)
        eq = piece(256, 64).rearrange("p (t e) -> p t e", t=NT)
        pre = piece(368, 64).rearrange("p (t e) -> p t e", t=NT)
        sel = piece(432, 64).rearrange("p (t e) -> p t e", t=NT)
        v8 = piece(496, 16).rearrange("p (t e) -> p t e", t=NT)
        neg_top, n_gt, need, wden, wrden = (piece(512 + 2 * n, 2) for n in range(5))
        over_in = small[0:NE, 522:525]
        over_cum = small[0:NE, 525:528]
        over_pos = small[0:NE, 528:531]
        over_n = small[0:NE, 531:532]
        oh = small[0:NE, 544:592].rearrange("p (l o) -> p l o", l=LEVELS)
        over_sel = small[0:NE, 592:608]
        over_shift = small[0:NE, 608:624]
        rank_cols = zu[0:NE, :, :].rearrange("p t n -> p (t n)")[:, 0:2 * S].rearrange("p (q s) -> p q s", q=2)

        ones_row = piece(640, NE)
        lgT = zu[0:NE, 1, 0:NT * P].rearrange("p (t s) -> p t s", t=NT)
        bank = [ctx.enter_context(nc.psum_tensor(f"bank{n}", [P, HALF], f32)) for n in range(8)]
        G, U, Y, M = bank[0:2], bank[2:4], bank[4:6], bank[6:8]

        cols = {"kv": (D, D + 2 * KVW), "q0": (0, HALF), "q1": (HALF, D),
                "u": (D + 2 * KVW, D + 2 * KVW + POOLW)}
        g0 = IN_W - 2 * D
        for n in range(4):
            cols[f"g{n}"] = (g0 + n * HALF, g0 + (n + 1) * HALF)
        order = ["kv", "q0", "q1", "u", "g0", "g1", "g2", "g3"]
        NIN = len(order)
        POOL_UP, WO, WOUT, MIXN = NIN, NIN + 1, NIN + 3, NIN + 5
        PLACES = RING * CH_KT * D // (KT * HALF)
        PW = KT * HALF

        def place(m):
            return ring[:, (m % PLACES) * PW:(m % PLACES + 1) * PW]

        def in_chunk(m):
            a, b = cols[order[m]]
            return place(m)[:, 0:KT * (b - a)].rearrange("p (k n) -> p k n", k=KT)

        def half_chunk(m):
            return place(m).rearrange("p (k n) -> p k n", k=KT)

        pool_up_sb = place(POOL_UP).rearrange("p (k n) -> p k n", k=NG)

        FIRST = 2

        def chunk_place(j):
            n = (j + FIRST) % RING
            return n, ring[:, n * CH_KT * D:(n + 1) * CH_KT * D].rearrange("p (k n) -> p k n", k=CH_KT)

        bonus_places = [m.rearrange("p (k n) -> p k n", k=CH_KT) for m in (
            bias_zkv[:, :], zq[:, :, :].rearrange("p t d -> p (t d)"), zg[:, 1, :, :].rearrange("p t d -> p (t d)"),
            soft[:, 0:CH_KT * D], hT[:, :, :].rearrange("p k s -> p (k s)"))]

        x_loaded = [sem(f"x_loaded{t}") for t in range(NT)]
        ident_loaded, small_loaded, wsmall_loaded = sem("ident_loaded"), sem("small_loaded"), sem("wsmall_loaded")
        g_mix_loaded, g_ffn_loaded, g_final_loaded = sem("g_mix_loaded"), sem("g_ffn_loaded"), sem("g_final_loaded")
        mix_loaded = [sem(f"mix_loaded{n}") for n in range(PLACES)]
        chunk_loaded = [sem(f"chunk_loaded{n}") for n in range(RING)]
        bonus_loaded = [sem(f"bonus_loaded{n}") for n in range(BONUS)]
        chunks_used = sem("chunks_used")
        bo_loaded, stage_loaded, bdn_loaded = sem("bo_loaded"), sem("stage_loaded"), sem("bdn_loaded")
        ones_ready, kpad_zeroed, bias_seq = sem("ones_ready"), sem("kpad_zeroed"), sem("bias_seq")
        bias3_ready = sem("bias3_ready")
        dve_seq, act_seq = sem("dve_seq"), sem("act_seq")
        sq_done, root_done, ms_ready, h_ready = sem("sq_done"), sem("root_done"), sem("ms_ready"), sem("h_ready")
        ht_done, ht_copied = sem("ht_done"), sem("ht_copied")
        z_done, z_ready = sem("z_done"), sem("z_ready")
        ang_ready, sin_ready = sem("ang_ready"), sem("sin_ready")
        krot_ready, qrot_ready = sem("krot_ready"), sem("qrot_ready")
        kt_done, kt_copied, qt_done, qt_copied = sem("kt_done"), sem("kt_copied"), sem("qt_done"), sem("qt_copied")
        pooled_done, pooled_copied, mixed_done, mixed_copied = (
            sem("pooled_done"), sem("pooled_copied"), sem("mixed_done"), sem("mixed_copied"))
        score_done, masked, max_ready, exp_done, probs_ready = (
            sem("score_done"), sem("masked"), sem("max_ready"), sem("exp_done"), sem("probs_ready"))
        pt_done, pt_copied, pv_done, o_copied = sem("pt_done"), sem("pt_copied"), sem("pv_done"), sem("o_copied")
        gates_ready, yp_done, ya_done, merged_ready = (
            sem("gates_ready"), sem("yp_done"), sem("ya_done"), sem("merged_ready"))
        mt_done, mt_copied, out_proj_done, x1_ready = (
            sem("mt_done"), sem("mt_copied"), sem("out_proj_done"), sem("x1_ready"))
        h2_ready, h2t_done, h2t_copied, logits_done, logits_copied, lt_done = (
            sem("h2_ready"), sem("h2t_done"), sem("h2t_copied"), sem("logits_done"),
            sem("logits_copied"), sem("lt_done"))
        top_ready, rexp_done, sel_ready, rank_done = (
            sem("top_ready"), sem("rexp_done"), sem("sel_ready"), sem("rank_done"))
        tabs_ready, cols_done, cols_ready, pos_done, oh_ready, over_done, over_ready = (
            sem("tabs_ready"), sem("cols_done"), sem("cols_ready"), sem("pos_done"), sem("oh_ready"),
            sem("over_done"), sem("over_ready"))
        pick_ready, pickw_ready, bsel_ready = sem("pick_ready"), sem("pickw_ready"), sem("bsel_ready")
        gathered, xgt_copied = sem("gathered"), sem("xgt_copied")
        gm_ready, sig_ready, um_ready, prod_ready, a_ready = (
            sem("gm_ready"), sem("sig_ready"), sem("um_ready"), sem("prod_ready"), sem("a_ready"))
        at_done, at_copied, back_done, back_copied = (
            sem("at_done"), sem("at_copied"), sem("back_done"), sem("back_copied"))
        y_copied, comb_done, comb_banks_free = (
            sem("y_copied"), sem("comb_done"), sem("comb_banks_free"))
        fin_sq, fin_root, fin_ms, fin_ready, stored = (
            sem("fin_sq"), sem("fin_root"), sem("fin_ms"), sem("fin_ready"), sem("stored"))

        def mixer_chunk_used(m):
            if m < NIN:
                return z_done, NT * (m + 1)
            if m == POOL_UP:
                return yp_done, NT * NH
            if m < WOUT:
                return ya_done, NT * (m - WO + 1)
            return out_proj_done, NT * (m - WOUT + 1)

        block = ctx.enter_context(nc.Block())

        UNITS = [(n, hp) for n in range(NT) for hp in range(NPAIR)]
        NU = len(UNITS)

        @block.sync
        def _(sp):
            for t in range(NT):
                sp.dma_start(resid[:, t, :], x[0, t * P:(t + 1) * P, :]).then_inc(x_loaded[t], 16)
                if t == 0:
                    sp.dma_start(gvec[:, :], norm_mix_g.to_broadcast([P, D])).then_inc(g_mix_loaded, 16)
            sp.dma_start(const[:, 0:P], consts[:, 0:P]).then_inc(ident_loaded, 16)

            def load_mixer(m):
                if m >= PLACES:
                    sp.wait_ge(*mixer_chunk_used(m - PLACES))
                if m < NIN:
                    a, b = cols[order[m]]
                    if m >= 3:
                        sp.wait_ge(z_ready, NT * (m - 2))
                    sp.dma_start(bias_in[:, m % 3, 0:b - a],
                                 b_in[:, a:b].to_broadcast([P, b - a])).then_inc(mix_loaded[m % PLACES], 16)
                    sp.dma_start(in_chunk(m), w_in[0, :, a:b].rearrange("(k p) n -> p k n", p=P)) \
                        .then_inc(mix_loaded[m % PLACES], 16)
                elif m == POOL_UP:
                    sp.dma_start(pool_up_sb, w_pool_up[0].rearrange("(k p) n -> p k n", p=P)) \
                        .then_inc(mix_loaded[m % PLACES], 16)
                else:
                    src, hh = (w_o_attn, m - WO) if m < WOUT else (w_out, m - WOUT)
                    sp.dma_start(half_chunk(m), src[0, :, hh * HALF:(hh + 1) * HALF]
                                 .rearrange("(k p) n -> p k n", p=P)).then_inc(mix_loaded[m % PLACES], 16)

            load_mixer(0)
            with nc.allow_non_contiguous_dma(reason="a few hundred words"):
                sp.dma_start(pos_i[:, :], positions[0].rearrange("(t p) -> p t", p=P)).then_inc(small_loaded, 16)
                sp.dma_start(pscale, pool_scale[0].rearrange("(g p) -> p g", p=P)).then_inc(small_loaded, 16)
            load_mixer(1)
            sp.dma_start(const[:, P:], consts[:, P:]).then_inc(small_loaded, 16)
            sp.dma_start(sinks, attn_sinks.to_broadcast([P, NQ])).then_inc(small_loaded, 16)
            sp.dma_start(b_rt, b_router.to_broadcast([P, NE])).then_inc(small_loaded, 16)
            load_mixer(2)
            sp.dma_start(wmix[:, :, :], w_pool_mix[0].rearrange("g c d -> c g d")).then_inc(wsmall_loaded, 16)
            sp.dma_start(w_rt[:, :, :], w_router[0].rearrange("(k p) e -> p k e", p=P)).then_inc(wsmall_loaded, 16)
            for m in range(3, MIXN):
                load_mixer(m)

            matrices = (w_gate, w_up, w_down)

            def load_chunk(j, expert_a, expert_b, bonus=None):
                which, piece_no, side = j // 8, j % 8 // 2, j % 2
                e = (expert_a, expert_b)[side]
                n, dst = chunk_place(j)
                signal = chunk_loaded[n]
                if bonus is not None:
                    dst, signal = bonus_places[bonus], bonus_loaded[bonus]
                rows = slice(piece_no * CH_KT * P, (piece_no + 1) * CH_KT * P)
                sp.dma_start(dst, matrices[which][0, bass.ds(e, 1), rows, :]
                             .rearrange("o (k p) n -> p (o k) n", p=P)).then_inc(signal, 16)

            def chunk_free(count):
                sp.wait_ge(chunks_used, count)
                sp.nop(nofuse=True)

            for j in range(RING):
                n = chunk_place(j)[0] // 2
                last = max(m for m in range(MIXN) if m % PLACES == n)
                sp.wait_ge(*mixer_chunk_used(last))
                load_chunk(j, 0, 1)
                if j == RING - 3:
                    sp.wait_ge(pv_done, NU)
                    load_chunk(RING, 0, 1, bonus=0)
                    sp.wait_ge(ya_done, NT * NH)
                    load_chunk(RING + 1, 0, 1, bonus=1)
                    sp.wait_ge(mt_done, NT * NH)
                    load_chunk(RING + 2, 0, 1, bonus=2)
                    sp.wait_ge(bias3_ready, 2)
                    load_chunk(RING + 3, 0, 1, bonus=3)
            sp.wait_ge(logits_done, NT)
            load_chunk(RING + 4, 0, 1, bonus=4)
            for j in range(RING + BONUS, CHUNKS):
                chunk_free(j - RING + 1)
                load_chunk(j, 0, 1)
            for j in range(RING):
                chunk_free(CHUNKS + j - RING + 1)
                load_chunk(j, 2, 3)
            with sp.Fori(1, PAIRS - 1) as i:
                for j in range(RING, CHUNKS):
                    chunk_free(i * CHUNKS + (j - RING + 1))
                    load_chunk(j, i * 2, i * 2 + 1)
                for j in range(RING):
                    chunk_free(i * CHUNKS + (CHUNKS + j - RING + 1))
                    load_chunk(j, i * 2 + 2, i * 2 + 3)
            for j in range(RING, CHUNKS):
                chunk_free((PAIRS - 1) * CHUNKS + j - RING + 1)
                load_chunk(j, NE - 2, NE - 1)

            sp.wait_ge(over_ready, 1)
            n_over = sp.value_load(over_i[0:1, OVER:OVER + 1], min_val=0, max_val=OVER)
            with sp.If(n_over > 0):
                with sp.Fori(0, OVER // 2) as k:
                    with sp.If(k * 2 < n_over):
                        expert_a = sp.value_load(over_i[0:1, bass.ds(k * 2, 1)], min_val=0, max_val=NE - 1)
                        expert_b = sp.value_load(over_i[0:1, bass.ds(k * 2 + 1, 1)], min_val=0, max_val=NE - 1)
                        for j in range(CHUNKS):
                            chunk_free((k + PAIRS) * CHUNKS + (j - RING + 1))
                            load_chunk(j, expert_a, expert_b)

            for t in range(NT):
                sp.wait_ge(fin_ready, t + 1)
                sp.dma_start(out[0, t * P:(t + 1) * P, :], h[:, t, :]).then_inc(stored, 16)
            sp.wait_ge(stored, 16 * NT)

        @block.tensor
        def _(pe):
            mm = nc.tensor.matmul
            ident = cst("ident")

            def transposes(dst, srcs, identity=ident):
                for n, src in enumerate(srcs):
                    last = nc.tensor.transpose(dst[:, n * P:(n + 1) * P], src, identity)
                return last

            mix_seen = [0] * PLACES

            def mix_arrived(m):
                mix_seen[m % PLACES] += 32 if m < NIN else 16
                pe.wait_ge(mix_loaded[m % PLACES], mix_seen[m % PLACES])

            pe.wait_ge(ident_loaded, 16)
            for t in range(NT):
                pe.wait_ge(h_ready, t + 1)
                for q in range(2):
                    transposes(bank[4 + 2 * t + q], [h[:, t, (4 * q + n) * P:(4 * q + n + 1) * P] for n in range(4)]) \
                        .then_inc(ht_done, 1)

            def project(m, t, kts=range(KT)):
                a, b = cols[order[m]]
                for k in kts:
                    last = mm(bank[2 * (m % 2) + t][:, 0:b - a], hT[:, k, t * P:(t + 1) * P], in_chunk(m)[:, k, :],
                              start=(k == 0), stop=(k == KT - 1))
                return last

            def project_all(m):
                mix_arrived(m)
                if m >= 2:
                    pe.wait_ge(z_ready, NT * (m - 1))
                for t in range(NT):
                    if m == 0:
                        pe.wait_ge(ht_copied, 2 * t + 2)
                    last = project(m, t)
                    last.then_inc(z_done, 1)

            project_all(0)
            project_all(1)
            pe.wait_ge(krot_ready, 1)
            for t in range(NT):
                transposes(bank[4 + t], [kpad[:, t, n, :] for n in range(2 * NKV)]).then_inc(kt_done, 1)
            project_all(2)
            project_all(3)
            pe.wait_ge(z_ready, NT * 4)
            pe.wait_ge(small_loaded, 16 * 5)
            band = cst("band").rearrange("p (g n) -> p g n", g=NG)
            for g in range(NG):
                dst = bank[6 + g // 2][:, (g % 2) * S:(g % 2 + 1) * S]
                mm(dst[:, 0:P], zu[:, 0, g * P:(g + 1) * P], band[:, g, 0:P], start=True, stop=True)
                mm(dst[:, P:S], zu[:, 0, g * P:(g + 1) * P], band[:, g, P:S], start=True, stop=False)
                mm(dst[:, P:S], zu[:, 1, g * P:(g + 1) * P], band[:, g, S:S + P], start=False, stop=True) \
                    .then_inc(pooled_done, 1)
            project_all(4)
            pe.wait_ge(pooled_copied, 2)
            pe.wait_ge(wsmall_loaded, 32)
            for g in range(NG):
                mm(bank[6 + g // 2][:, (g % 2) * S:(g % 2 + 1) * S], wmix[:, g, :], pooledT[:, g, :],
                   start=True, stop=True).then_inc(mixed_done, 1)
            pe.wait_ge(qrot_ready, 1)
            pe.wait_ge(kt_copied, 2)
            for q in range(4):
                if q < 2:
                    dst = bank[4 + q]
                else:
                    pe.wait_ge(mixed_copied, NG if q == 2 else NG)
                    dst = bank[4 + q]
                t, half = q // 2, q % 2
                transposes(dst, [zq[:, t, (4 * half + n) * P:(4 * half + n + 1) * P] for n in range(4)]) \
                    .then_inc(qt_done, 1)
            pe.wait_ge(qt_copied, 4)

            todo = [(m, t, k) for m in range(5, NIN) for t in range(NT) for k in range(KT)]
            per_step = -(-len(todo) // NU)

            def scores(s):
                n, hp = UNITS[s]
                if s >= 2:
                    pe.wait_ge(masked, s - 1)
                keys = P * (n + 1)
                mm(bank[4 + s % 2][:, 0:2 * keys], qT[:, hp, n * P:(n + 1) * P],
                   kT[:, hp // (NPAIR // NKV), :, 0:keys], start=True, stop=True).then_inc(score_done, 1)

            def probs_transposed(s):
                n, hp = UNITS[s]
                pe.wait_ge(probs_ready, s + 1)
                if s >= 1:
                    pe.wait_ge(pt_copied, s)
                transposes(bank[6], [probs[:, s % 3, c * P:(c + 1) * P] for c in range(2 * (n + 1))]) \
                    .then_inc(pt_done, 1)

            def outputs(s):
                n, hp = UNITS[s]
                g = hp // (NPAIR // NKV)
                pe.wait_ge(pt_copied, s + 1)
                if s >= 1:
                    pe.wait_ge(o_copied, s)
                for k in range(n + 1):
                    for par in range(2):
                        last = mm(bank[7][DH * par:DH * (par + 1), (s % 4) * P:(s % 4 + 1) * P],
                                  zkv[:, k, KVW + g * DH:KVW + (g + 1) * DH],
                                  pT[:, s % 2, (par * (n + 1) + k) * P:(par * (n + 1) + k + 1) * P],
                                  start=(k == 0), stop=(k == n), skip_group_check=True)
                last.then_inc(pv_done, 1)

            for s in range(NU + 3):
                if s < NU:
                    scores(s)
                if 2 <= s < NU + 2:
                    probs_transposed(s - 2)
                for m, t, k in todo[s * per_step:(s + 1) * per_step]:
                    if t == 0 and k == 0:
                        mix_arrived(m)
                        pe.wait_ge(z_ready, NT * (m - 1))
                    last = project(m, t, [k])
                    if k == KT - 1:
                        last.then_inc(z_done, 1)
                if s >= 3:
                    outputs(s - 3)

            mix_arrived(POOL_UP)
            pe.wait_ge(z_ready, NT * NIN)
            for t in range(NT):
                for hh in range(NH):
                    for g in range(NG):
                        last = mm(bank[2 * t + hh][:, :], mixedT[:, g, t * P:(t + 1) * P],
                                  pool_up_sb[:, g, hh * HALF:(hh + 1) * HALF], start=(g == 0), stop=(g == NG - 1))
                    last.then_inc(yp_done, 1)
            pe.wait_ge(o_copied, NU)
            for hh in range(NH):
                mix_arrived(WO + hh)
                for t in range(NT):
                    for k in range(KT):
                        last = mm(bank[4 + 2 * t + hh][:, :], attnT[:, k, t * P:(t + 1) * P],
                                  half_chunk(WO + hh)[:, k, :], start=(k == 0), stop=(k == KT - 1))
                    last.then_inc(ya_done, 1)
            for q in range(4):
                hh, t = q // 2, q % 2
                pe.wait_ge(merged_ready, q + 1)
                transposes(bank[2 * t + hh], [zg[:, 0, t, (4 * hh + n) * P:(4 * hh + n + 1) * P] for n in range(4)]) \
                    .then_inc(mt_done, 1)
            pe.wait_ge(mt_copied, 4)
            for hh in range(NH):
                mix_arrived(WOUT + hh)
                for t in range(NT):
                    for k in range(KT):
                        last = mm(bank[4 + 2 * t + hh][:, :], hT[:, k, t * P:(t + 1) * P],
                                  half_chunk(WOUT + hh)[:, k, :], start=(k == 0), stop=(k == KT - 1))
                    last.then_inc(out_proj_done, 1)

            for t in range(NT):
                pe.wait_ge(h2_ready, t + 1)
                for q in range(2):
                    transposes(bank[2 * t + q], [h[:, t, (4 * q + n) * P:(4 * q + n + 1) * P] for n in range(4)]) \
                        .then_inc(h2t_done, 1)
            for t in range(NT):
                pe.wait_ge(h2t_copied, 2 * t + 2)
                for k in range(KT):
                    last = mm(bank[4 + t][0:NE, 0:P], w_rt[:, k, :], hT[:, k, t * P:(t + 1) * P],
                              start=(k == 0), stop=(k == KT - 1))
                last.then_inc(logits_done, 1)
            for t in range(NT):
                pe.wait_ge(logits_copied, t + 1)
                nc.tensor.transpose(bank[6 + t][:, 0:NE], lgT[:, t, :], ident[0:NE, 0:NE]).then_inc(lt_done, 1)
            pe.wait_ge(ones_ready, 4)
            pe.wait_ge(sel_ready, 1)
            mm(bank[5][:, 0:NE], upper_bf[:, :], sel_bf[:, 0, :], start=True, stop=True)
            mm(bank[5][:, NE:2 * NE], ones_bf[:, :], sel_bf[:, 0, :], start=True, stop=False)
            mm(bank[5][:, NE:2 * NE], upper_bf[:, :], sel_bf[:, 1, :], start=False, stop=True)
            for t in range(NT):
                last = mm(bank[4][0:NE, 0:CAP], sel_bf[:, t, :], ones_bf[:, 0:CAP], start=(t == 0), stop=(t == NT - 1))
            last.then_inc(rank_done, 1)

            def gather(first=False):
                for k in range(KT):
                    for t in range(NT):
                        last = mm(M[k // 4][:, (k % 4) * P:(k % 4 + 1) * P], h[:, t, k * P:(k + 1) * P],
                                  pick[:, t, :, :], start=(t == 0), stop=(t == NT - 1))
                    if k % 4 == 3:
                        last.then_inc(gathered, 1)

            def overflow_places():
                pe.wait_ge(cols_ready, 1)
                mm(bank[5][0:NE, 0:LEVELS], cst("upper32", NE), over_in, start=True, stop=False)
                mm(bank[5][0:NE, 0:LEVELS], ones_f[:, 0:NE], over_cum, start=False, stop=True)
                mm(bank[5][0:1, 32:33], ones_f[:, 0:1], over_n, start=True, stop=True).then_inc(pos_done, 1)

            def overflow_columns():
                pe.wait_ge(oh_ready, 1)
                for t in range(NT):
                    mm(bank[5][:, 64 + t * OVER:64 + (t + 1) * OVER], rank_cols[:, 0, t * P:(t + 1) * P], over_sel,
                       start=True, stop=False)
                    mm(bank[5][:, 64 + t * OVER:64 + (t + 1) * OVER], ones_f[:, :], over_shift,
                       start=False, stop=True)
                    mm(bank[5][:, 128 + t * OVER:128 + (t + 1) * OVER], rank_cols[:, 1, t * P:(t + 1) * P], over_sel,
                       start=True, stop=True)
                mm(bank[5][0:1, 192:192 + OVER], cst("expert_no", NE)[:, 0:1], over_sel, start=True, stop=True) \
                    .then_inc(over_done, 1)

            pe.wait_ge(pick_ready, 1)
            gather()
            for q in range(2):
                for t in range(NT):
                    last = nc.tensor.transpose(bank[4][0:NE, (2 * q + t) * P:(2 * q + t + 1) * P],
                                               (rank_tab, comb_tab)[q][:, t, 0:NE], ident)
            last.then_inc(cols_done, 1)
            pe.wait_ge(bias3_ready, 2)

            def expert_pair(i, first=False):
                def weights(j):
                    n, src = chunk_place(j)
                    if first and RING <= j < RING + BONUS:
                        pe.wait_ge(bonus_loaded[j - RING], 16)
                        return bonus_places[j - RING]
                    skipped = any(chunk_place(RING + b)[0] == n for b in range(BONUS))
                    count = (16 if j < RING else 32) - (16 if skipped and not first else 0)
                    pe.wait_ge(chunk_loaded[n], i * 32 + count)
                    return src

                def layer(which, dst, lhs, after=None):
                    for c in range(4):
                        if after is not None:
                            after(c)
                        wa, wb = weights(8 * which + 2 * c), weights(8 * which + 2 * c + 1)
                        for k in range(CH_KT):
                            kt = c * CH_KT + k
                            for hh in range(NH):
                                for side, w in ((0, wa), (1, wb)):
                                    last = mm(dst[hh][side * CAP:(side + 1) * CAP, :],
                                              lhs[:, kt, side * CAP:(side + 1) * CAP],
                                              w[:, k, hh * HALF:(hh + 1) * HALF],
                                              start=(which == 2 and kt == 0), stop=(kt == KT - 1),
                                              skip_group_check=True)
                        last.then_inc(chunks_used, 2)

                def biases(dst, at):
                    for hh in range(NH):
                        mm(dst[hh][:, :], bsel[:, :, :].rearrange("p x s -> p (x s)"),
                           bias3[:, at + hh * HALF:at + (hh + 1) * HALF], start=True, stop=False,
                           skip_group_check=True)

                pe.wait_ge(bsel_ready, i + 1)
                biases(G, 0)
                layer(0, G, xgT, after=lambda c: pe.wait_ge(xgt_copied, i * 2 + 1 + c // 2) if c % 2 == 0 else None)
                if first:
                    overflow_places()
                else:
                    pe.wait_ge(comb_banks_free, i * 4)
                biases(U, D)
                layer(1, U, xgT)
                pe.wait_ge(pick_ready, i + 2)
                gather()
                if first:
                    overflow_columns()
                for hh in range(NH):
                    pe.wait_ge(a_ready, i * 2 + hh + 1)
                    transposes(G[hh], [act_a[:, (4 * hh + n) * P:(4 * hh + n + 1) * P] for n in range(4)]) \
                        .then_inc(at_done, 1)
                    if hh == 0:
                        pe.wait_ge(pickw_ready, i + 1)
                        for t in range(NT):
                            last = nc.tensor.transpose(
                                U[0][:, t * P:(t + 1) * P],
                                pickw[:, t, :, :].rearrange("p x s -> p (x s)"), ident)
                        last.then_inc(back_done, 1)
                if first:
                    pe.wait_ge(over_ready, 1)
                layer(2, Y, aT, after=lambda c: pe.wait_ge(at_copied, i * 2 + 1 + c // 2) if c % 2 == 0 else None)
                pe.wait_ge(back_copied, i + 1)
                pe.wait_ge(xgt_copied, i * 2 + 4)
                if first:
                    pe.wait_ge(bdn_loaded, 16)
                for t in range(NT):
                    for hh in range(NH):
                        sl = slice(hh * HALF, (hh + 1) * HALF)
                        if t == 0:
                            pe.wait_ge(y_copied, i * 2 + hh + 1)
                        last = mm((M, U)[t][hh][:, :], back[:, t * P:(t + 1) * P], y_sb[:, sl],
                                  start=True, stop=not first)
                        if first:
                            last = mm((M, U)[t][hh][:, :], rank_cols[:, 1, t * P:(t + 1) * P], b_dn[:, sl],
                                      start=False, stop=True)
                        last.then_inc(comb_done, 1)

            expert_pair(0, first=True)
            n_over = pe.value_load(over_i[0:1, OVER:OVER + 1], min_val=0, max_val=OVER)
            with pe.Fori(1, PAIRS) as i:
                expert_pair(i)
            with pe.If(n_over > 0):
                with pe.Fori(0, OVER // 2) as k:
                    with pe.If(k * 2 < n_over):
                        expert_pair(pe.snap(k + PAIRS))

        @block.scalar
        def _(act):
            def copy(dst, src):
                return nc.scalar.activation(dst, src, ACT.Copy)

            nc.scalar.preload_act_table(ACT.Sqrt)
            for t in range(NT):
                act.wait_ge(x_loaded[t], 16)
                nc.scalar.activation(h[:, t, :], resid[:, t, :], ACT.Square, accum_out=ssq[:, t:t + 1]) \
                    .then_inc(sq_done, 1)
                act.wait_ge(ms_ready, t + 1)
                nc.scalar.activation(rms[:, t:t + 1], ms[:, t:t + 1], ACT.Sqrt).then_inc(root_done, 1)
            for t in range(NT):
                for q in range(2):
                    act.wait_ge(ht_done, 2 * t + q + 1)
                    copy(hT[:, 4 * q:4 * q + 4, t * P:(t + 1) * P],
                         bank[4 + 2 * t + q][:, :].rearrange("p (k s) -> p k s", k=4)).then_inc(ht_copied, 1)
            act.wait_ge(ang_ready, 1)
            nc.scalar.activation(sin_t, ang, ACT.Sin).then_inc(sin_ready, 1)
            nc.scalar.activation(cos_t, rk, ACT.Sin).then_inc(sin_ready, 1)
            for t in range(NT):
                act.wait_ge(kt_done, t + 1)
                copy(kT[:, :, :, t * P:(t + 1) * P],
                     bank[4 + t][:, :].rearrange("p (g r s) -> p g r s", g=NKV, r=2)).then_inc(kt_copied, 1)
            for q in range(2):
                act.wait_ge(pooled_done, 2 * q + 2)
                copy(pooledT[:, 2 * q:2 * q + 2, :],
                     bank[6 + q][:, :].rearrange("p (g s) -> p g s", g=2)).then_inc(pooled_copied, 1)
            for g in range(NG):
                act.wait_ge(mixed_done, g // 2 * 2 + 2)
                nc.scalar.activation(mixedT[:, g, :], bank[6 + g // 2][:, (g % 2) * S:(g % 2 + 1) * S],
                                     ACT.Copy, scale=pscale[:, g:g + 1]).then_inc(mixed_copied, 1)
            for q in range(4):
                t, half = q // 2, q % 2
                act.wait_ge(qt_done, q + 1)
                copy(qT[:, 4 * half:4 * half + 4, t * P:(t + 1) * P],
                     bank[4 + q][:, :].rearrange("p (k s) -> p k s", k=4)).then_inc(qt_copied, 1)

            def exps(s):
                n, hp = UNITS[s]
                act.wait_ge(max_ready, s + 1)
                keys = P * (n + 1)
                for par in range(2):
                    sl = probs[:, s % 3, par * keys:(par + 1) * keys]
                    nc.scalar.activation(sl, sl, ACT.Exp, bias=mneg[:, par:par + 1],
                                         accum_out=sume[:, par:par + 1])
                nc.scalar.activation(esink, esink, ACT.Exp).then_inc(exp_done, 1)

            def pt_copy(s):
                n, hp = UNITS[s]
                act.wait_ge(pt_done, s + 1)
                if s >= 2:
                    act.wait_ge(pv_done, s - 1)
                copy(pT[:, s % 2, 0:2 * P * (n + 1)], bank[6][:, 0:2 * P * (n + 1)]).then_inc(pt_copied, 1)

            def o_copy(s):
                n, hp = UNITS[s]
                act.wait_ge(pv_done, s + 1)
                copy(attnT[:, hp, n * P:(n + 1) * P], bank[7][:, (s % 4) * P:(s % 4 + 1) * P]).then_inc(o_copied, 1)

            for s in range(NU + 3):
                if s < NU:
                    exps(s)
                if 2 <= s < NU + 2:
                    pt_copy(s - 2)
                if s >= 3:
                    o_copy(s - 3)
            act.wait_ge(z_ready, NT * NIN)
            for br in (1, 0):
                for t in range(NT):
                    nc.scalar.activation(zg[:, br, t, :], zg[:, br, t, :], ACT.Sigmoid).then_inc(gates_ready, 1)
            for q in range(4):
                hh, t = q // 2, q % 2
                act.wait_ge(mt_done, q + 1)
                copy(hT[:, 4 * hh:4 * hh + 4, t * P:(t + 1) * P],
                     bank[2 * t + hh][:, :].rearrange("p (k s) -> p k s", k=4)).then_inc(mt_copied, 1)
            for t in range(NT):
                act.wait_ge(x1_ready, NT + t + 1)
                nc.scalar.activation(h[:, t, :], resid[:, t, :], ACT.Square, accum_out=ssq[:, t:t + 1]) \
                    .then_inc(sq_done, 1)
                act.wait_ge(ms_ready, NT + t + 1)
                nc.scalar.activation(rms[:, t:t + 1], ms[:, t:t + 1], ACT.Sqrt).then_inc(root_done, 1)
            for q in range(4):
                act.wait_ge(h2t_done, q + 1)
                copy(hT[:, 4 * (q % 2):4 * (q % 2) + 4, (q // 2) * P:(q // 2 + 1) * P],
                     bank[q][:, :].rearrange("p (k s) -> p k s", k=4)).then_inc(h2t_copied, 1)
            for t in range(NT):
                act.wait_ge(logits_done, t + 1)
                copy(lgT[:, t, :], bank[4 + t][0:NE, 0:P]).then_inc(logits_copied, 1)
            for t in range(NT):
                act.wait_ge(top_ready, t + 1)
                nc.scalar.activation(ex[:, t, :], lg[:, t, :], ACT.Exp, bias=neg_top[:, t:t + 1]) \
                    .then_inc(rexp_done, 1)

            def copy_gathered(n):
                for q in range(2):
                    act.wait_ge(gathered, n + q)
                    copy(xgT[:, 4 * q:4 * q + 4, :],
                         M[q][:, :].rearrange("p (k s) -> p k s", k=4)).then_inc(xgt_copied, 1)

            copy_gathered(1)

            def expert_pair(i):
                for hh in range(NH):
                    act.wait_ge(gm_ready, i * 2 + hh + 1)
                    nc.scalar.activation(sg[:, hh * HALF:(hh + 1) * HALF], gm[:, hh * HALF:(hh + 1) * HALF],
                                         ACT.Sigmoid, scale=ALPHA).then_inc(sig_ready, 1)
                copy_gathered(i * 2 + 3)
                for hh in range(NH):
                    act.wait_ge(at_done, i * 2 + hh + 1)
                    copy(aT[:, 4 * hh:4 * hh + 4, :],
                         G[hh][:, :].rearrange("p (k s) -> p k s", k=4)).then_inc(at_copied, 1)
                    if hh == 0:
                        act.wait_ge(back_done, i + 1)
                        copy(back[:, :], U[0][:, 0:S]).then_inc(back_copied, 1)
                act.wait_ge(chunks_used, i * CHUNKS + CHUNKS)
                for hh in range(NH):
                    copy(y_sb[:, hh * HALF:(hh + 1) * HALF], Y[hh][:, :]).then_inc(y_copied, 1)

            expert_pair(0)
            act.wait_ge(over_ready, 1)
            n_over = act.value_load(over_i[0:1, OVER:OVER + 1], min_val=0, max_val=OVER)
            with act.Fori(1, PAIRS) as i:
                expert_pair(i)
            with act.If(n_over > 0):
                with act.Fori(0, OVER // 2) as k:
                    with act.If(k * 2 < n_over):
                        expert_pair(act.snap(k + PAIRS))
            nc.scalar.preload_act_table(ACT.Sqrt)
            for t in range(NT):
                act.wait_ge(fin_ms, t + 1)
                nc.scalar.activation(sg[:, :], resid[:, t, :], ACT.Square, accum_out=ssq[:, t:t + 1]) \
                    .then_inc(fin_sq, 1)
                act.wait_ge(fin_ms, NT + t + 1)
                nc.scalar.activation(rms[:, t:t + 1], ms[:, t:t + 1], ACT.Sqrt).then_inc(fin_root, 1)

        @block.vector
        def _(dve):
            v = nc.vector
            seq = [0]

            def link(ins):
                seq[0] += 1
                ins.then_inc(dve_seq, 1)
                dve.wait_ge(dve_seq, seq[0])

            def norm(t, n, ready):
                dve.wait_ge(sq_done, n)
                v.tensor_scalar(ms[:, t:t + 1], ssq[:, t:t + 1], 1.0 / D, EPS, ALU.mult, ALU.add) \
                    .then_inc(ms_ready, 1)
                dve.wait_ge(root_done, n)
                link(v.reciprocal(rstd[:, t:t + 1], rms[:, t:t + 1]))
                v.scalar_tensor_tensor(h[:, t, :], resid[:, t, :], rstd[:, t:t + 1], gvec[:, :],
                                       ALU.mult, ALU.mult).then_inc(ready, 1)

            dve.wait_ge(g_mix_loaded, 16)
            for t in range(NT):
                norm(t, t + 1, h_ready)

            dve.wait_ge(small_loaded, 16 * 5)
            link(v.tensor_copy(posf, pos_i[:, :]))
            for t in range(NT):
                link(v.tensor_scalar(ang[:, t, :], cst("inv_freq"), posf[:, t:t + 1], None, ALU.mult))
            MAGIC = 12582912.0
            link(v.tensor_scalar(rk, ang, 0.15915494309189535, MAGIC, ALU.mult, ALU.add))
            link(v.tensor_scalar(rk, rk, MAGIC, None, ALU.subtract))
            for part in (6.28125, 0.0019350051879882812, 3.0199159819305583e-07):
                link(v.scalar_tensor_tensor(ang, rk, -part, ang, ALU.mult, ALU.add))
            link(v.tensor_scalar(ang, ang, 3.1415925, -3.1415925, ALU.min, ALU.max))
            link(v.tensor_scalar(rk, ang, -1.0, None, ALU.mult))
            link(v.tensor_tensor(rk, rk, ang, ALU.min))
            v.tensor_scalar(rk, rk, 1.5707963267948966, None, ALU.add).then_inc(ang_ready, 1)

            z_dst = {"kv": lambda t: zkv[:, t, :], "q0": lambda t: zq[:, t, 0:HALF], "q1": lambda t: zq[:, t, HALF:D],
                     "u": lambda t: zu[:, t, :]}
            for n in range(4):
                z_dst[f"g{n}"] = lambda t, n=n: zg[:, n // 2, t, (n % 2) * HALF:(n % 2 + 1) * HALF]

            def take_z(m, t):
                dve.wait_ge(z_done, NT * m + t + 1)
                a, b = cols[order[m]]
                v.tensor_tensor(z_dst[order[m]](t), bank[2 * (m % 2) + t][:, 0:b - a], bias_in[:, m % 3, 0:b - a],
                                ALU.add).then_inc(z_ready, 1)

            def rope(src, heads, dst, t):
                def wide(table):
                    return table[:, t, None, :].to_broadcast([P, 2 * heads, ROT])
                s4 = src.rearrange("p (a r) -> p a r", r=ROT)
                sn = tmp[:, 0:heads * DH]
                link(v.tensor_tensor(sn.rearrange("p (a r) -> p a r", r=ROT), s4, wide(sin_t), ALU.mult))
                link(v.tensor_tensor(s4, s4, wide(cos_t), ALU.mult))
                s_ = src.rearrange("p (a c r) -> p a c r", c=2, r=ROT)
                n_ = sn.rearrange("p (a c r) -> p a c r", c=2, r=ROT)
                link(v.tensor_tensor(dst[:, :, 0, :], s_[:, :, 0, :], n_[:, :, 1, :], ALU.subtract))
                return v.tensor_tensor(dst[:, :, 1, :], s_[:, :, 1, :], n_[:, :, 0, :], ALU.add)

            for t in range(NT):
                take_z(0, t)
            dve.wait_ge(z_ready, NT)
            dve.wait_ge(sin_ready, 2)
            dve.wait_ge(kpad_zeroed, 1)
            for t in range(NT):
                k4 = kpad[:, t, :, :].rearrange("p (g r) (c d) -> p g r c d", g=NKV, c=2)
                link(rope(zkv[:, t, 0:KVW], NKV, k4[:, :, 0, 0, :].rearrange("p g (c r) -> p g c r", c=2), t))
                last = v.tensor_copy(k4[:, :, 1, 1, :], k4[:, :, 0, 0, :])
            last.then_inc(krot_ready, 1)
            for m in (1, 2):
                for t in range(NT):
                    take_z(m, t)
            dve.wait_ge(z_ready, NT * 3)
            for t in range(NT):
                ins = rope(zq[:, t, :], NQ, zq[:, t, :].rearrange("p (a c r) -> p a c r", c=2, r=ROT), t)
                if t < NT - 1:
                    link(ins)
                    take_z(3, 0)
            take_z(3, 1)
            ins.then_inc(qrot_ready, 1)
            for t in range(NT):
                take_z(4, t)

            def soft_a(s):
                n, hp = UNITS[s]
                keys = P * (n + 1)
                pr = probs[:, s % 3, 0:2 * keys].rearrange("p (a k) -> p a k", a=2)
                dve.wait_ge(score_done, s + 1)
                mask = cst("mask")[:, 2 * P - keys:2 * P]
                for par in range(2):
                    ins = v.scalar_tensor_tensor(pr[:, par, :],
                                                 bank[4 + s % 2][:, par * keys:(par + 1) * keys],
                                                 DH ** -0.5, mask, ALU.mult, ALU.add)
                ins.then_inc(masked, 1)
                dve.wait_ge(masked, s + 1)
                link(v.tensor_reduce(mx, pr, AX.X, ALU.max))
                snk = sinks[:, 2 * hp:2 * hp + 2]
                link(v.tensor_tensor(mx, mx, snk, ALU.max))
                v.tensor_scalar(mneg, mx, -1.0, None, ALU.mult)
                v.tensor_tensor(esink, snk, mx, ALU.subtract).then_inc(max_ready, 1)

            def soft_b(s):
                n, hp = UNITS[s]
                keys = P * (n + 1)
                dve.wait_ge(exp_done, s + 1)
                link(v.tensor_tensor(dens, sume, esink, ALU.add))
                link(v.reciprocal(rden, dens))
                for par in range(2):
                    sl = probs[:, s % 3, par * keys:(par + 1) * keys]
                    ins = v.tensor_scalar(sl, sl, rden[:, par:par + 1], None, ALU.mult)
                ins.then_inc(probs_ready, 1)

            done_per_step = -(-((NIN - 5) * NT * KT) // NU)
            taken = 5 * NT
            for s in range(NU):
                if s >= 3:
                    dve.wait_ge(pt_done, s - 2)
                soft_a(s)
                soft_b(s)
                while taken < NT * NIN and (taken - 5 * NT + 1) * KT <= s * done_per_step:
                    take_z(taken // NT, taken % NT)
                    taken += 1
            while taken < NT * NIN:
                take_z(taken // NT, taken % NT)
                taken += 1

            dve.wait_ge(bo_loaded, 16)
            for t in range(NT):
                dve.wait_ge(gates_ready, t + 1)
                for hh in range(NH):
                    sl = slice(hh * HALF, (hh + 1) * HALF)
                    dve.wait_ge(yp_done, 2 * t + hh + 1)
                    v.tensor_tensor(pool_g[:, t, sl], bank[2 * t + hh][:, :], zg[:, 1, t, sl], ALU.mult) \
                        .then_inc(dve_seq, 1)
                    seq[0] += 1
            dve.wait_ge(dve_seq, seq[0])
            for t in range(NT):
                dve.wait_ge(gates_ready, NT + t + 1)
                link(v.tensor_tensor(zg[:, 1, t, :], zg[:, 0, t, :], b_oa, ALU.mult))
                link(v.tensor_tensor(pool_g[:, t, :], pool_g[:, t, :], zg[:, 1, t, :], ALU.add))
            for q in range(4):
                hh, t = q // 2, q % 2
                sl = slice(hh * HALF, (hh + 1) * HALF)
                dve.wait_ge(ya_done, q + 1)
                link(v.tensor_tensor(zg[:, 0, t, sl], bank[4 + 2 * t + hh][:, :], zg[:, 0, t, sl], ALU.mult))
                v.tensor_tensor(zg[:, 0, t, sl], zg[:, 0, t, sl], pool_g[:, t, sl], ALU.add) \
                    .then_inc(merged_ready, 1)
            for q in range(4):
                hh, t = q // 2, q % 2
                sl = slice(hh * HALF, (hh + 1) * HALF)
                dve.wait_ge(out_proj_done, q + 1)
                v.tensor_tensor(resid[:, t, sl], resid[:, t, sl], bank[4 + 2 * t + hh][:, :], ALU.add) \
                    .then_inc(x1_ready, 1)
            dve.wait_ge(x1_ready, 4)
            dve.wait_ge(g_ffn_loaded, 16)
            for t in range(NT):
                norm(t, NT + t + 1, h2_ready)

            dve.wait_ge(ones_ready, 4)
            for t in range(NT):
                dve.wait_ge(lt_done, t + 1)
                link(v.tensor_tensor(lg[:, t, :], bank[6 + t][:, 0:NE], b_rt, ALU.add))
                link(v.max(v8[:, t, :], lg[:, t, :]))
                v.tensor_scalar(neg_top[:, t:t + 1], v8[:, t, 0:1], -1.0, None, ALU.mult).then_inc(top_ready, 1)
                kth = v8[:, t, TOPK - 1:TOPK]
                v.tensor_scalar(gt[:, t, :], lg[:, t, :], kth, None, ALU.is_gt)
                link(v.tensor_scalar(eq[:, t, :], lg[:, t, :], kth, None, ALU.is_equal))
                link(v.tensor_tensor_scan(pre[:, t, :], ones_row, eq[:, t, :], 0.0,
                                          ALU.mult, ALU.add))
            link(v.tensor_reduce(n_gt, gt, AX.X, ALU.add))
            link(v.tensor_scalar(need, n_gt, -1.0, float(TOPK), ALU.mult, ALU.add))
            for t in range(NT):
                link(v.scalar_tensor_tensor(pre[:, t, :], pre[:, t, :], need[:, t:t + 1], eq[:, t, :],
                                            ALU.is_le, ALU.mult))
            link(v.tensor_tensor(sel, pre, gt, ALU.add))
            v.tensor_copy(sel_bf[:, :, :], sel).then_inc(sel_ready, 1)
            dve.wait_ge(rexp_done, 2)
            link(v.tensor_tensor(ex, ex, sel, ALU.mult))
            link(v.tensor_reduce(wden, ex, AX.X, ALU.add))
            link(v.reciprocal(wrden, wden))
            v.memset(rank_tab[:, :, NE + OVER:ENTRIES], 0.0)
            v.memset(comb_tab[:, :, NE + OVER:ENTRIES], 0.0)
            v.memset(bsel_tab[:, NE + OVER:ENTRIES], 0.0)
            v.tensor_copy(bsel_tab[:, 0:NE], cst("bias_sel", BPARTS * NE))
            for t in range(NT):
                v.tensor_scalar(comb_tab[:, t, 0:NE], ex[:, t, :], wrden[:, t:t + 1], None, ALU.mult)
            dve.wait_ge(rank_done, 1)
            v.scalar_tensor_tensor(rank_tab[:, :, 0:NE], bank[5][:, 0:NT * NE].rearrange("p (t e) -> p t e", t=NT),
                                   1.0, sel, ALU.add, ALU.mult)
            v.memset(over_cum[:, 0:1], 0.0)
            for lv in range(LEVELS):
                ins = v.tensor_scalar(over_in[:, lv:lv + 1], bank[4][0:NE, 0:1], float(CAP * (lv + 1)), None,
                                      ALU.is_gt)
            ins.then_inc(tabs_ready, 1)

            slots = cst("slot_no")

            def make_pick(i):
                v.tensor_tensor(pick[:, :, :, :], slots[:, None, None, :].to_broadcast([P, NT, 2, CAP]),
                                rank_tab[:, :, bass.ds(i * 2, 2), None].to_broadcast([P, NT, 2, CAP]),
                                ALU.is_equal).then_inc(pick_ready, 1)

            def make_bsel(i):
                v.tensor_copy(bsel[:, :, :],
                              bsel_tab[:, bass.ds(i * 2, 2), None].to_broadcast([BPARTS * NE, 2, CAP])) \
                    .then_inc(bsel_ready, 1)

            dve.wait_ge(tabs_ready, 1)
            make_pick(0)
            make_bsel(0)
            v.tensor_copy(over_cum[:, 1:2], over_in[:, 0:1])
            link(v.tensor_tensor(over_cum[:, 2:3], over_in[:, 0:1], over_in[:, 1:2], ALU.add))
            link(v.tensor_reduce(over_n, over_in, AX.X, ALU.add))
            dve.wait_ge(cols_done, 1)
            v.tensor_copy(rank_cols[:, :, :], bank[4][0:NE, :].rearrange("p (q s) -> p q s", q=2)) \
                .then_inc(cols_ready, 1)
            def overflow_one_hot():
                dve.wait_ge(pos_done, 1)
                link(v.tensor_copy(over_pos, bank[5][0:NE, 0:LEVELS]))
                for lv in range(LEVELS):
                    link(v.tensor_scalar(oh[:, lv, :], cst("entry_no", NE), over_pos[:, lv:lv + 1],
                                         over_in[:, lv:lv + 1], ALU.is_equal, ALU.mult))
                link(v.tensor_tensor(over_sel, oh[:, 0, :], oh[:, 1, :], ALU.add))
                link(v.tensor_tensor(over_sel, over_sel, oh[:, 2, :], ALU.add))
                link(v.tensor_scalar(over_shift, oh[:, 0, :], -float(CAP), None, ALU.mult))
                for lv in range(1, LEVELS):
                    link(v.scalar_tensor_tensor(over_shift, oh[:, lv, :], -float(CAP * (lv + 1)), over_shift,
                                                ALU.mult, ALU.add))
                for q in range(BPARTS):
                    v.tensor_copy(bsel_tab[q * NE:(q + 1) * NE, NE:NE + OVER], over_sel)
                v.tensor_copy(over_i[:, OVER:OVER + 1], bank[5][0:1, 32:33]).then_inc(oh_ready, 1)

            def overflow_tables():
                dve.wait_ge(over_done, 1)
                tab = bank[5][:, 64:64 + NT * OVER].rearrange("p (t o) -> p t o", t=NT)
                v.tensor_copy(rank_tab[:, :, NE:NE + OVER], tab)
                tab = bank[5][:, 128:128 + NT * OVER].rearrange("p (t o) -> p t o", t=NT)
                v.tensor_copy(comb_tab[:, :, NE:NE + OVER], tab)
                v.tensor_copy(over_i[:, 0:OVER], bank[5][0:1, 192:192 + OVER]).then_inc(over_ready, 1)

            def expert_pair(i, first=False):
                dve.wait_ge(pick_ready, i + 1)
                v.tensor_tensor(pickw[:, :, :, :], pick[:, :, :, :],
                                comb_tab[:, :, bass.ds(i * 2, 2), None].to_broadcast([P, NT, 2, CAP]),
                                ALU.mult).then_inc(pickw_ready, 1)
                dve.wait_ge(pickw_ready, i + 1)
                dve.wait_ge(gathered, i * 2 + 2)
                make_pick(i + 1)
                dve.wait_ge(chunks_used, i * CHUNKS + 8)
                for hh in range(NH):
                    v.tensor_scalar(gm[:, hh * HALF:(hh + 1) * HALF], G[hh][:, :], LIMIT, None, ALU.min) \
                        .then_inc(gm_ready, 1)
                if first:
                    overflow_one_hot()
                dve.wait_ge(chunks_used, i * CHUNKS + 16)
                for hh in range(NH):
                    sl = slice(hh * HALF, (hh + 1) * HALF)
                    v.tensor_scalar(um[:, sl], U[hh][:, :], LIMIT, -LIMIT, ALU.min, ALU.max).then_inc(um_ready, 1)
                    dve.wait_ge(um_ready, i * 2 + hh + 1)
                    v.scalar_tensor_tensor(um[:, sl], um[:, sl], 1.0, gm[:, sl], ALU.add, ALU.mult) \
                        .then_inc(prod_ready, 1)
                    dve.wait_ge(prod_ready, i * 2 + hh + 1)
                    dve.wait_ge(sig_ready, i * 2 + hh + 1)
                    v.tensor_tensor(act_a[:, sl], um[:, sl], sg[:, sl], ALU.mult).then_inc(a_ready, 1)
                make_bsel(i + 1)
                if first:
                    overflow_tables()
                for n in range(4):
                    t, hh = n // 2, n % 2
                    sl = slice(hh * HALF, (hh + 1) * HALF)
                    dve.wait_ge(comb_done, i * 4 + n + 1)
                    v.tensor_tensor(resid[:, t, sl], resid[:, t, sl], (M, U)[t][hh][:, :], ALU.add) \
                        .then_inc(comb_banks_free, 1)

            expert_pair(0, first=True)
            dve.wait_ge(over_ready, 1)
            n_over = dve.value_load(over_i[0:1, OVER:OVER + 1], min_val=0, max_val=OVER)
            with dve.Fori(1, PAIRS) as i:
                expert_pair(i)
            with dve.If(n_over > 0):
                with dve.Fori(0, OVER // 2) as k:
                    with dve.If(k * 2 < n_over):
                        expert_pair(dve.snap(k + PAIRS))

            dve.wait_ge(g_final_loaded, 16)
            v.engine_nop().then_inc(fin_ms, 2)
            for t in range(NT):
                dve.wait_ge(fin_sq, t + 1)
                v.tensor_scalar(ms[:, t:t + 1], ssq[:, t:t + 1], 1.0 / D, EPS, ALU.mult, ALU.add).then_inc(fin_ms, 1)
                dve.wait_ge(fin_root, t + 1)
                link(v.reciprocal(rstd[:, t:t + 1], rms[:, t:t + 1]))
                v.scalar_tensor_tensor(h[:, t, :], resid[:, t, :], rstd[:, t:t + 1], gvec[:, :],
                                       ALU.mult, ALU.mult).then_inc(fin_ready, 1)

        @block.gpsimd
        def _(pool):
            g = nc.gpsimd
            g.memset(kpad[:, :, :, :], 0.0).then_inc(kpad_zeroed, 1)
            g.memset(ones_f[:, :], 1.0).then_inc(ones_ready, 1)
            g.memset(ones_bf[:, :], 1.0).then_inc(ones_ready, 1)
            g.memset(ones_row, 1.0).then_inc(ones_ready, 1)
            pool.wait_ge(small_loaded, 16 * 5)
            g.tensor_copy(upper_bf[:, :], cst("upper")).then_inc(ones_ready, 1)
            pool.wait_ge(h_ready, NT)
            pool.dma_start(gvec[:, :], norm_ffn_g.to_broadcast([P, D])).then_inc(g_ffn_loaded, 16)
            pool.wait_ge(qrot_ready, 1)
            pool.dma_start(b_oa, b_o_attn.to_broadcast([P, D])).then_inc(bo_loaded, 16)
            pool.wait_ge(o_copied, NU)
            pool.dma_start(b_dn, b_down[0]).then_inc(bdn_loaded, 16)
            step = [0]

            def settle(ins):
                step[0] += 1
                ins.then_inc(bias_seq, 1)
                pool.wait_ge(bias_seq, step[0])

            for n, b in enumerate((b_gate, b_up)):
                for q in range(BPARTS):
                    pool.dma_start(stage[q * NE:(q + 1) * NE, :], b[0]).then_inc(stage_loaded, 16)
                pool.wait_ge(stage_loaded, 16 * BPARTS * (n + 1))
                for q in range(BPARTS):
                    rows = slice(q * NE, (q + 1) * NE)
                    settle(g.tensor_copy(stage_h, stage))
                    last = g.tensor_copy(bias3[rows, n * D:(n + 1) * D], stage_h[rows, :])
                    if q == BPARTS - 1:
                        last.then_inc(bias3_ready, 1)
                        pool.wait_ge(bias3_ready, n + 1)
                        break
                    settle(last)
                    settle(g.tensor_copy(stage_r, stage_h))
                    settle(g.tensor_tensor(stage, stage, stage_r, ALU.subtract))
            pool.wait_ge(h2_ready, NT)
            pool.dma_start(gvec[:, :], norm_final_g.rearrange("(a d) -> a d", a=1).to_broadcast([P, D])) \
                .then_inc(g_final_loaded, 16)


_INS = ["x", "positions", "norm_mix_g", "w_in", "b_in", "attn_sinks", "w_o_attn", "b_o_attn", "w_pool_mix",
        "pool_scale", "w_pool_up", "w_out", "norm_ffn_g", "w_router", "b_router", "w_gate", "b_gate", "w_up",
        "b_up", "w_down", "b_down", "norm_final_g"]
_OUTS = [((1, S, D), "float32")]


def shape_constants():
    import numpy as np

    def at(name):
        a, b = CONST_COLS[name]
        return slice(a, b)

    c = np.zeros((P, CONST_W), np.float32)
    r = np.arange(P)
    c[:, at("ident")] = np.eye(P)
    key = np.arange(2 * P)[None, :]
    dist = r[:, None] + P - key
    c[:, at("mask")] = np.where((dist >= 0) & (dist < P), 0.0, -1e30)
    band = np.zeros((P, NG, 3 * P))
    for g, w in enumerate(WINDOWS):
        for blk, (src, t0) in enumerate(((0, 0), (0, P), (P, P))):
            s_tok = src + r[:, None]
            tok = t0 + r[None, :]
            inside = (tok >= s_tok) & (tok - s_tok < w)
            band[:, g, blk * P:(blk + 1) * P] = inside / np.minimum(tok + 1, w) - (tok == s_tok)
    c[:, at("band")] = band.reshape(P, -1)
    c[:, at("upper")] = r[:, None] < r[None, :]
    c[:, at("slot_no")] = np.arange(1, CAP + 1)
    c[:BPARTS * NE, at("bias_sel")] = (np.arange(BPARTS * NE)[:, None] % NE) == np.arange(NE)
    c[:, at("entry_no")] = np.arange(OVER)
    c[:NE, at("upper32")] = np.arange(NE)[:, None] < np.arange(NE)[None, :]
    c[:NE, at("expert_no")] = np.arange(NE)[:, None]
    c[:, at("inv_freq")] = 10000.0 ** (-np.arange(0, DH, 2) / DH)
    return c


def kernel(**inputs):
    import numpy as _np
    import concourse.bacc as _bacc
    from concourse import mybir as _mybir
    from concourse.bass_utils import run_bass_kernel_spmd as _run

    nc = _bacc.Bacc("TRN2", target_bir_lowering=False, num_devices=1)
    arrays, args = {}, []
    given = {name: inputs[name] for name in _INS}
    given["consts"] = shape_constants()
    for name, a in given.items():
        a = _np.ascontiguousarray(a)
        arrays[f"in_{name}_dram"] = a
        args.append(nc.dram_tensor(f"in_{name}_dram", a.shape, _mybir.dt.from_np(a.dtype), kind="ExternalInput").ap())
    for i, (shape, dtype) in enumerate(_OUTS):
        dt = _mybir.dt.from_np(_np.dtype(dtype))
        args.append(nc.dram_tensor(f"out_{i}_dram", shape, dt, kind="ExternalOutput").ap())
    hybrid_block(nc, *args)
    r = _run(nc, [arrays], core_ids=[0])
    return _np.asarray(r.results[0]["out_0_dram"])
```

```python
from contextlib import ExitStack

import concourse.bass as bass
from concourse import mybir

D = 1024
S = 256
P = 128
NT = S // P
KT = D // P
HALF = 512
NH = D // HALF
DH = 64
NQ = D // DH
NKV = NQ // 8
NPAIR = NQ // 2
ROT = DH // 2
KVW = NKV * DH
POOLW = D // 2
NG = 4
WINDOWS = (2, 4, 8, 16)
IN_W = D + 2 * KVW + POOLW + 2 * D
EPS = 1e-5
LIMIT = 7.0
ALPHA = 1.702
NE = 32
TOPK = 4
CAP = 64
LEVELS = S // CAP - 1
OVER = 16
PAIRS = NE // 2
ENTRIES = NE + OVER + 2
CHUNKS = 24
RING = 12
BONUS = 7
CH_KT = 2
BPARTS = 3

CONST_COLS = {}
_at = 0
for _name, _width in (("ident", P), ("upper", P), ("slot_no", CAP), ("bias_sel", NE), ("entry_no", OVER),
                      ("upper32", NE), ("expert_no", 2), ("inv_freq", ROT), ("mask", 2 * P),
                      ("band", NG * 3 * P)):
    CONST_COLS[_name] = (_at, _at + _width)
    _at += _width
CONST_W = _at


def hybrid_block(nc, x, positions, norm_mix_g, w_in, b_in, attn_sinks, w_o_attn, b_o_attn, w_pool_mix,
                 pool_scale, w_pool_up, w_out, norm_ffn_g, w_router, b_router, w_gate, b_gate, w_up,
                 b_up, w_down, b_down, norm_final_g, consts, out):
    f32 = mybir.dt.float32
    f32r = mybir.dt.float32r
    bf16 = mybir.dt.bfloat16
    i32 = mybir.dt.int32
    ALU = mybir.AluOpType
    ACT = mybir.ActivationFunctionType
    AX = mybir.AxisListType

    ctx = ExitStack()
    with ctx:
        def sb(name, shape, dt=f32):
            return ctx.enter_context(nc.sbuf_tensor(name, shape, dt))

        def sem(name):
            return ctx.enter_context(nc.semaphore(name))

        ring = sb("ring", [P, RING * CH_KT * D])
        resid = sb("resid", [P, NT, D])
        gvec = sb("gvec", [P, D])
        const_wmix = sb("const_wmix", [P, CONST_W + NG * P])
        const = const_wmix[:, 0:CONST_W]
        wmix = const_wmix[:, CONST_W:].rearrange("p (g n) -> p g n", g=NG)
        hT = sb("hT", [P, KT, S])
        h = sb("h", [P, NT, D])
        zq = sb("zq", [P, NT, D])
        zg = sb("zg", [P, 2, NT, D])
        zu_qT = sb("zu_qT", [P, NT * POOLW + NPAIR * S])
        zu = zu_qT[:, 0:NT * POOLW].rearrange("p (t n) -> p t n", t=NT)
        qT = zu_qT[:, NT * POOLW:].rearrange("p (q s) -> p q s", q=NPAIR)
        kpad = sb("kpad", [P, NT, 2 * NKV, P])
        kT = sb("kT", [P, NKV, 2, S])
        bias_zkv = sb("bias_zkv", [P, 3 * HALF + NT * 2 * KVW])
        bias_in = bias_zkv[:, 0:3 * HALF].rearrange("p (m n) -> p m n", m=3)
        zkv = bias_zkv[:, 3 * HALF:].rearrange("p (t n) -> p t n", t=NT)
        tmp = sb("tmp", [P, D + 2 * KVW])
        soft = sb("soft", [P, 5 * HALF])
        probs = soft[:, 0:3 * HALF].rearrange("p (m n) -> p m n", m=3)
        pT = soft[:, 3 * HALF:].rearrange("p (m n) -> p m n", m=2)
        w_rt = sb("w_rt", [P, KT, NE])
        small = sb("small", [P, 672])
        pos_i = sb("pos_i", [P, NT], i32)
        sel_bf = sb("sel_bf", [P, NT, NE], bf16)
        upper_bf = sb("upper_bf", [P, P], bf16)
        ones_bf = sb("ones_bf", [P, P], bf16)
        ones_f = sb("ones_f", [NE, P])
        rank_tab = sb("rank_tab", [P, NT, ENTRIES])
        comb_tab = sb("comb_tab", [P, NT, ENTRIES])
        bsel_tab = sb("bsel_tab", [BPARTS * NE, ENTRIES], bf16)
        bsel = sb("bsel", [BPARTS * NE, 2, CAP], bf16)
        over_i = sb("over_i", [1, OVER + 2], i32)

        def cst(name, rows=P):
            a, b = CONST_COLS[name]
            return const[0:rows, a:b]

        xgT = qT[:, 4:8, :].rearrange("p a (b c) -> p (a b) c", c=P)
        gm = zg[:, 0, 0, :]
        sg = zg[:, 0, 1, :]
        um = zg[:, 1, 0, :]
        act_a = zg[:, 1, 1, :]
        aT = zq[:, 0, :].rearrange("p (k s) -> p k s", s=P)
        y_sb = zq[:, 1, :]
        pick = tmp[:, 0:2 * NT * CAP].rearrange("p (t x s) -> p t x s", t=NT, x=2)
        pickw = tmp[:, 256:512].rearrange("p (t x s) -> p t x s", t=NT, x=2)
        back = tmp[:, 512:768]
        bias3 = kT[:, :, :, :].rearrange("p a b s -> p (a b s)").bitcast(bf16)[0:BPARTS * NE, :]
        b_dn = kpad[0:NE, :, :, :].rearrange("p a b s -> p (a b s)")
        stage = soft[0:BPARTS * NE, 0:2 * D].rearrange("p (b n) -> p b n", b=2)
        attnT = zq[:, :, :].rearrange("p t (k s) -> p (t k) s", s=S)
        pooledT = h[:, 0, :].rearrange("p (g s) -> p g s", s=S)
        mixedT = h[:, 1, :].rearrange("p (g s) -> p g s", s=S)
        pool_g = qT[:, :, :].rearrange("p (t k) s -> p t (k s)", t=NT)
        b_oa = tmp[:, 0:D]

        def piece(at, width):
            return small[:, at:at + width]

        ssq, ms, rms, rstd = piece(0, 2), piece(2, 2), piece(4, 2), piece(6, 2)
        pscale, sinks = piece(8, 4), piece(16, NQ)
        posf = piece(32, 2)
        ang = piece(64, 64).rearrange("p (t r) -> p t r", t=NT)
        rk = piece(128, 64).rearrange("p (t r) -> p t r", t=NT)
        cos_t = piece(192, 64).rearrange("p (t r) -> p t r", t=NT)
        sin_t = piece(256, 64).rearrange("p (t r) -> p t r", t=NT)
        mx, mneg, sume, esink, dens, rden = (piece(320 + 2 * n, 2) for n in range(6))
        b_rt = piece(336, NE)
        lg = piece(64, 64).rearrange("p (t e) -> p t e", t=NT)
        ex = piece(128, 64).rearrange("p (t e) -> p t e", t=NT)
        gt = piece(192, 64).rearrange("p (t e) -> p t e", t=NT)
        eq = piece(256, 64).rearrange("p (t e) -> p t e", t=NT)
        pre = piece(368, 64).rearrange("p (t e) -> p t e", t=NT)
        sel = piece(432, 64).rearrange("p (t e) -> p t e", t=NT)
        v8 = piece(496, 16).rearrange("p (t e) -> p t e", t=NT)
        neg_top, n_gt, need, wden, wrden = (piece(512 + 2 * n, 2) for n in range(5))
        over_in = small[0:NE, 522:525]
        over_cum = small[0:NE, 525:528]
        over_pos = small[0:NE, 528:531]
        over_n = small[0:NE, 531:532]
        oh = small[0:NE, 544:592].rearrange("p (l o) -> p l o", l=LEVELS)
        over_sel = small[0:NE, 592:608]
        over_shift = small[0:NE, 608:624]
        rank_cols = tmp[0:NE, 768:768 + 2 * S].rearrange("p (q s) -> p q s", q=2)
        ones_row = piece(640, NE)
        lgT = tmp[0:NE, 0:NT * P].rearrange("p (t s) -> p t s", t=NT)
        bank = [ctx.enter_context(nc.psum_tensor(f"bank{n}", [P, HALF], f32)) for n in range(8)]
        G, U, Y, M = bank[0:2], bank[2:4], bank[4:6], bank[6:8]

        cols = {"kv": (D, D + 2 * KVW), "q0": (0, HALF), "q1": (HALF, D),
                "u": (D + 2 * KVW, D + 2 * KVW + POOLW)}
        g0 = IN_W - 2 * D
        for n in range(4):
            cols[f"g{n}"] = (g0 + n * HALF, g0 + (n + 1) * HALF)
        order = ["kv", "q0", "q1", "u", "g0", "g1", "g2", "g3"]
        NIN = len(order)
        POOL_UP, WO, WOUT, MIXN = NIN, NIN + 1, NIN + 3, NIN + 5
        PLACES = 4
        PW = KT * HALF

        def place(m):
            return ring[:, (m % PLACES) * PW:(m % PLACES + 1) * PW]

        def in_chunk(m):
            a, b = cols[order[m]]
            return place(m)[:, 0:KT * (b - a)].rearrange("p (k n) -> p k n", k=KT)

        def half_chunk(m):
            return place(m).rearrange("p (k n) -> p k n", k=KT)

        pool_up_sb = place(POOL_UP).rearrange("p (k n) -> p k n", k=NG)

        def f32r_at(name, words, base, shift=0):
            addr = nc.lookup_mls(base).memorylocations[0].addr + 4 * shift
            return nc.alloc_sbuf_tensor_at(name, [P, words], f32r, offset=addr).ap()

        def by_tokens(ap):
            return ap.rearrange("p (k s) -> p k s", s=S)

        GRAN = 1024
        SLOTS = 4
        w_low_all = f32r_at("w_low", PLACES * PW, ring)
        x_high = by_tokens(f32r_at("x_high", KT * S, ring, PLACES * PW))
        x_low = by_tokens(f32r_at("x_low", KT * S, ring, PLACES * PW + KT * S))
        w_high_all = f32r_at("w_high", SLOTS * GRAN, ring, PLACES * PW + 2 * KT * S)
        m_high = by_tokens(f32r_at("m_high", KT * S, hT))
        m_low = by_tokens(f32r_at("m_low", KT * S, zq))

        PIECES = []
        first_piece = {}
        for m in list(range(5)) + list(range(WO, MIXN)):
            first_piece[m] = len(PIECES)
            width = cols[order[m]][1] - cols[order[m]][0] if m < NIN else HALF
            PIECES += [(m, c) for c in range(KT * width // GRAN)]
        NP_IN = first_piece[WO]

        def piece_views(n):
            m, c = PIECES[n]
            width = cols[order[m]][1] - cols[order[m]][0] if m < NIN else HALF
            nk = GRAN // width
            at = (m % PLACES) * PW + c * GRAN
            return (range(c * nk, (c + 1) * nk), ring[:, at:at + GRAN],
                    w_high_all[:, n % SLOTS * GRAN:(n % SLOTS + 1) * GRAN], w_low_all[:, at:at + GRAN])

        def mixer_loaded(m):
            return mix_loaded[m % PLACES], sum(32 if n < NIN else 16 for n in range(m % PLACES, m + 1, PLACES))

        FIRST = 2

        def chunk_place(j, early=False):
            n = (j + FIRST - (0 if early else BONUS)) % RING
            return n, ring[:, n * CH_KT * D:(n + 1) * CH_KT * D].rearrange("p (k n) -> p k n", k=CH_KT)

        mask_at = CONST_COLS["mask"][0]
        bonus_places = [m.rearrange("p (k n) -> p k n", k=CH_KT) for m in (
            zq[:, :, :].rearrange("p t d -> p (t d)"), zg[:, 1, :, :].rearrange("p t d -> p (t d)"),
            soft[:, 0:CH_KT * D], const_wmix[:, mask_at:mask_at + CH_KT * D], bias_zkv[:, :],
            zu_qT[:, 0:CH_KT * D], hT[:, :, :].rearrange("p k s -> p (k s)"))]
        B_ZQ, B_ZG, B_SOFT, B_CONST, B_ZKV, B_ZU, B_HT = range(BONUS)

        x_loaded = [sem(f"x_loaded{t}") for t in range(NT)]
        ident_loaded, small_loaded, wsmall_loaded = sem("ident_loaded"), sem("small_loaded"), sem("wsmall_loaded")
        g_mix_loaded, g_ffn_loaded, g_final_loaded = sem("g_mix_loaded"), sem("g_ffn_loaded"), sem("g_final_loaded")
        mix_loaded = [sem(f"mix_loaded{n}") for n in range(PLACES)]
        chunk_loaded = [sem(f"chunk_loaded{n}") for n in range(RING)]
        bonus_loaded = [sem(f"bonus_loaded{n}") for n in range(BONUS)]
        chunks_used = sem("chunks_used")
        bo_loaded, stage_loaded, bdn_loaded = sem("bo_loaded"), sem("stage_loaded"), sem("bdn_loaded")
        ones_ready, kpad_zeroed = sem("ones_ready"), sem("kpad_zeroed")
        bias3_ready = sem("bias3_ready")
        dve_seq, act_seq = sem("dve_seq"), sem("act_seq")
        sq_done, root_done, ms_ready, h_ready = sem("sq_done"), sem("root_done"), sem("ms_ready"), sem("h_ready")
        ht_done, ht_copied = sem("ht_done"), sem("ht_copied")
        w_high_ready, w_low_ready, w_high_used = sem("w_high_ready"), sem("w_low_ready"), sem("w_high_used")
        ht_high_ready, ht_low_ready = sem("ht_high_ready"), sem("ht_low_ready")
        at_high_ready, at_low_ready = sem("at_high_ready"), sem("at_low_ready")
        z_done, z_ready = sem("z_done"), sem("z_ready")
        ang_ready, sin_ready = sem("ang_ready"), sem("sin_ready")
        krot_ready, qrot_ready = sem("krot_ready"), sem("qrot_ready")
        kt_done, kt_copied, qt_done, qt_copied = sem("kt_done"), sem("kt_copied"), sem("qt_done"), sem("qt_copied")
        pooled_done, pooled_copied, mixed_done, mixed_copied = (
            sem("pooled_done"), sem("pooled_copied"), sem("mixed_done"), sem("mixed_copied"))
        score_done, masked, max_ready, exp_done, probs_ready = (
            sem("score_done"), sem("masked"), sem("max_ready"), sem("exp_done"), sem("probs_ready"))
        pt_done, pt_copied, pv_done, o_copied = sem("pt_done"), sem("pt_copied"), sem("pv_done"), sem("o_copied")
        gates_ready, yp_done, ya_done, merged_ready = (
            sem("gates_ready"), sem("yp_done"), sem("ya_done"), sem("merged_ready"))
        mt_done, mt_high_ready, mt_low_ready, out_proj_done, x1_ready = (
            sem("mt_done"), sem("mt_high_ready"), sem("mt_low_ready"), sem("out_proj_done"), sem("x1_ready"))
        h2_ready, h2t_done, h2t_copied, logits_done, logits_copied, lt_done = (
            sem("h2_ready"), sem("h2t_done"), sem("h2t_copied"), sem("logits_done"),
            sem("logits_copied"), sem("lt_done"))
        top_ready, rexp_done, sel_ready, rank_done = (
            sem("top_ready"), sem("rexp_done"), sem("sel_ready"), sem("rank_done"))
        tabs_ready, cols_done, cols_ready, pos_done, oh_ready, over_done, over_ready = (
            sem("tabs_ready"), sem("cols_done"), sem("cols_ready"), sem("pos_done"), sem("oh_ready"),
            sem("over_done"), sem("over_ready"))
        pick_ready, pickw_ready, bsel_ready = sem("pick_ready"), sem("pickw_ready"), sem("bsel_ready")
        gathered, xgt_copied = sem("gathered"), sem("xgt_copied")
        gm_ready, sig_ready, um_ready, prod_ready, a_ready = (
            sem("gm_ready"), sem("sig_ready"), sem("um_ready"), sem("prod_ready"), sem("a_ready"))
        at_done, at_copied, back_done, back_copied = (
            sem("at_done"), sem("at_copied"), sem("back_done"), sem("back_copied"))
        y_copied, comb_done, comb_banks_free = (
            sem("y_copied"), sem("comb_done"), sem("comb_banks_free"))
        fin_sq, fin_root, fin_ms, fin_ready, stored = (
            sem("fin_sq"), sem("fin_root"), sem("fin_ms"), sem("fin_ready"), sem("stored"))

        def mixer_chunk_used(m):
            if m < NIN:
                return z_done, NT * (m + 1)
            if m == POOL_UP:
                return yp_done, NT * NH
            if m < WOUT:
                return ya_done, NT * (m - WO + 1)
            return out_proj_done, NT * (m - WOUT + 1)

        block = ctx.enter_context(nc.Block())

        UNITS = [(n, hp) for n in range(NT) for hp in range(NPAIR)]
        NU = len(UNITS)

        @block.sync
        def _(sp):
            for t in range(NT):
                sp.dma_start(resid[:, t, :], x[0, t * P:(t + 1) * P, :]).then_inc(x_loaded[t], 16)
                if t == 0:
                    sp.dma_start(gvec[:, :], norm_mix_g.to_broadcast([P, D])).then_inc(g_mix_loaded, 16)
            sp.dma_start(const[:, 0:P], consts[:, 0:P]).then_inc(ident_loaded, 16)

            def load_mixer(m):
                if m >= PLACES:
                    sp.wait_ge(*mixer_chunk_used(m - PLACES))
                if m < NIN:
                    a, b = cols[order[m]]
                    if m >= 3:
                        sp.wait_ge(z_ready, NT * (m - 2))
                    sp.dma_start(bias_in[:, m % 3, 0:b - a],
                                 b_in[:, a:b].to_broadcast([P, b - a])).then_inc(mix_loaded[m % PLACES], 16)
                    sp.dma_start(in_chunk(m), w_in[0, :, a:b].rearrange("(k p) n -> p k n", p=P)) \
                        .then_inc(mix_loaded[m % PLACES], 16)
                elif m == POOL_UP:
                    sp.dma_start(pool_up_sb, w_pool_up[0].rearrange("(k p) n -> p k n", p=P)) \
                        .then_inc(mix_loaded[m % PLACES], 16)
                else:
                    src, hh = (w_o_attn, m - WO) if m < WOUT else (w_out, m - WOUT)
                    sp.dma_start(half_chunk(m), src[0, :, hh * HALF:(hh + 1) * HALF]
                                 .rearrange("(k p) n -> p k n", p=P)).then_inc(mix_loaded[m % PLACES], 16)

            load_mixer(0)
            with nc.allow_non_contiguous_dma(reason="a few hundred words"):
                sp.dma_start(pos_i[:, :], positions[0].rearrange("(t p) -> p t", p=P)).then_inc(small_loaded, 16)
                sp.dma_start(pscale, pool_scale[0].rearrange("(g p) -> p g", p=P)).then_inc(small_loaded, 16)
            load_mixer(1)
            sp.dma_start(const[:, P:], consts[:, P:]).then_inc(small_loaded, 16)
            sp.dma_start(sinks, attn_sinks.to_broadcast([P, NQ])).then_inc(small_loaded, 16)
            sp.dma_start(b_rt, b_router.to_broadcast([P, NE])).then_inc(small_loaded, 16)
            load_mixer(2)
            sp.dma_start(wmix[:, :, :], w_pool_mix[0].rearrange("g c d -> c g d")).then_inc(wsmall_loaded, 16)
            sp.dma_start(w_rt[:, :, :], w_router[0].rearrange("(k p) e -> p k e", p=P)).then_inc(wsmall_loaded, 16)
            for m in range(3, MIXN):
                load_mixer(m)

            matrices = (w_gate, w_up, w_down)

            def load_chunk(j, expert_a, expert_b, early=False, bonus=None):
                which, piece_no, side = j // 8, j % 8 // 2, j % 2
                e = (expert_a, expert_b)[side]
                n, dst = chunk_place(j, early)
                signal = chunk_loaded[n]
                if bonus is not None:
                    dst, signal = bonus_places[bonus], bonus_loaded[bonus]
                rows = slice(piece_no * CH_KT * P, (piece_no + 1) * CH_KT * P)
                sp.dma_start(dst, matrices[which][0, bass.ds(e, 1), rows, :]
                             .rearrange("o (k p) n -> p (o k) n", p=P)).then_inc(signal, 16)

            def chunk_free(count):
                sp.wait_ge(chunks_used, count)
                sp.nop(nofuse=True)

            def load_first(*js):
                for j in js:
                    n = chunk_place(j, early=True)[0] // 2
                    if n == PLACES:
                        sp.wait_ge(ya_done, NT * NH)
                    elif n > PLACES:
                        sp.wait_ge(out_proj_done, NT * NH)
                    else:
                        sp.wait_ge(*mixer_chunk_used(max(m for m in range(MIXN) if m % PLACES == n)))
                    load_chunk(j, 0, 1, early=True)

            def load_bonus(b):
                load_chunk(RING + b, 0, 1, bonus=b)

            sp.wait_ge(pv_done, NU)
            sp.wait_ge(z_ready, NT * NIN)
            load_bonus(B_ZKV)
            load_bonus(B_CONST)
            load_first(0, 1, 2, 3, 6, 7)
            sp.wait_ge(merged_ready, NT * NH)
            load_bonus(B_ZG)
            load_bonus(B_ZU)
            sp.wait_ge(bias3_ready, 2)
            load_bonus(B_SOFT)
            load_first(4, 5, 8, 9, 10, 11)
            load_bonus(B_ZQ)
            sp.wait_ge(logits_done, NT)
            load_bonus(B_HT)
            for j in range(RING + BONUS, CHUNKS):
                chunk_free(j - RING - BONUS + 1)
                load_chunk(j, 0, 1)
            for j in range(BONUS):
                chunk_free(CHUNKS + j - RING - BONUS + 1)
                load_chunk(j, 2, 3)
            with sp.Fori(1, PAIRS - 1) as i:
                for j in range(BONUS, CHUNKS):
                    chunk_free(i * CHUNKS + (j - RING + 1))
                    load_chunk(j, i * 2, i * 2 + 1)
                for j in range(BONUS):
                    chunk_free(i * CHUNKS + (CHUNKS + j - RING + 1))
                    load_chunk(j, i * 2 + 2, i * 2 + 3)
            for j in range(BONUS, CHUNKS):
                chunk_free((PAIRS - 1) * CHUNKS + j - RING + 1)
                load_chunk(j, NE - 2, NE - 1)

            sp.wait_ge(over_ready, 1)
            n_over = sp.value_load(over_i[0:1, OVER:OVER + 1], min_val=0, max_val=OVER)
            with sp.If(n_over > 0):
                with sp.Fori(0, OVER // 2) as k:
                    with sp.If(k * 2 < n_over):
                        expert_a = sp.value_load(over_i[0:1, bass.ds(k * 2, 1)], min_val=0, max_val=NE - 1)
                        expert_b = sp.value_load(over_i[0:1, bass.ds(k * 2 + 1, 1)], min_val=0, max_val=NE - 1)
                        for j in range(CHUNKS):
                            chunk_free((k + PAIRS) * CHUNKS + (j - RING + 1))
                            load_chunk(j, expert_a, expert_b)

            for t in range(NT):
                sp.wait_ge(fin_ready, t + 1)
                sp.dma_start(out[0, t * P:(t + 1) * P, :], h[:, t, :]).then_inc(stored, 16)
            sp.wait_ge(stored, 16 * NT)

        @block.tensor
        def _(pe):
            mm = nc.tensor.matmul
            ident = cst("ident")

            def transposes(dst, srcs, identity=ident):
                for n, src in enumerate(srcs):
                    last = nc.tensor.transpose(dst[:, n * P:(n + 1) * P], src, identity)
                return last

            def mix_arrived(m):
                pe.wait_ge(*mixer_loaded(m))

            pe.wait_ge(ident_loaded, 16)
            for t in range(NT):
                pe.wait_ge(h_ready, t + 1)
                for q in range(2):
                    transposes(bank[4 + 2 * t + q], [h[:, t, (4 * q + n) * P:(4 * q + n + 1) * P] for n in range(4)]) \
                        .then_inc(ht_done, 1)

            def project(m, t, kts=range(KT)):
                a, b = cols[order[m]]
                for k in kts:
                    last = mm(bank[2 * (m % 2) + t][:, 0:b - a], hT[:, k, t * P:(t + 1) * P], in_chunk(m)[:, k, :],
                              start=(k == 0), stop=(k == KT - 1))
                return last

            def split_piece(n, dst, x_hi, x_lo, ts=range(NT), done=None):
                kts, _, high, low = piece_views(n)
                high = high.rearrange("p (k n) -> p k n", k=len(kts))
                low = low.rearrange("p (k n) -> p k n", k=len(kts))
                pe.wait_ge(w_low_ready, n + 1)
                for t in ts:
                    x = slice(t * P, (t + 1) * P)
                    for kk, k in enumerate(kts):
                        mm(dst(t), x_lo[:, k, x], high[:, kk, :], start=(k == 0), stop=False)
                        ins = mm(dst(t), x_hi[:, k, x], high[:, kk, :], start=False, stop=False)
                        if t == NT - 1 and k == kts[-1]:
                            ins.then_inc(w_high_used, 1)
                        ins = mm(dst(t), x_hi[:, k, x], low[:, kk, :], start=False, stop=(k == KT - 1))
                        if k == KT - 1:
                            ins.then_inc(done, 1)

            def project_all(m):
                if m >= 2:
                    pe.wait_ge(z_ready, NT * (m - 1))
                a, b = cols[order[m]]
                for n in range(first_piece[m], first_piece[m + 1] if m < 4 else NP_IN):
                    split_piece(n, lambda t: bank[2 * (m % 2) + t][:, 0:b - a], x_high, x_low, done=z_done)

            pe.wait_ge(ht_low_ready, 2 * NT)
            project_all(0)
            project_all(1)
            pe.wait_ge(krot_ready, 1)
            pe.wait_ge(ht_copied, 2 * NT)
            for t in range(NT):
                transposes(bank[4 + t], [kpad[:, t, n, :] for n in range(2 * NKV)]).then_inc(kt_done, 1)
            project_all(2)
            project_all(3)
            pe.wait_ge(z_ready, NT * 4)
            pe.wait_ge(small_loaded, 16 * 5)
            band = cst("band").rearrange("p (g n) -> p g n", g=NG)
            for g in range(NG):
                dst = bank[6 + g // 2][:, (g % 2) * S:(g % 2 + 1) * S]
                mm(dst[:, 0:P], zu[:, 0, g * P:(g + 1) * P], band[:, g, 0:P], start=True, stop=True)
                mm(dst[:, P:S], zu[:, 0, g * P:(g + 1) * P], band[:, g, P:S], start=True, stop=False)
                mm(dst[:, P:S], zu[:, 1, g * P:(g + 1) * P], band[:, g, S:S + P], start=False, stop=True) \
                    .then_inc(pooled_done, 1)
            project_all(4)
            pe.wait_ge(pooled_copied, 2)
            pe.wait_ge(wsmall_loaded, 32)
            for g in range(NG):
                mm(bank[6 + g // 2][:, (g % 2) * S:(g % 2 + 1) * S], wmix[:, g, :], pooledT[:, g, :],
                   start=True, stop=True).then_inc(mixed_done, 1)
            pe.wait_ge(qrot_ready, 1)
            pe.wait_ge(kt_copied, 2)
            for q in range(4):
                if q < 2:
                    dst = bank[4 + q]
                else:
                    pe.wait_ge(mixed_copied, NG if q == 2 else NG)
                    dst = bank[4 + q]
                t, half = q // 2, q % 2
                transposes(dst, [zq[:, t, (4 * half + n) * P:(4 * half + n + 1) * P] for n in range(4)]) \
                    .then_inc(qt_done, 1)
            pe.wait_ge(qt_copied, 4)

            todo = [(m, t, k) for m in range(5, NIN) for t in range(NT) for k in range(KT)]
            per_step = -(-len(todo) // NU)

            def scores(s):
                n, hp = UNITS[s]
                if s >= 2:
                    pe.wait_ge(masked, s - 1)
                keys = P * (n + 1)
                mm(bank[4 + s % 2][:, 0:2 * keys], qT[:, hp, n * P:(n + 1) * P],
                   kT[:, hp // (NPAIR // NKV), :, 0:keys], start=True, stop=True).then_inc(score_done, 1)

            def probs_transposed(s):
                n, hp = UNITS[s]
                pe.wait_ge(probs_ready, s + 1)
                if s >= 1:
                    pe.wait_ge(pt_copied, s)
                transposes(bank[6], [probs[:, s % 3, c * P:(c + 1) * P] for c in range(2 * (n + 1))]) \
                    .then_inc(pt_done, 1)

            def outputs(s):
                n, hp = UNITS[s]
                g = hp // (NPAIR // NKV)
                pe.wait_ge(pt_copied, s + 1)
                if s >= 1:
                    pe.wait_ge(o_copied, s)
                for k in range(n + 1):
                    for par in range(2):
                        last = mm(bank[7][DH * par:DH * (par + 1), (s % 4) * P:(s % 4 + 1) * P],
                                  zkv[:, k, KVW + g * DH:KVW + (g + 1) * DH],
                                  pT[:, s % 2, (par * (n + 1) + k) * P:(par * (n + 1) + k + 1) * P],
                                  start=(k == 0), stop=(k == n), skip_group_check=True)
                last.then_inc(pv_done, 1)

            for s in range(NU + 3):
                if s < NU:
                    scores(s)
                if 2 <= s < NU + 2:
                    probs_transposed(s - 2)
                for m, t, k in todo[s * per_step:(s + 1) * per_step]:
                    if t == 0 and k == 0:
                        mix_arrived(m)
                        pe.wait_ge(z_ready, NT * (m - 1))
                    last = project(m, t, [k])
                    if k == KT - 1:
                        last.then_inc(z_done, 1)
                if s >= 3:
                    outputs(s - 3)

            mix_arrived(POOL_UP)
            pe.wait_ge(z_ready, NT * NIN)
            for t in range(NT):
                for hh in range(NH):
                    for g in range(NG):
                        last = mm(bank[2 * t + hh][:, :], mixedT[:, g, t * P:(t + 1) * P],
                                  pool_up_sb[:, g, hh * HALF:(hh + 1) * HALF], start=(g == 0), stop=(g == NG - 1))
                    last.then_inc(yp_done, 1)
            def merged_transposed(hh):
                for t in range(NT):
                    pe.wait_ge(merged_ready, 2 * hh + t + 1)
                    transposes(bank[2 * t + hh],
                               [zg[:, 0, t, (4 * hh + n) * P:(4 * hh + n + 1) * P] for n in range(4)]) \
                        .then_inc(mt_done, 1)

            pe.wait_ge(at_low_ready, 2)
            pe.wait_ge(o_copied, NU)
            for n in range(NP_IN, first_piece[WOUT]):
                hh = PIECES[n][0] - WO
                split_piece(n, lambda t: bank[4 + 2 * t + hh][:, :], x_high, x_low, done=ya_done)
                if n == first_piece[WOUT] - 2:
                    merged_transposed(0)
            for n in range(first_piece[WOUT], first_piece[WOUT + 1]):
                pe.wait_ge(mt_low_ready, 2 if n < first_piece[WOUT] + 2 else 4)
                split_piece(n, lambda t: bank[4 + 2 * t][:, :], m_high, m_low, done=out_proj_done)
                if n == first_piece[WOUT]:
                    merged_transposed(1)
            for t in range(NT):
                for n in range(first_piece[WOUT + 1], len(PIECES)):
                    split_piece(n, lambda t: bank[4 + 2 * t + 1][:, :], m_high, m_low, ts=[t], done=out_proj_done)

            for t in range(NT):
                pe.wait_ge(h2_ready, t + 1)
                for q in range(2):
                    transposes(bank[2 * t + q], [h[:, t, (4 * q + n) * P:(4 * q + n + 1) * P] for n in range(4)]) \
                        .then_inc(h2t_done, 1)
            for t in range(NT):
                pe.wait_ge(h2t_copied, 2 * t + 2)
                for k in range(KT):
                    last = mm(bank[4 + t][0:NE, 0:P], w_rt[:, k, :], hT[:, k, t * P:(t + 1) * P],
                              start=(k == 0), stop=(k == KT - 1))
                last.then_inc(logits_done, 1)
            for t in range(NT):
                pe.wait_ge(logits_copied, t + 1)
                nc.tensor.transpose(bank[6 + t][:, 0:NE], lgT[:, t, :], ident[0:NE, 0:NE]).then_inc(lt_done, 1)
            pe.wait_ge(ones_ready, 4)
            pe.wait_ge(sel_ready, 1)
            mm(bank[5][:, 0:NE], upper_bf[:, :], sel_bf[:, 0, :], start=True, stop=True)
            mm(bank[5][:, NE:2 * NE], ones_bf[:, :], sel_bf[:, 0, :], start=True, stop=False)
            mm(bank[5][:, NE:2 * NE], upper_bf[:, :], sel_bf[:, 1, :], start=False, stop=True)
            for t in range(NT):
                last = mm(bank[4][0:NE, 0:CAP], sel_bf[:, t, :], ones_bf[:, 0:CAP], start=(t == 0), stop=(t == NT - 1))
            last.then_inc(rank_done, 1)

            def gather(first=False):
                for k in range(KT):
                    for t in range(NT):
                        last = mm(M[k // 4][:, (k % 4) * P:(k % 4 + 1) * P], h[:, t, k * P:(k + 1) * P],
                                  pick[:, t, :, :], start=(t == 0), stop=(t == NT - 1))
                    if k % 4 == 3:
                        last.then_inc(gathered, 1)

            def overflow_places():
                pe.wait_ge(cols_ready, 1)
                mm(bank[5][0:NE, 0:LEVELS], cst("upper32", NE), over_in, start=True, stop=False)
                mm(bank[5][0:NE, 0:LEVELS], ones_f[:, 0:NE], over_cum, start=False, stop=True)
                mm(bank[5][0:1, 32:33], ones_f[:, 0:1], over_n, start=True, stop=True).then_inc(pos_done, 1)

            def overflow_columns():
                pe.wait_ge(oh_ready, 1)
                for t in range(NT):
                    mm(bank[5][:, 64 + t * OVER:64 + (t + 1) * OVER], rank_cols[:, 0, t * P:(t + 1) * P], over_sel,
                       start=True, stop=False)
                    mm(bank[5][:, 64 + t * OVER:64 + (t + 1) * OVER], ones_f[:, :], over_shift,
                       start=False, stop=True)
                    mm(bank[5][:, 128 + t * OVER:128 + (t + 1) * OVER], rank_cols[:, 1, t * P:(t + 1) * P], over_sel,
                       start=True, stop=True)
                mm(bank[5][0:1, 192:192 + OVER], cst("expert_no", NE)[:, 0:1], over_sel, start=True, stop=True) \
                    .then_inc(over_done, 1)

            pe.wait_ge(pick_ready, 1)
            gather()
            for q in range(2):
                for t in range(NT):
                    last = nc.tensor.transpose(bank[4][0:NE, (2 * q + t) * P:(2 * q + t + 1) * P],
                                               (rank_tab, comb_tab)[q][:, t, 0:NE], ident)
            last.then_inc(cols_done, 1)
            pe.wait_ge(bias3_ready, 2)

            def expert_pair(i, first=False):
                def weights(j):
                    if first and RING <= j < RING + BONUS:
                        pe.wait_ge(bonus_loaded[j - RING], 16)
                        return bonus_places[j - RING]
                    n, src = chunk_place(j, early=first and j < RING)
                    loads = 1 if first and j < RING else (j - BONUS) // RING + 1
                    pe.wait_ge(chunk_loaded[n], i * 32 + 16 * loads)
                    return src

                def layer(which, dst, lhs, after=None):
                    for c in range(4):
                        if after is not None:
                            after(c)
                        wa, wb = weights(8 * which + 2 * c), weights(8 * which + 2 * c + 1)
                        for k in range(CH_KT):
                            kt = c * CH_KT + k
                            for hh in range(NH):
                                for side, w in ((0, wa), (1, wb)):
                                    last = mm(dst[hh][side * CAP:(side + 1) * CAP, :],
                                              lhs[:, kt, side * CAP:(side + 1) * CAP],
                                              w[:, k, hh * HALF:(hh + 1) * HALF],
                                              start=(which == 2 and kt == 0), stop=(kt == KT - 1),
                                              skip_group_check=True)
                        last.then_inc(chunks_used, 2)

                def biases(dst, at):
                    for hh in range(NH):
                        mm(dst[hh][:, :], bsel[:, :, :].rearrange("p x s -> p (x s)"),
                           bias3[:, at + hh * HALF:at + (hh + 1) * HALF], start=True, stop=False,
                           skip_group_check=True)

                pe.wait_ge(bsel_ready, i + 1)
                biases(G, 0)
                layer(0, G, xgT, after=lambda c: pe.wait_ge(xgt_copied, i * 2 + 1 + c // 2) if c % 2 == 0 else None)
                if first:
                    overflow_places()
                else:
                    pe.wait_ge(comb_banks_free, i * 4)
                biases(U, D)
                layer(1, U, xgT)
                pe.wait_ge(pick_ready, i + 2)
                gather()
                if first:
                    overflow_columns()
                for hh in range(NH):
                    pe.wait_ge(a_ready, i * 2 + hh + 1)
                    transposes(G[hh], [act_a[:, (4 * hh + n) * P:(4 * hh + n + 1) * P] for n in range(4)]) \
                        .then_inc(at_done, 1)
                    if hh == 0:
                        pe.wait_ge(pickw_ready, i + 1)
                        for t in range(NT):
                            last = nc.tensor.transpose(
                                U[0][:, t * P:(t + 1) * P],
                                pickw[:, t, :, :].rearrange("p x s -> p (x s)"), ident)
                        last.then_inc(back_done, 1)
                if first:
                    pe.wait_ge(over_ready, 1)
                layer(2, Y, aT, after=lambda c: pe.wait_ge(at_copied, i * 2 + 1 + c // 2) if c % 2 == 0 else None)
                pe.wait_ge(back_copied, i + 1)
                pe.wait_ge(xgt_copied, i * 2 + 4)
                if first:
                    pe.wait_ge(bdn_loaded, 16)
                for t in range(NT):
                    for hh in range(NH):
                        sl = slice(hh * HALF, (hh + 1) * HALF)
                        if t == 0:
                            pe.wait_ge(y_copied, i * 2 + hh + 1)
                        last = mm((M, U)[t][hh][:, :], back[:, t * P:(t + 1) * P], y_sb[:, sl],
                                  start=True, stop=not first)
                        if first:
                            last = mm((M, U)[t][hh][:, :], rank_cols[:, 1, t * P:(t + 1) * P], b_dn[:, sl],
                                      start=False, stop=True)
                        last.then_inc(comb_done, 1)

            expert_pair(0, first=True)
            n_over = pe.value_load(over_i[0:1, OVER:OVER + 1], min_val=0, max_val=OVER)
            with pe.Fori(1, PAIRS) as i:
                expert_pair(i)
            with pe.If(n_over > 0):
                with pe.Fori(0, OVER // 2) as k:
                    with pe.If(k * 2 < n_over):
                        expert_pair(pe.snap(k + PAIRS))

        @block.scalar
        def _(act):
            def copy(dst, src):
                return nc.scalar.activation(dst, src, ACT.Copy)

            nc.scalar.preload_act_table(ACT.Sqrt)
            for t in range(NT):
                act.wait_ge(x_loaded[t], 16)
                nc.scalar.activation(h[:, t, :], resid[:, t, :], ACT.Square, accum_out=ssq[:, t:t + 1]) \
                    .then_inc(sq_done, 1)
                act.wait_ge(ms_ready, t + 1)
                nc.scalar.activation(rms[:, t:t + 1], ms[:, t:t + 1], ACT.Sqrt).then_inc(root_done, 1)
            def w_high(*pieces):
                for n in pieces:
                    _, raw, high, _ = piece_views(n)
                    act.wait_ge(*mixer_loaded(PIECES[n][0]))
                    if n >= SLOTS:
                        act.wait_ge(w_high_used, n - SLOTS + 1)
                    copy(high, raw).then_inc(w_high_ready, 1)

            for t in range(NT):
                for q in range(2):
                    act.wait_ge(ht_done, 2 * t + q + 1)
                    copy(x_high[:, 4 * q:4 * q + 4, t * P:(t + 1) * P],
                         bank[4 + 2 * t + q][:, :].rearrange("p (k s) -> p k s", k=4)).then_inc(ht_high_ready, 1)
            w_high(0, 1, 2, 3)
            for t in range(NT):
                for q in range(2):
                    act.wait_ge(ht_low_ready, 2 * t + q + 1)
                    copy(hT[:, 4 * q:4 * q + 4, t * P:(t + 1) * P],
                         bank[4 + 2 * t + q][:, :].rearrange("p (k s) -> p k s", k=4)).then_inc(ht_copied, 1)
            act.wait_ge(ang_ready, 1)
            nc.scalar.activation(sin_t, ang, ACT.Sin).then_inc(sin_ready, 1)
            nc.scalar.activation(cos_t, rk, ACT.Sin).then_inc(sin_ready, 1)
            w_high(4, 5, 6, 7, 8, 9)
            for t in range(NT):
                act.wait_ge(kt_done, t + 1)
                copy(kT[:, :, :, t * P:(t + 1) * P],
                     bank[4 + t][:, :].rearrange("p (g r s) -> p g r s", g=NKV, r=2)).then_inc(kt_copied, 1)
            w_high(*range(10, NP_IN))
            for q in range(2):
                act.wait_ge(pooled_done, 2 * q + 2)
                copy(pooledT[:, 2 * q:2 * q + 2, :],
                     bank[6 + q][:, :].rearrange("p (g s) -> p g s", g=2)).then_inc(pooled_copied, 1)
            for g in range(NG):
                act.wait_ge(mixed_done, g // 2 * 2 + 2)
                nc.scalar.activation(mixedT[:, g, :], bank[6 + g // 2][:, (g % 2) * S:(g % 2 + 1) * S],
                                     ACT.Copy, scale=pscale[:, g:g + 1]).then_inc(mixed_copied, 1)
            for q in range(4):
                t, half = q // 2, q % 2
                act.wait_ge(qt_done, q + 1)
                copy(qT[:, 4 * half:4 * half + 4, t * P:(t + 1) * P],
                     bank[4 + q][:, :].rearrange("p (k s) -> p k s", k=4)).then_inc(qt_copied, 1)

            def exps(s):
                n, hp = UNITS[s]
                act.wait_ge(max_ready, s + 1)
                keys = P * (n + 1)
                for par in range(2):
                    sl = probs[:, s % 3, par * keys:(par + 1) * keys]
                    nc.scalar.activation(sl, sl, ACT.Exp, bias=mneg[:, par:par + 1],
                                         accum_out=sume[:, par:par + 1])
                nc.scalar.activation(esink, esink, ACT.Exp).then_inc(exp_done, 1)

            def pt_copy(s):
                n, hp = UNITS[s]
                act.wait_ge(pt_done, s + 1)
                if s >= 2:
                    act.wait_ge(pv_done, s - 1)
                copy(pT[:, s % 2, 0:2 * P * (n + 1)], bank[6][:, 0:2 * P * (n + 1)]).then_inc(pt_copied, 1)

            def o_copy(s):
                n, hp = UNITS[s]
                act.wait_ge(pv_done, s + 1)
                copy(attnT[:, hp, n * P:(n + 1) * P], bank[7][:, (s % 4) * P:(s % 4 + 1) * P]).then_inc(o_copied, 1)

            for s in range(NU + 3):
                if s < NU:
                    exps(s)
                if 2 <= s < NU + 2:
                    pt_copy(s - 2)
                if s >= 3:
                    o_copy(s - 3)
                if NU - SLOTS <= s < NU:
                    w_high(NP_IN + s - (NU - SLOTS))
            act.wait_ge(o_copied, NU)
            for q in range(2):
                copy(x_high[:, 4 * q:4 * q + 4, :], attnT[:, 4 * q:4 * q + 4, :]).then_inc(at_high_ready, 1)
            act.wait_ge(z_ready, NT * NIN)
            for br in (1, 0):
                for t in range(NT):
                    nc.scalar.activation(zg[:, br, t, :], zg[:, br, t, :], ACT.Sigmoid).then_inc(gates_ready, 1)
            def merged_high(hh):
                for t in range(NT):
                    act.wait_ge(mt_done, 2 * hh + t + 1)
                    copy(m_high[:, 4 * hh:4 * hh + 4, t * P:(t + 1) * P],
                         bank[2 * t + hh][:, :].rearrange("p (k s) -> p k s", k=4)).then_inc(mt_high_ready, 1)

            w_high(*range(NP_IN + SLOTS, NP_IN + 11))
            merged_high(0)
            w_high(NP_IN + 11)
            merged_high(1)
            w_high(*range(NP_IN + 12, len(PIECES)))
            for t in range(NT):
                act.wait_ge(x1_ready, NT + t + 1)
                nc.scalar.activation(h[:, t, :], resid[:, t, :], ACT.Square, accum_out=ssq[:, t:t + 1]) \
                    .then_inc(sq_done, 1)
                act.wait_ge(ms_ready, NT + t + 1)
                nc.scalar.activation(rms[:, t:t + 1], ms[:, t:t + 1], ACT.Sqrt).then_inc(root_done, 1)
            for q in range(4):
                act.wait_ge(h2t_done, q + 1)
                copy(hT[:, 4 * (q % 2):4 * (q % 2) + 4, (q // 2) * P:(q // 2 + 1) * P],
                     bank[q][:, :].rearrange("p (k s) -> p k s", k=4)).then_inc(h2t_copied, 1)
            for t in range(NT):
                act.wait_ge(logits_done, t + 1)
                copy(lgT[:, t, :], bank[4 + t][0:NE, 0:P]).then_inc(logits_copied, 1)
            for t in range(NT):
                act.wait_ge(top_ready, t + 1)
                nc.scalar.activation(ex[:, t, :], lg[:, t, :], ACT.Exp, bias=neg_top[:, t:t + 1]) \
                    .then_inc(rexp_done, 1)

            def copy_gathered(n):
                for q in range(2):
                    act.wait_ge(gathered, n + q)
                    copy(xgT[:, 4 * q:4 * q + 4, :],
                         M[q][:, :].rearrange("p (k s) -> p k s", k=4)).then_inc(xgt_copied, 1)

            copy_gathered(1)

            def expert_pair(i):
                for hh in range(NH):
                    act.wait_ge(gm_ready, i * 2 + hh + 1)
                    nc.scalar.activation(sg[:, hh * HALF:(hh + 1) * HALF], gm[:, hh * HALF:(hh + 1) * HALF],
                                         ACT.Sigmoid, scale=ALPHA).then_inc(sig_ready, 1)
                copy_gathered(i * 2 + 3)
                for hh in range(NH):
                    act.wait_ge(at_done, i * 2 + hh + 1)
                    copy(aT[:, 4 * hh:4 * hh + 4, :],
                         G[hh][:, :].rearrange("p (k s) -> p k s", k=4)).then_inc(at_copied, 1)
                    if hh == 0:
                        act.wait_ge(back_done, i + 1)
                        copy(back[:, :], U[0][:, 0:S]).then_inc(back_copied, 1)
                act.wait_ge(chunks_used, i * CHUNKS + CHUNKS)
                for hh in range(NH):
                    copy(y_sb[:, hh * HALF:(hh + 1) * HALF], Y[hh][:, :]).then_inc(y_copied, 1)

            expert_pair(0)
            act.wait_ge(over_ready, 1)
            n_over = act.value_load(over_i[0:1, OVER:OVER + 1], min_val=0, max_val=OVER)
            with act.Fori(1, PAIRS) as i:
                expert_pair(i)
            with act.If(n_over > 0):
                with act.Fori(0, OVER // 2) as k:
                    with act.If(k * 2 < n_over):
                        expert_pair(act.snap(k + PAIRS))
            nc.scalar.preload_act_table(ACT.Sqrt)
            for t in range(NT):
                act.wait_ge(fin_ms, t + 1)
                nc.scalar.activation(sg[:, :], resid[:, t, :], ACT.Square, accum_out=ssq[:, t:t + 1]) \
                    .then_inc(fin_sq, 1)
                act.wait_ge(fin_ms, NT + t + 1)
                nc.scalar.activation(rms[:, t:t + 1], ms[:, t:t + 1], ACT.Sqrt).then_inc(fin_root, 1)

        @block.vector
        def _(dve):
            v = nc.vector
            seq = [0]

            def link(ins):
                seq[0] += 1
                ins.then_inc(dve_seq, 1)
                dve.wait_ge(dve_seq, seq[0])

            def norm(t, n, ready):
                dve.wait_ge(sq_done, n)
                v.tensor_scalar(ms[:, t:t + 1], ssq[:, t:t + 1], 1.0 / D, EPS, ALU.mult, ALU.add) \
                    .then_inc(ms_ready, 1)
                dve.wait_ge(root_done, n)
                link(v.reciprocal(rstd[:, t:t + 1], rms[:, t:t + 1]))
                v.scalar_tensor_tensor(h[:, t, :], resid[:, t, :], rstd[:, t:t + 1], gvec[:, :],
                                       ALU.mult, ALU.mult).then_inc(ready, 1)

            def w_low(*pieces):
                for n in pieces:
                    _, raw, high, low = piece_views(n)
                    dve.wait_ge(w_high_ready, n + 1)
                    v.tensor_tensor(low, raw, high.bitcast(f32), ALU.subtract).then_inc(w_low_ready, 1)

            def low_of_bank(dst, src, high, ready):
                v.tensor_tensor(dst, src[:, :].rearrange("p (k s) -> p k s", k=4), high.bitcast(f32),
                                ALU.subtract).then_inc(ready, 1)

            dve.wait_ge(g_mix_loaded, 16)
            for t in range(NT):
                norm(t, t + 1, h_ready)
            for t in range(NT):
                for q in range(2):
                    at = (slice(None), slice(4 * q, 4 * q + 4), slice(t * P, (t + 1) * P))
                    dve.wait_ge(ht_high_ready, 2 * t + q + 1)
                    low_of_bank(x_low[at], bank[4 + 2 * t + q], x_high[at], ht_low_ready)
            w_low(0, 1, 2, 3)

            dve.wait_ge(small_loaded, 16 * 5)
            link(v.tensor_copy(posf, pos_i[:, :]))
            for t in range(NT):
                link(v.tensor_scalar(ang[:, t, :], cst("inv_freq"), posf[:, t:t + 1], None, ALU.mult))
            MAGIC = 12582912.0
            link(v.tensor_scalar(rk, ang, 0.15915494309189535, MAGIC, ALU.mult, ALU.add))
            link(v.tensor_scalar(rk, rk, MAGIC, None, ALU.subtract))
            for part in (6.28125, 0.0019350051879882812, 3.0199159819305583e-07):
                link(v.scalar_tensor_tensor(ang, rk, -part, ang, ALU.mult, ALU.add))
            link(v.tensor_scalar(ang, ang, 3.1415925, -3.1415925, ALU.min, ALU.max))
            link(v.tensor_scalar(rk, ang, -1.0, None, ALU.mult))
            link(v.tensor_tensor(rk, rk, ang, ALU.min))
            v.tensor_scalar(rk, rk, 1.5707963267948966, None, ALU.add).then_inc(ang_ready, 1)

            z_dst = {"kv": lambda t: zkv[:, t, :], "q0": lambda t: zq[:, t, 0:HALF], "q1": lambda t: zq[:, t, HALF:D],
                     "u": lambda t: zu[:, t, :]}
            for n in range(4):
                z_dst[f"g{n}"] = lambda t, n=n: zg[:, n // 2, t, (n % 2) * HALF:(n % 2 + 1) * HALF]

            def take_z(m, t):
                dve.wait_ge(z_done, NT * m + t + 1)
                a, b = cols[order[m]]
                v.tensor_tensor(z_dst[order[m]](t), bank[2 * (m % 2) + t][:, 0:b - a], bias_in[:, m % 3, 0:b - a],
                                ALU.add).then_inc(z_ready, 1)

            def rope(src, heads, dst, t):
                def wide(table):
                    return table[:, t, None, :].to_broadcast([P, 2 * heads, ROT])
                s4 = src.rearrange("p (a r) -> p a r", r=ROT)
                sn = tmp[:, 0:heads * DH]
                link(v.tensor_tensor(sn.rearrange("p (a r) -> p a r", r=ROT), s4, wide(sin_t), ALU.mult))
                link(v.tensor_tensor(s4, s4, wide(cos_t), ALU.mult))
                s_ = src.rearrange("p (a c r) -> p a c r", c=2, r=ROT)
                n_ = sn.rearrange("p (a c r) -> p a c r", c=2, r=ROT)
                link(v.tensor_tensor(dst[:, :, 0, :], s_[:, :, 0, :], n_[:, :, 1, :], ALU.subtract))
                return v.tensor_tensor(dst[:, :, 1, :], s_[:, :, 1, :], n_[:, :, 0, :], ALU.add)

            for t in range(NT):
                take_z(0, t)
            w_low(4, 5)
            dve.wait_ge(z_ready, NT)
            dve.wait_ge(sin_ready, 2)
            dve.wait_ge(kpad_zeroed, 1)
            for t in range(NT):
                k4 = kpad[:, t, :, :].rearrange("p (g r) (c d) -> p g r c d", g=NKV, c=2)
                link(rope(zkv[:, t, 0:KVW], NKV, k4[:, :, 0, 0, :].rearrange("p g (c r) -> p g c r", c=2), t))
                last = v.tensor_copy(k4[:, :, 1, 1, :], k4[:, :, 0, 0, :])
            last.then_inc(krot_ready, 1)
            w_low(6, 7)
            for t in range(NT):
                take_z(1, t)
            w_low(8, 9, 10, 11)
            for t in range(NT):
                take_z(2, t)
            w_low(12, 13)
            dve.wait_ge(z_ready, NT * 3)
            link(rope(zq[:, 0, :], NQ, zq[:, 0, :].rearrange("p (a c r) -> p a c r", c=2, r=ROT), 0))
            w_low(14, 15)
            for t in range(NT):
                take_z(3, t)
            rope(zq[:, 1, :], NQ, zq[:, 1, :].rearrange("p (a c r) -> p a c r", c=2, r=ROT), 1) \
                .then_inc(qrot_ready, 1)
            w_low(16, 17)
            for t in range(NT):
                take_z(4, t)

            def soft_a(s):
                n, hp = UNITS[s]
                keys = P * (n + 1)
                pr = probs[:, s % 3, 0:2 * keys].rearrange("p (a k) -> p a k", a=2)
                dve.wait_ge(score_done, s + 1)
                mask = cst("mask")[:, 2 * P - keys:2 * P]
                for par in range(2):
                    ins = v.scalar_tensor_tensor(pr[:, par, :],
                                                 bank[4 + s % 2][:, par * keys:(par + 1) * keys],
                                                 DH ** -0.5, mask, ALU.mult, ALU.add)
                ins.then_inc(masked, 1)
                dve.wait_ge(masked, s + 1)
                link(v.tensor_reduce(mx, pr, AX.X, ALU.max))
                snk = sinks[:, 2 * hp:2 * hp + 2]
                link(v.tensor_tensor(mx, mx, snk, ALU.max))
                v.tensor_scalar(mneg, mx, -1.0, None, ALU.mult)
                v.tensor_tensor(esink, snk, mx, ALU.subtract).then_inc(max_ready, 1)

            def soft_b(s):
                n, hp = UNITS[s]
                keys = P * (n + 1)
                dve.wait_ge(exp_done, s + 1)
                link(v.tensor_tensor(dens, sume, esink, ALU.add))
                link(v.reciprocal(rden, dens))
                for par in range(2):
                    sl = probs[:, s % 3, par * keys:(par + 1) * keys]
                    ins = v.tensor_scalar(sl, sl, rden[:, par:par + 1], None, ALU.mult)
                ins.then_inc(probs_ready, 1)

            done_per_step = -(-((NIN - 5) * NT * KT) // NU)
            taken = 5 * NT
            for s in range(NU):
                if s >= 3:
                    dve.wait_ge(pt_done, s - 2)
                soft_a(s)
                soft_b(s)
                while taken < NT * NIN and (taken - 5 * NT + 1) * KT <= s * done_per_step:
                    take_z(taken // NT, taken % NT)
                    taken += 1
            while taken < NT * NIN:
                take_z(taken // NT, taken % NT)
                taken += 1

            w_low(NP_IN, NP_IN + 1)
            for q in range(2):
                dve.wait_ge(at_high_ready, q + 1)
                v.tensor_tensor(x_low[:, 4 * q:4 * q + 4, :], attnT[:, 4 * q:4 * q + 4, :],
                                x_high[:, 4 * q:4 * q + 4, :].bitcast(f32), ALU.subtract).then_inc(at_low_ready, 1)
            w_low(NP_IN + 2, NP_IN + 3)

            def split_bias(n, q):
                rows = slice(0, q * NE)
                ins = v.tensor_copy(bias3[rows, n * D:(n + 1) * D], stage[rows, n, :])
                if q > 1:
                    link(ins)
                    rows = slice(0, (q - 1) * NE)
                    link(v.tensor_tensor(stage[rows, n, :], stage[rows, n, :],
                                         bias3[rows, n * D:(n + 1) * D], ALU.subtract))
                else:
                    ins.then_inc(bias3_ready, 1)

            dve.wait_ge(bo_loaded, 16)
            for t in range(NT):
                dve.wait_ge(gates_ready, t + 1)
                for hh in range(NH):
                    sl = slice(hh * HALF, (hh + 1) * HALF)
                    dve.wait_ge(yp_done, 2 * t + hh + 1)
                    v.tensor_tensor(pool_g[:, t, sl], bank[2 * t + hh][:, :], zg[:, 1, t, sl], ALU.mult) \
                        .then_inc(dve_seq, 1)
                    seq[0] += 1
            dve.wait_ge(dve_seq, seq[0])
            for t in range(NT):
                dve.wait_ge(gates_ready, NT + t + 1)
                link(v.tensor_tensor(zg[:, 1, t, :], zg[:, 0, t, :], b_oa, ALU.mult))
                link(v.tensor_tensor(pool_g[:, t, :], pool_g[:, t, :], zg[:, 1, t, :], ALU.add))

            def merge(hh):
                sl = slice(hh * HALF, (hh + 1) * HALF)
                for t in range(NT):
                    dve.wait_ge(ya_done, 2 * hh + t + 1)
                    link(v.tensor_tensor(zg[:, 0, t, sl], bank[4 + 2 * t + hh][:, :], zg[:, 0, t, sl], ALU.mult))
                    v.tensor_tensor(zg[:, 0, t, sl], zg[:, 0, t, sl], pool_g[:, t, sl], ALU.add) \
                        .then_inc(merged_ready, 1)

            def merged_low(hh):
                for t in range(NT):
                    at = (slice(None), slice(4 * hh, 4 * hh + 4), slice(t * P, (t + 1) * P))
                    dve.wait_ge(mt_high_ready, 2 * hh + t + 1)
                    low_of_bank(m_low[at], bank[2 * t + hh], m_high[at], mt_low_ready)

            w_low(NP_IN + 4, NP_IN + 5)
            dve.wait_ge(stage_loaded, 16 * 2 * BPARTS)
            split_bias(0, 3)
            split_bias(0, 2)
            w_low(NP_IN + 6, NP_IN + 7)
            merge(0)
            split_bias(0, 1)
            w_low(NP_IN + 8, NP_IN + 9)
            merged_low(0)
            merge(1)
            w_low(NP_IN + 10, NP_IN + 11)
            merged_low(1)
            split_bias(1, 3)
            w_low(NP_IN + 12, NP_IN + 13)
            split_bias(1, 2)
            w_low(NP_IN + 14, NP_IN + 15)
            split_bias(1, 1)
            dve.wait_ge(g_ffn_loaded, 16)

            def add_mixer(hh, t):
                sl = slice(hh * HALF, (hh + 1) * HALF)
                dve.wait_ge(out_proj_done, 2 * hh + t + 1)
                v.tensor_tensor(resid[:, t, sl], resid[:, t, sl], bank[4 + 2 * t + hh][:, :], ALU.add) \
                    .then_inc(x1_ready, 1)

            for t in range(NT):
                add_mixer(0, t)
            for t in range(NT):
                add_mixer(1, t)
                dve.wait_ge(x1_ready, NT + t + 1)
                norm(t, NT + t + 1, h2_ready)

            dve.wait_ge(ones_ready, 4)
            for t in range(NT):
                dve.wait_ge(lt_done, t + 1)
                link(v.tensor_tensor(lg[:, t, :], bank[6 + t][:, 0:NE], b_rt, ALU.add))
                link(v.max(v8[:, t, :], lg[:, t, :]))
                v.tensor_scalar(neg_top[:, t:t + 1], v8[:, t, 0:1], -1.0, None, ALU.mult).then_inc(top_ready, 1)
                kth = v8[:, t, TOPK - 1:TOPK]
                v.tensor_scalar(gt[:, t, :], lg[:, t, :], kth, None, ALU.is_gt)
                link(v.tensor_scalar(eq[:, t, :], lg[:, t, :], kth, None, ALU.is_equal))
                link(v.tensor_tensor_scan(pre[:, t, :], ones_row, eq[:, t, :], 0.0,
                                          ALU.mult, ALU.add))
            link(v.tensor_reduce(n_gt, gt, AX.X, ALU.add))
            link(v.tensor_scalar(need, n_gt, -1.0, float(TOPK), ALU.mult, ALU.add))
            for t in range(NT):
                link(v.scalar_tensor_tensor(pre[:, t, :], pre[:, t, :], need[:, t:t + 1], eq[:, t, :],
                                            ALU.is_le, ALU.mult))
            link(v.tensor_tensor(sel, pre, gt, ALU.add))
            v.tensor_copy(sel_bf[:, :, :], sel).then_inc(sel_ready, 1)
            dve.wait_ge(rexp_done, 2)
            link(v.tensor_tensor(ex, ex, sel, ALU.mult))
            link(v.tensor_reduce(wden, ex, AX.X, ALU.add))
            link(v.reciprocal(wrden, wden))
            v.memset(rank_tab[:, :, NE + OVER:ENTRIES], 0.0)
            v.memset(comb_tab[:, :, NE + OVER:ENTRIES], 0.0)
            v.memset(bsel_tab[:, NE + OVER:ENTRIES], 0.0)
            v.tensor_copy(bsel_tab[:, 0:NE], cst("bias_sel", BPARTS * NE))
            for t in range(NT):
                v.tensor_scalar(comb_tab[:, t, 0:NE], ex[:, t, :], wrden[:, t:t + 1], None, ALU.mult)
            dve.wait_ge(rank_done, 1)
            v.scalar_tensor_tensor(rank_tab[:, :, 0:NE], bank[5][:, 0:NT * NE].rearrange("p (t e) -> p t e", t=NT),
                                   1.0, sel, ALU.add, ALU.mult)
            v.memset(over_cum[:, 0:1], 0.0)
            for lv in range(LEVELS):
                ins = v.tensor_scalar(over_in[:, lv:lv + 1], bank[4][0:NE, 0:1], float(CAP * (lv + 1)), None,
                                      ALU.is_gt)
            ins.then_inc(tabs_ready, 1)

            slots = cst("slot_no")

            def make_pick(i):
                v.tensor_tensor(pick[:, :, :, :], slots[:, None, None, :].to_broadcast([P, NT, 2, CAP]),
                                rank_tab[:, :, bass.ds(i * 2, 2), None].to_broadcast([P, NT, 2, CAP]),
                                ALU.is_equal).then_inc(pick_ready, 1)

            def make_bsel(i):
                v.tensor_copy(bsel[:, :, :],
                              bsel_tab[:, bass.ds(i * 2, 2), None].to_broadcast([BPARTS * NE, 2, CAP])) \
                    .then_inc(bsel_ready, 1)

            dve.wait_ge(tabs_ready, 1)
            make_pick(0)
            make_bsel(0)
            v.tensor_copy(over_cum[:, 1:2], over_in[:, 0:1])
            link(v.tensor_tensor(over_cum[:, 2:3], over_in[:, 0:1], over_in[:, 1:2], ALU.add))
            link(v.tensor_reduce(over_n, over_in, AX.X, ALU.add))
            dve.wait_ge(cols_done, 1)
            v.tensor_copy(rank_cols[:, :, :], bank[4][0:NE, :].rearrange("p (q s) -> p q s", q=2)) \
                .then_inc(cols_ready, 1)
            def overflow_one_hot():
                dve.wait_ge(pos_done, 1)
                link(v.tensor_copy(over_pos, bank[5][0:NE, 0:LEVELS]))
                for lv in range(LEVELS):
                    link(v.tensor_scalar(oh[:, lv, :], cst("entry_no", NE), over_pos[:, lv:lv + 1],
                                         over_in[:, lv:lv + 1], ALU.is_equal, ALU.mult))
                link(v.tensor_tensor(over_sel, oh[:, 0, :], oh[:, 1, :], ALU.add))
                link(v.tensor_tensor(over_sel, over_sel, oh[:, 2, :], ALU.add))
                link(v.tensor_scalar(over_shift, oh[:, 0, :], -float(CAP), None, ALU.mult))
                for lv in range(1, LEVELS):
                    link(v.scalar_tensor_tensor(over_shift, oh[:, lv, :], -float(CAP * (lv + 1)), over_shift,
                                                ALU.mult, ALU.add))
                for q in range(BPARTS):
                    v.tensor_copy(bsel_tab[q * NE:(q + 1) * NE, NE:NE + OVER], over_sel)
                v.tensor_copy(over_i[:, OVER:OVER + 1], bank[5][0:1, 32:33]).then_inc(oh_ready, 1)

            def overflow_tables():
                dve.wait_ge(over_done, 1)
                tab = bank[5][:, 64:64 + NT * OVER].rearrange("p (t o) -> p t o", t=NT)
                v.tensor_copy(rank_tab[:, :, NE:NE + OVER], tab)
                tab = bank[5][:, 128:128 + NT * OVER].rearrange("p (t o) -> p t o", t=NT)
                v.tensor_copy(comb_tab[:, :, NE:NE + OVER], tab)
                v.tensor_copy(over_i[:, 0:OVER], bank[5][0:1, 192:192 + OVER]).then_inc(over_ready, 1)

            def expert_pair(i, first=False):
                dve.wait_ge(pick_ready, i + 1)
                v.tensor_tensor(pickw[:, :, :, :], pick[:, :, :, :],
                                comb_tab[:, :, bass.ds(i * 2, 2), None].to_broadcast([P, NT, 2, CAP]),
                                ALU.mult).then_inc(pickw_ready, 1)
                dve.wait_ge(pickw_ready, i + 1)
                dve.wait_ge(gathered, i * 2 + 2)
                make_pick(i + 1)
                dve.wait_ge(chunks_used, i * CHUNKS + 8)
                for hh in range(NH):
                    v.tensor_scalar(gm[:, hh * HALF:(hh + 1) * HALF], G[hh][:, :], LIMIT, None, ALU.min) \
                        .then_inc(gm_ready, 1)
                if first:
                    overflow_one_hot()
                dve.wait_ge(chunks_used, i * CHUNKS + 16)
                for hh in range(NH):
                    sl = slice(hh * HALF, (hh + 1) * HALF)
                    v.tensor_scalar(um[:, sl], U[hh][:, :], LIMIT, -LIMIT, ALU.min, ALU.max).then_inc(um_ready, 1)
                    dve.wait_ge(um_ready, i * 2 + hh + 1)
                    v.scalar_tensor_tensor(um[:, sl], um[:, sl], 1.0, gm[:, sl], ALU.add, ALU.mult) \
                        .then_inc(prod_ready, 1)
                    dve.wait_ge(prod_ready, i * 2 + hh + 1)
                    dve.wait_ge(sig_ready, i * 2 + hh + 1)
                    v.tensor_tensor(act_a[:, sl], um[:, sl], sg[:, sl], ALU.mult).then_inc(a_ready, 1)
                make_bsel(i + 1)
                if first:
                    overflow_tables()
                for n in range(4):
                    t, hh = n // 2, n % 2
                    sl = slice(hh * HALF, (hh + 1) * HALF)
                    dve.wait_ge(comb_done, i * 4 + n + 1)
                    v.tensor_tensor(resid[:, t, sl], resid[:, t, sl], (M, U)[t][hh][:, :], ALU.add) \
                        .then_inc(comb_banks_free, 1)

            expert_pair(0, first=True)
            dve.wait_ge(over_ready, 1)
            n_over = dve.value_load(over_i[0:1, OVER:OVER + 1], min_val=0, max_val=OVER)
            with dve.Fori(1, PAIRS) as i:
                expert_pair(i)
            with dve.If(n_over > 0):
                with dve.Fori(0, OVER // 2) as k:
                    with dve.If(k * 2 < n_over):
                        expert_pair(dve.snap(k + PAIRS))

            dve.wait_ge(g_final_loaded, 16)
            v.engine_nop().then_inc(fin_ms, 2)
            for t in range(NT):
                dve.wait_ge(fin_sq, t + 1)
                v.tensor_scalar(ms[:, t:t + 1], ssq[:, t:t + 1], 1.0 / D, EPS, ALU.mult, ALU.add).then_inc(fin_ms, 1)
                dve.wait_ge(fin_root, t + 1)
                link(v.reciprocal(rstd[:, t:t + 1], rms[:, t:t + 1]))
                v.scalar_tensor_tensor(h[:, t, :], resid[:, t, :], rstd[:, t:t + 1], gvec[:, :],
                                       ALU.mult, ALU.mult).then_inc(fin_ready, 1)

        @block.gpsimd
        def _(pool):
            g = nc.gpsimd
            g.memset(kpad[:, :, :, :], 0.0).then_inc(kpad_zeroed, 1)
            g.memset(ones_f[:, :], 1.0).then_inc(ones_ready, 1)
            g.memset(ones_bf[:, :], 1.0).then_inc(ones_ready, 1)
            g.memset(ones_row, 1.0).then_inc(ones_ready, 1)
            pool.wait_ge(small_loaded, 16 * 5)
            g.tensor_copy(upper_bf[:, :], cst("upper")).then_inc(ones_ready, 1)
            pool.wait_ge(h_ready, NT)
            pool.dma_start(gvec[:, :], norm_ffn_g.to_broadcast([P, D])).then_inc(g_ffn_loaded, 16)
            pool.wait_ge(qrot_ready, 1)
            pool.dma_start(b_oa, b_o_attn.to_broadcast([P, D])).then_inc(bo_loaded, 16)
            pool.wait_ge(o_copied, NU)
            pool.dma_start(b_dn, b_down[0]).then_inc(bdn_loaded, 16)
            for n, b in enumerate((b_gate, b_up)):
                for q in range(BPARTS):
                    pool.dma_start(stage[q * NE:(q + 1) * NE, n, :], b[0]).then_inc(stage_loaded, 16)
            pool.wait_ge(h2_ready, NT)
            pool.dma_start(gvec[:, :], norm_final_g.rearrange("(a d) -> a d", a=1).to_broadcast([P, D])) \
                .then_inc(g_final_loaded, 16)


_INS = ["x", "positions", "norm_mix_g", "w_in", "b_in", "attn_sinks", "w_o_attn", "b_o_attn", "w_pool_mix",
        "pool_scale", "w_pool_up", "w_out", "norm_ffn_g", "w_router", "b_router", "w_gate", "b_gate", "w_up",
        "b_up", "w_down", "b_down", "norm_final_g"]
_OUTS = [((1, S, D), "float32")]


def shape_constants():
    import numpy as np

    def at(name):
        a, b = CONST_COLS[name]
        return slice(a, b)

    c = np.zeros((P, CONST_W), np.float32)
    r = np.arange(P)
    c[:, at("ident")] = np.eye(P)
    key = np.arange(2 * P)[None, :]
    dist = r[:, None] + P - key
    c[:, at("mask")] = np.where((dist >= 0) & (dist < P), 0.0, -1e30)
    band = np.zeros((P, NG, 3 * P))
    for g, w in enumerate(WINDOWS):
        for blk, (src, t0) in enumerate(((0, 0), (0, P), (P, P))):
            s_tok = src + r[:, None]
            tok = t0 + r[None, :]
            inside = (tok >= s_tok) & (tok - s_tok < w)
            band[:, g, blk * P:(blk + 1) * P] = inside / np.minimum(tok + 1, w) - (tok == s_tok)
    c[:, at("band")] = band.reshape(P, -1)
    c[:, at("upper")] = r[:, None] < r[None, :]
    c[:, at("slot_no")] = np.arange(1, CAP + 1)
    c[:BPARTS * NE, at("bias_sel")] = (np.arange(BPARTS * NE)[:, None] % NE) == np.arange(NE)
    c[:, at("entry_no")] = np.arange(OVER)
    c[:NE, at("upper32")] = np.arange(NE)[:, None] < np.arange(NE)[None, :]
    c[:NE, at("expert_no")] = np.arange(NE)[:, None]
    c[:, at("inv_freq")] = 10000.0 ** (-np.arange(0, DH, 2) / DH)
    return c


def kernel(**inputs):
    import numpy as _np
    import concourse.bacc as _bacc
    from concourse import mybir as _mybir
    from concourse.bass_utils import run_bass_kernel_spmd as _run

    nc = _bacc.Bacc("TRN2", target_bir_lowering=False, num_devices=1)
    arrays, args = {}, []
    given = {name: inputs[name] for name in _INS}
    given["consts"] = shape_constants()
    for name, a in given.items():
        a = _np.ascontiguousarray(a)
        arrays[f"in_{name}_dram"] = a
        args.append(nc.dram_tensor(f"in_{name}_dram", a.shape, _mybir.dt.from_np(a.dtype), kind="ExternalInput").ap())
    for i, (shape, dtype) in enumerate(_OUTS):
        dt = _mybir.dt.from_np(_np.dtype(dtype))
        args.append(nc.dram_tensor(f"out_{i}_dram", shape, dt, kind="ExternalOutput").ap())
    hybrid_block(nc, *args)
    r = _run(nc, [arrays], core_ids=[0])
    return _np.asarray(r.results[0]["out_0_dram"])
```

```python
from contextlib import ExitStack

import concourse.bass as bass
from concourse import mybir

D = 1024
S = 256
P = 128
NT = S // P
KT = D // P
HALF = 512
NH = D // HALF
DH = 64
NQ = D // DH
NKV = NQ // 8
NPAIR = NQ // 2
ROT = DH // 2
KVW = NKV * DH
POOLW = D // 2
NG = 4
WINDOWS = (2, 4, 8, 16)
IN_W = D + 2 * KVW + POOLW + 2 * D
EPS = 1e-5
LIMIT = 7.0
ALPHA = 1.702
NE = 32
TOPK = 4
CAP = 64
LEVELS = S // CAP - 1
OVER = 16
PAIRS = NE // 2
ENTRIES = NE + OVER + 2
CHUNKS = 24
RING = 12
BONUS = 7
CH_KT = 2
BPARTS = 3

CONST_COLS = {}
_at = 0
for _name, _width in (("ident", P), ("upper", P), ("slot_no", CAP), ("bias_sel", NE), ("entry_no", OVER),
                      ("upper32", NE), ("expert_no", 2), ("inv_freq", ROT), ("mask", 2 * P),
                      ("band", NG * 3 * P)):
    CONST_COLS[_name] = (_at, _at + _width)
    _at += _width
CONST_W = _at


def hybrid_block(nc, x, positions, norm_mix_g, w_in, b_in, attn_sinks, w_o_attn, b_o_attn, w_pool_mix,
                 pool_scale, w_pool_up, w_out, norm_ffn_g, w_router, b_router, w_gate, b_gate, w_up,
                 b_up, w_down, b_down, norm_final_g, consts, out):
    f32 = mybir.dt.float32
    f32r = mybir.dt.float32r
    bf16 = mybir.dt.bfloat16
    i32 = mybir.dt.int32
    ALU = mybir.AluOpType
    ACT = mybir.ActivationFunctionType
    AX = mybir.AxisListType

    ctx = ExitStack()
    with ctx:
        def sb(name, shape, dt=f32):
            return ctx.enter_context(nc.sbuf_tensor(name, shape, dt))

        def sem(name):
            return ctx.enter_context(nc.semaphore(name))

        ring = sb("ring", [P, RING * CH_KT * D])
        resid = sb("resid", [P, NT, D])
        gvec = sb("gvec", [P, D])
        const_wmix = sb("const_wmix", [P, CONST_W + NG * P])
        const = const_wmix[:, 0:CONST_W]
        wmix = const_wmix[:, CONST_W:].rearrange("p (g n) -> p g n", g=NG)
        hT = sb("hT", [P, KT, S])
        h = sb("h", [P, NT, D])
        zq = sb("zq", [P, NT, D])
        zg = sb("zg", [P, 2, NT, D])
        zu_qT = sb("zu_qT", [P, NT * POOLW + NPAIR * S])
        zu = zu_qT[:, 0:NT * POOLW].rearrange("p (t n) -> p t n", t=NT)
        qT = zu_qT[:, NT * POOLW:].rearrange("p (q s) -> p q s", q=NPAIR)
        kpad = sb("kpad", [P, NT, 2 * NKV, P])
        kT = sb("kT", [P, NKV, 2, S])
        bias_zkv = sb("bias_zkv", [P, 3 * HALF + NT * 2 * KVW])
        bias_in = bias_zkv[:, 0:3 * HALF].rearrange("p (m n) -> p m n", m=3)
        zkv = bias_zkv[:, 3 * HALF:].rearrange("p (t n) -> p t n", t=NT)
        tmp = sb("tmp", [P, D + 2 * KVW])
        soft = sb("soft", [P, 5 * HALF])
        probs = soft[:, 0:3 * HALF].rearrange("p (m n) -> p m n", m=3)
        pT = soft[:, 3 * HALF:].rearrange("p (m n) -> p m n", m=2)
        w_rt = sb("w_rt", [P, KT, NE])
        small = sb("small", [P, 672])
        pos_i = sb("pos_i", [P, NT], i32)
        sel_bf = sb("sel_bf", [P, NT, NE], bf16)
        upper_bf = sb("upper_bf", [P, P], bf16)
        ones_bf = sb("ones_bf", [P, P], bf16)
        ones_f = sb("ones_f", [NE, P])
        rank_tab = sb("rank_tab", [P, NT, ENTRIES])
        comb_tab = sb("comb_tab", [P, NT, ENTRIES])
        bsel_tab = sb("bsel_tab", [BPARTS * NE, ENTRIES], bf16)
        bsel = sb("bsel", [BPARTS * NE, 2, CAP], bf16)
        over_i = sb("over_i", [1, OVER + 2], i32)

        def cst(name, rows=P):
            a, b = CONST_COLS[name]
            return const[0:rows, a:b]

        xgT = qT[:, 4:8, :].rearrange("p a (b c) -> p (a b) c", c=P)
        gm = zg[:, 0, 0, :]
        sg = zg[:, 0, 1, :]
        um = zg[:, 1, 0, :]
        act_a = zg[:, 1, 1, :]
        aT = zq[:, 0, :].rearrange("p (k s) -> p k s", s=P)
        y_sb = zq[:, 1, :]
        pick = tmp[:, 0:2 * NT * CAP].rearrange("p (t x s) -> p t x s", t=NT, x=2)
        pickw = tmp[:, 256:512].rearrange("p (t x s) -> p t x s", t=NT, x=2)
        back = tmp[:, 512:768]
        bias3 = kT[:, :, :, :].rearrange("p a b s -> p (a b s)").bitcast(bf16)[0:BPARTS * NE, :]
        b_dn = kpad[0:NE, :, :, :].rearrange("p a b s -> p (a b s)")
        stage = soft[:, 0:HALF]
        stage_part = [soft[:, HALF + q * HALF // 2:HALF + (q + 1) * HALF // 2].bitcast(bf16) for q in range(BPARTS)]
        attnT = zq[:, :, :].rearrange("p t (k s) -> p (t k) s", s=S)
        pooledT = h[:, 0, :].rearrange("p (g s) -> p g s", s=S)
        mixedT = h[:, 1, :].rearrange("p (g s) -> p g s", s=S)
        pool_g = qT[:, :, :].rearrange("p (t k) s -> p t (k s)", t=NT)
        y_pool = [h[:, 0, :], zu_qT[:, 0:NT * POOLW]]
        b_oa = tmp[:, 0:D]

        def piece(at, width):
            return small[:, at:at + width]

        ssq, ms, rms, rstd = piece(0, 2), piece(2, 2), piece(4, 2), piece(6, 2)
        pscale, sinks = piece(8, 4), piece(16, NQ)
        posf = piece(32, 2)
        ang = piece(64, 64).rearrange("p (t r) -> p t r", t=NT)
        rk = piece(128, 64).rearrange("p (t r) -> p t r", t=NT)
        cos_t = piece(192, 64).rearrange("p (t r) -> p t r", t=NT)
        sin_t = piece(256, 64).rearrange("p (t r) -> p t r", t=NT)
        mx, dens = piece(320, 2), piece(322, 2)
        rden = [piece(324 + 2 * b, 2) for b in range(2)]
        mneg, sume, esink = ([piece(34 + 6 * b + 2 * n, 2) for b in range(2)] for n in range(3))
        b_rt = piece(336, NE)
        lg = piece(64, 64).rearrange("p (t e) -> p t e", t=NT)
        ex = piece(128, 64).rearrange("p (t e) -> p t e", t=NT)
        gt = piece(192, 64).rearrange("p (t e) -> p t e", t=NT)
        eq = piece(256, 64).rearrange("p (t e) -> p t e", t=NT)
        pre = piece(368, 64).rearrange("p (t e) -> p t e", t=NT)
        sel = piece(432, 64).rearrange("p (t e) -> p t e", t=NT)
        v8 = piece(496, 16).rearrange("p (t e) -> p t e", t=NT)
        neg_top, n_gt, need, wden, wrden = (piece(512 + 2 * n, 2) for n in range(5))
        over_in = small[0:NE, 522:525]
        over_cum = small[0:NE, 525:528]
        over_pos = small[0:NE, 528:531]
        over_n = small[0:NE, 531:532]
        oh = small[0:NE, 544:592].rearrange("p (l o) -> p l o", l=LEVELS)
        over_sel = small[0:NE, 592:608]
        over_shift = small[0:NE, 608:624]
        rank_cols = tmp[0:NE, 768:768 + 2 * S].rearrange("p (q s) -> p q s", q=2)
        ones_row = piece(640, NE)
        lgT = tmp[0:NE, 0:NT * P].rearrange("p (t s) -> p t s", t=NT)
        bank = [ctx.enter_context(nc.psum_tensor(f"bank{n}", [P, HALF], f32)) for n in range(8)]
        G, U, Y, M = bank[0:2], bank[2:4], bank[4:6], bank[6:8]

        cols = {"kv": (D, D + 2 * KVW), "q0": (0, HALF), "q1": (HALF, D),
                "u": (D + 2 * KVW, D + 2 * KVW + POOLW)}
        g0 = IN_W - 2 * D
        for n, name in enumerate(("ga0", "ga1", "gb0", "gb1")):
            cols[name] = (g0 + n * HALF, g0 + (n + 1) * HALF)
        order = ["kv", "q0", "q1", "u", "gb0", "gb1", None, "ga0", "ga1"]
        POOL_UP, WO = order.index(None), len(order)
        WOUT, MIXN = WO + 2, WO + 4
        NIN = len(order) - 1
        PLACES = 4
        PW = KT * HALF

        def is_input(m):
            return m < WO and m != POOL_UP

        def z_no(m):
            return m - (m > POOL_UP)

        def width_of(m):
            return cols[order[m]][1] - cols[order[m]][0] if is_input(m) else HALF

        def place(m):
            return ring[:, (m % PLACES) * PW:(m % PLACES + 1) * PW]

        def in_chunk(m):
            a, b = cols[order[m]]
            return place(m)[:, 0:KT * (b - a)].rearrange("p (k n) -> p k n", k=KT)

        def half_chunk(m):
            return place(m).rearrange("p (k n) -> p k n", k=KT)

        pool_up_sb = place(POOL_UP).rearrange("p (k n) -> p k n", k=NG)

        def f32r_at(name, words, base, shift=0):
            addr = nc.lookup_mls(base).memorylocations[0].addr + 4 * shift
            return nc.alloc_sbuf_tensor_at(name, [P, words], f32r, offset=addr).ap()

        def by_tokens(ap):
            return ap.rearrange("p (k s) -> p k s", s=S)

        GRAN = 1024
        SLOTS = 4
        w_low_all = f32r_at("w_low", PLACES * PW, ring)
        x_high = by_tokens(f32r_at("x_high", KT * S, ring, PLACES * PW))
        x_low = by_tokens(f32r_at("x_low", KT * S, ring, PLACES * PW + KT * S))
        w_high_all = f32r_at("w_high", SLOTS * GRAN, ring, PLACES * PW + 2 * KT * S)
        a_high = by_tokens(f32r_at("a_high", KT * S, hT))
        a_low = by_tokens(f32r_at("a_low", KT * S, zq))

        PIECES = []
        first_piece = {}
        for m in range(MIXN):
            if m != POOL_UP:
                first_piece[m] = len(PIECES)
                PIECES += [(m, c) for c in range(KT * width_of(m) // GRAN)]
        NP_A = first_piece[POOL_UP + 1]
        NP_B = first_piece[POOL_UP + 2]

        def piece_views(n):
            m, c = PIECES[n]
            nk = GRAN // width_of(m)
            at = (m % PLACES) * PW + c * GRAN
            return (range(c * nk, (c + 1) * nk), ring[:, at:at + GRAN],
                    w_high_all[:, n % SLOTS * GRAN:(n % SLOTS + 1) * GRAN], w_low_all[:, at:at + GRAN])

        def mixer_loaded(m):
            return mix_loaded[m % PLACES], sum(32 if is_input(n) else 16 for n in range(m % PLACES, m + 1, PLACES))

        FIRST = 2

        def chunk_place(j, early=False):
            n = (j + FIRST - (0 if early else BONUS)) % RING
            return n, ring[:, n * CH_KT * D:(n + 1) * CH_KT * D].rearrange("p (k n) -> p k n", k=CH_KT)

        mask_at = CONST_COLS["mask"][0]
        bonus_places = [m.rearrange("p (k n) -> p k n", k=CH_KT) for m in (
            zq[:, :, :].rearrange("p t d -> p (t d)"), zg[:, 1, :, :].rearrange("p t d -> p (t d)"),
            soft[:, 0:CH_KT * D], const_wmix[:, mask_at:mask_at + CH_KT * D], bias_zkv[:, :],
            zu_qT[:, 0:CH_KT * D], hT[:, :, :].rearrange("p k s -> p (k s)"))]
        B_ZQ, B_ZG, B_SOFT, B_CONST, B_ZKV, B_ZU, B_HT = range(BONUS)

        x_loaded = [sem(f"x_loaded{t}") for t in range(NT)]
        ident_loaded, small_loaded, wsmall_loaded = sem("ident_loaded"), sem("small_loaded"), sem("wsmall_loaded")
        g_mix_loaded, g_ffn_loaded, g_final_loaded = sem("g_mix_loaded"), sem("g_ffn_loaded"), sem("g_final_loaded")
        mix_loaded = [sem(f"mix_loaded{n}") for n in range(PLACES)]
        chunk_loaded = [sem(f"chunk_loaded{n}") for n in range(RING)]
        bonus_loaded = [sem(f"bonus_loaded{n}") for n in range(BONUS)]
        chunks_used = sem("chunks_used")
        bo_loaded, stage_loaded, bdn_loaded = sem("bo_loaded"), sem("stage_loaded"), sem("bdn_loaded")
        ones_ready, kpad_zeroed = sem("ones_ready"), sem("kpad_zeroed")
        parts_ready, bias3_ready = sem("parts_ready"), sem("bias3_ready")
        dve_seq = sem("dve_seq")
        sq_done, root_done, ms_ready, h_ready = sem("sq_done"), sem("root_done"), sem("ms_ready"), sem("h_ready")
        ht_done, first_loaded = sem("ht_done"), sem("first_loaded")
        w_high_ready, w_low_ready, w_high_used = sem("w_high_ready"), sem("w_low_ready"), sem("w_high_used")
        ht_high_ready, ht_low_ready = sem("ht_high_ready"), sem("ht_low_ready")
        at_high_ready, at_low_ready = sem("at_high_ready"), sem("at_low_ready")
        z_done, z_ready = sem("z_done"), sem("z_ready")
        ang_ready, sin_ready = sem("ang_ready"), sem("sin_ready")
        krot_ready, qrot_ready = sem("krot_ready"), sem("qrot_ready")
        kt_done, kt_copied, qt_done, qt_copied = sem("kt_done"), sem("kt_copied"), sem("qt_done"), sem("qt_copied")
        pooled_done, pooled_copied, mixed_done, mixed_copied = (
            sem("pooled_done"), sem("pooled_copied"), sem("mixed_done"), sem("mixed_copied"))
        score_done, masked, max_ready, exp_done, probs_ready = (
            sem("score_done"), sem("masked"), sem("max_ready"), sem("exp_done"), sem("probs_ready"))
        rden_ready = sem("rden_ready")
        pt_done, pt_copied, pv_done, o_copied = sem("pt_done"), sem("pt_copied"), sem("pv_done"), sem("o_copied")
        gates_ready, yp_done, yp_copied, ya_done, merged_ready = (
            sem("gates_ready"), sem("yp_done"), sem("yp_copied"), sem("ya_done"), sem("merged_ready"))
        mt_done, mt_high_ready, mt_low_ready, out_proj_done, x1_ready = (
            sem("mt_done"), sem("mt_high_ready"), sem("mt_low_ready"), sem("out_proj_done"), sem("x1_ready"))
        h2_ready, h2t_done, h2t_copied, logits_done, logits_copied, lt_done = (
            sem("h2_ready"), sem("h2t_done"), sem("h2t_copied"), sem("logits_done"),
            sem("logits_copied"), sem("lt_done"))
        top_ready, rexp_done, sel_ready, rank_done = (
            sem("top_ready"), sem("rexp_done"), sem("sel_ready"), sem("rank_done"))
        tabs_ready, cols_done, cols_ready, pos_done, oh_ready, over_done, over_ready = (
            sem("tabs_ready"), sem("cols_done"), sem("cols_ready"), sem("pos_done"), sem("oh_ready"),
            sem("over_done"), sem("over_ready"))
        pick_ready, pickw_ready, bsel_ready = sem("pick_ready"), sem("pickw_ready"), sem("bsel_ready")
        gathered, xgt_copied = sem("gathered"), sem("xgt_copied")
        gm_ready, sig_ready, um_ready, prod_ready, a_ready = (
            sem("gm_ready"), sem("sig_ready"), sem("um_ready"), sem("prod_ready"), sem("a_ready"))
        at_done, at_copied, back_done, back_copied = (
            sem("at_done"), sem("at_copied"), sem("back_done"), sem("back_copied"))
        y_copied = [sem(f"y_copied{hh}") for hh in range(NH)]
        comb_done, comb_banks_free = sem("comb_done"), sem("comb_banks_free")
        all_added = sem("all_added")
        fin_sq, fin_root, fin_ms, fin_ready, stored = (
            sem("fin_sq"), sem("fin_root"), sem("fin_ms"), sem("fin_ready"), sem("stored"))

        def mixer_chunk_used(m):
            if is_input(m):
                return z_done, NT * (z_no(m) + 1)
            if m == POOL_UP:
                return yp_done, NT * NH
            if m < WOUT:
                return ya_done, NT * (m - WO + 1)
            return out_proj_done, NT * (m - WOUT + 1)

        block = ctx.enter_context(nc.Block())

        W_STEPS = [1, 3, 5, 7, 12, 14]
        UNITS = [(n, hp) for n in range(NT) for hp in range(NPAIR)]
        NU = len(UNITS)

        @block.sync
        def _(sp):
            for t in range(NT):
                sp.dma_start(resid[:, t, :], x[0, t * P:(t + 1) * P, :]).then_inc(x_loaded[t], 16)
                if t == 0:
                    sp.dma_start(gvec[:, :], norm_mix_g.to_broadcast([P, D])).then_inc(g_mix_loaded, 16)
            sp.dma_start(const[:, 0:P], consts[:, 0:P]).then_inc(ident_loaded, 16)

            def load_mixer(m):
                if m >= PLACES:
                    sp.wait_ge(*mixer_chunk_used(m - PLACES))
                if is_input(m):
                    a, b = cols[order[m]]
                    z = z_no(m)
                    if z >= 3:
                        sp.wait_ge(z_ready, NT * (z - 2))
                    src = w_in[0, :, a:b].rearrange("(k p) n -> p k n", p=P)
                    k0 = 0
                    if m == 0:
                        k0 = KT // 2
                        sp.dma_start(in_chunk(m)[:, 0:k0, :], src[:, 0:k0, :]).then_inc(first_loaded, 16)
                    sp.dma_start(bias_in[:, z % 3, 0:b - a],
                                 b_in[:, a:b].to_broadcast([P, b - a])).then_inc(mix_loaded[m % PLACES], 16)
                    sp.dma_start(in_chunk(m)[:, k0:KT, :], src[:, k0:KT, :]).then_inc(mix_loaded[m % PLACES], 16)
                elif m == POOL_UP:
                    sp.dma_start(pool_up_sb, w_pool_up[0].rearrange("(k p) n -> p k n", p=P)) \
                        .then_inc(mix_loaded[m % PLACES], 16)
                else:
                    src, hh = (w_o_attn, m - WO) if m < WOUT else (w_out, m - WOUT)
                    sp.dma_start(half_chunk(m), src[0, :, hh * HALF:(hh + 1) * HALF]
                                 .rearrange("(k p) n -> p k n", p=P)).then_inc(mix_loaded[m % PLACES], 16)

            load_mixer(0)
            with nc.allow_non_contiguous_dma(reason="a few hundred words"):
                sp.dma_start(pos_i[:, :], positions[0].rearrange("(t p) -> p t", p=P)).then_inc(small_loaded, 16)
                sp.dma_start(pscale, pool_scale[0].rearrange("(g p) -> p g", p=P)).then_inc(small_loaded, 16)
            load_mixer(1)
            sp.dma_start(const[:, P:], consts[:, P:]).then_inc(small_loaded, 16)
            sp.dma_start(sinks, attn_sinks.to_broadcast([P, NQ])).then_inc(small_loaded, 16)
            sp.dma_start(b_rt, b_router.to_broadcast([P, NE])).then_inc(small_loaded, 16)
            load_mixer(2)
            sp.dma_start(wmix[:, :, :], w_pool_mix[0].rearrange("g c d -> c g d")).then_inc(wsmall_loaded, 16)
            sp.dma_start(w_rt[:, :, :], w_router[0].rearrange("(k p) e -> p k e", p=P)).then_inc(wsmall_loaded, 16)
            for m in range(3, MIXN):
                load_mixer(m)

            matrices = (w_gate, w_up, w_down)

            def load_chunk(j, expert_a, expert_b, early=False, bonus=None):
                which, piece_no, side = j // 8, j % 8 // 2, j % 2
                e = (expert_a, expert_b)[side]
                n, dst = chunk_place(j, early)
                signal = chunk_loaded[n]
                if bonus is not None:
                    dst, signal = bonus_places[bonus], bonus_loaded[bonus]
                rows = slice(piece_no * CH_KT * P, (piece_no + 1) * CH_KT * P)
                sp.dma_start(dst, matrices[which][0, bass.ds(e, 1), rows, :]
                             .rearrange("o (k p) n -> p (o k) n", p=P)).then_inc(signal, 16)

            def chunk_free(count):
                sp.wait_ge(chunks_used, count)
                sp.nop(nofuse=True)

            def load_first(*js):
                for j in js:
                    n = chunk_place(j, early=True)[0] // 2
                    if n >= PLACES:
                        sp.wait_ge(out_proj_done, NT * NH)
                    else:
                        sp.wait_ge(*mixer_chunk_used(max(m for m in range(MIXN) if m % PLACES == n)))
                    load_chunk(j, 0, 1, early=True)

            def load_bonus(b):
                load_chunk(RING + b, 0, 1, bonus=b)

            sp.wait_ge(pv_done, NU)
            load_bonus(B_CONST)
            sp.wait_ge(z_ready, NT * NIN)
            load_bonus(B_ZKV)
            load_first(0, 1, 2, 3)
            load_bonus(B_ZQ)
            sp.wait_ge(merged_ready, NT * NH)
            load_bonus(B_ZG)
            load_bonus(B_ZU)
            load_first(4, 5)
            sp.wait_ge(bias3_ready, 16 * BPARTS * 2 * NH)
            load_bonus(B_SOFT)
            load_first(6, 7, 8, 9, 10, 11)
            sp.wait_ge(logits_done, NT)
            load_bonus(B_HT)
            for j in range(RING + BONUS, CHUNKS):
                chunk_free(j - RING - BONUS + 1)
                load_chunk(j, 0, 1)
            for j in range(BONUS):
                chunk_free(CHUNKS + j - RING - BONUS + 1)
                load_chunk(j, 2, 3)
            with sp.Fori(1, PAIRS - 1) as i:
                for j in range(BONUS, CHUNKS):
                    chunk_free(i * CHUNKS + (j - RING + 1))
                    load_chunk(j, i * 2, i * 2 + 1)
                for j in range(BONUS):
                    chunk_free(i * CHUNKS + (CHUNKS + j - RING + 1))
                    load_chunk(j, i * 2 + 2, i * 2 + 3)
            for j in range(BONUS, CHUNKS):
                chunk_free((PAIRS - 1) * CHUNKS + j - RING + 1)
                load_chunk(j, NE - 2, NE - 1)

            sp.wait_ge(over_ready, 1)
            n_over = sp.value_load(over_i[0:1, OVER:OVER + 1], min_val=0, max_val=OVER)
            with sp.If(n_over > 0):
                with sp.Fori(0, OVER // 2) as k:
                    with sp.If(k * 2 < n_over):
                        expert_a = sp.value_load(over_i[0:1, bass.ds(k * 2, 1)], min_val=0, max_val=NE - 1)
                        expert_b = sp.value_load(over_i[0:1, bass.ds(k * 2 + 1, 1)], min_val=0, max_val=NE - 1)
                        for j in range(CHUNKS):
                            chunk_free((k + PAIRS) * CHUNKS + (j - RING + 1))
                            load_chunk(j, expert_a, expert_b)

            for n in range(NT * NH):
                t, sl = n // NH, slice(n % NH * HALF, (n % NH + 1) * HALF)
                sp.wait_ge(fin_ready, n + 1)
                sp.dma_start(out[0, t * P:(t + 1) * P, sl], h[:, t, sl]).then_inc(stored, 16)
            sp.wait_ge(stored, 16 * NT * NH)

        @block.tensor
        def _(pe):
            mm = nc.tensor.matmul
            ident = cst("ident")

            def transposes(dst, srcs, identity=ident):
                for n, src in enumerate(srcs):
                    last = nc.tensor.transpose(dst[:, n * P:(n + 1) * P], src, identity)
                return last

            def mix_arrived(m):
                pe.wait_ge(*mixer_loaded(m))

            pe.wait_ge(ident_loaded, 16)
            for t in range(NT):
                pe.wait_ge(h_ready, t + 1)
                for q in range(2):
                    transposes(bank[4 + 2 * t + q], [h[:, t, (4 * q + n) * P:(4 * q + n + 1) * P] for n in range(4)]) \
                        .then_inc(ht_done, 1)

            def z_bank(m, t):
                return bank[2 * (z_no(m) % 2) + t][:, 0:width_of(m)]

            def split_piece(n, dst, x_hi, x_lo, ts=range(NT), done=None):
                kts, _, high, low = piece_views(n)
                high = high.rearrange("p (k n) -> p k n", k=len(kts))
                low = low.rearrange("p (k n) -> p k n", k=len(kts))
                pe.wait_ge(w_low_ready, n + 1)
                for t in ts:
                    x = slice(t * P, (t + 1) * P)
                    for kk, k in enumerate(kts):
                        mm(dst(t), x_lo[:, k, x], high[:, kk, :], start=(k == 0), stop=False)
                        ins = mm(dst(t), x_hi[:, k, x], high[:, kk, :], start=False, stop=False)
                        if t == NT - 1 and k == kts[-1]:
                            ins.then_inc(w_high_used, 1)
                        ins = mm(dst(t), x_hi[:, k, x], low[:, kk, :], start=False, stop=(k == KT - 1))
                        if k == KT - 1:
                            ins.then_inc(done, 1)

            def project_all(m, skip=0):
                if 2 <= m < POOL_UP:
                    pe.wait_ge(z_ready, NT * (m - 1))
                elif m > POOL_UP:
                    pe.wait_ge(yp_copied, NT * (m - POOL_UP))
                for n in range(first_piece[m] + skip, first_piece[m] + KT * width_of(m) // GRAN):
                    split_piece(n, lambda t: z_bank(m, t), x_high, x_low, done=z_done)

            for t in range(NT):
                pe.wait_ge(ht_low_ready, 2 * t + 2)
                for n in range(first_piece[1]):
                    split_piece(n, lambda t: z_bank(0, t), x_high, x_low, ts=[t], done=z_done)
            project_all(1)
            pe.wait_ge(krot_ready, 1)
            for t in range(NT):
                transposes(bank[4 + t], [kpad[:, t, n, :] for n in range(2 * NKV)]).then_inc(kt_done, 1)
            project_all(2)
            project_all(3)
            pe.wait_ge(z_ready, NT * 4)
            pe.wait_ge(small_loaded, 16 * 5)
            band = cst("band").rearrange("p (g n) -> p g n", g=NG)
            for g in range(NG):
                dst = bank[6 + g // 2][:, (g % 2) * S:(g % 2 + 1) * S]
                mm(dst[:, 0:P], zu[:, 0, g * P:(g + 1) * P], band[:, g, 0:P], start=True, stop=True)
                mm(dst[:, P:S], zu[:, 0, g * P:(g + 1) * P], band[:, g, P:S], start=True, stop=False)
                mm(dst[:, P:S], zu[:, 1, g * P:(g + 1) * P], band[:, g, S:S + P], start=False, stop=True) \
                    .then_inc(pooled_done, 1)
            project_all(4)
            pe.wait_ge(pooled_copied, 2)
            pe.wait_ge(wsmall_loaded, 32)
            for g in range(NG):
                mm(bank[6 + g // 2][:, (g % 2) * S:(g % 2 + 1) * S], wmix[:, g, :], pooledT[:, g, :],
                   start=True, stop=True).then_inc(mixed_done, 1)
            project_all(5)
            pe.wait_ge(qrot_ready, 1)
            pe.wait_ge(kt_copied, 2)
            for q in range(4):
                if q < 2:
                    dst = bank[4 + q]
                else:
                    pe.wait_ge(mixed_copied, NG if q == 2 else NG)
                    dst = bank[4 + q]
                t, half = q // 2, q % 2
                transposes(dst, [zq[:, t, (4 * half + n) * P:(4 * half + n + 1) * P] for n in range(4)]) \
                    .then_inc(qt_done, 1)
            pe.wait_ge(qt_copied, 4)

            pool_up = [(hh, t, g) for hh in range(NH) for t in range(NT) for g in range(NG)]
            BESIDE = 2
            next_input = [(n, t) for n in range(NP_A, NP_B + BESIDE) for t in range(NT)]
            POOL_STEPS = len(pool_up) // 2

            def pool_up_product(hh, t, g):
                if t == 0 and g == 0:
                    mix_arrived(POOL_UP)
                    pe.wait_ge(z_ready, NT * (POOL_UP - 1 + hh))
                ins = mm(bank[2 * hh + t][:, :], mixedT[:, g, t * P:(t + 1) * P],
                         pool_up_sb[:, g, hh * HALF:(hh + 1) * HALF], start=(g == 0), stop=(g == NG - 1))
                if g == NG - 1:
                    ins.then_inc(yp_done, 1)

            def between(s):
                if s < POOL_STEPS:
                    for step in pool_up[2 * s:2 * s + 2]:
                        pool_up_product(*step)
                elif s - POOL_STEPS < len(next_input):
                    n, t = next_input[s - POOL_STEPS]
                    m = PIECES[n][0]
                    pe.wait_ge(yp_copied, NT * (m - POOL_UP))
                    split_piece(n, lambda t: z_bank(m, t), x_high, x_low, ts=[t], done=z_done)

            def scores(s):
                n, hp = UNITS[s]
                if s >= 2:
                    pe.wait_ge(masked, s - 1)
                keys = P * (n + 1)
                mm(bank[4 + s % 2][:, 0:2 * keys], qT[:, hp, n * P:(n + 1) * P],
                   kT[:, hp // (NPAIR // NKV), :, 0:keys], start=True, stop=True).then_inc(score_done, 1)

            def probs_transposed(s):
                n, hp = UNITS[s]
                pe.wait_ge(probs_ready, s + 1)
                if s >= 1:
                    pe.wait_ge(pt_copied, s)
                transposes(bank[6], [probs[:, s % 3, c * P:(c + 1) * P] for c in range(2 * (n + 1))]) \
                    .then_inc(pt_done, 1)

            def outputs(s):
                n, hp = UNITS[s]
                g = hp // (NPAIR // NKV)
                pe.wait_ge(pt_copied, s + 1)
                if s >= 1:
                    pe.wait_ge(o_copied, s)
                for k in range(n + 1):
                    for par in range(2):
                        last = mm(bank[7][DH * par:DH * (par + 1), (s % 4) * P:(s % 4 + 1) * P],
                                  zkv[:, k, KVW + g * DH:KVW + (g + 1) * DH],
                                  pT[:, s % 2, (par * (n + 1) + k) * P:(par * (n + 1) + k + 1) * P],
                                  start=(k == 0), stop=(k == n), skip_group_check=True)
                last.then_inc(pv_done, 1)

            for s in range(NU + 3):
                if s < NU:
                    scores(s)
                between(s)
                if 2 <= s < NU + 2:
                    probs_transposed(s - 2)
                if s >= 3:
                    outputs(s - 3)

            between(NU + 3)
            project_all(POOL_UP + 2, skip=BESIDE)
            def merged_transposed(hh):
                for t in range(NT):
                    pe.wait_ge(merged_ready, 2 * hh + t + 1)
                    transposes(bank[2 * t + hh],
                               [zg[:, 0, t, (4 * hh + n) * P:(4 * hh + n + 1) * P] for n in range(4)]) \
                        .then_inc(mt_done, 1)

            pe.wait_ge(at_low_ready, 2)
            pe.wait_ge(o_copied, NU)
            for n in range(first_piece[WO], first_piece[WOUT]):
                hh = PIECES[n][0] - WO
                split_piece(n, lambda t: bank[4 + 2 * t + hh][:, :], a_high, a_low, done=ya_done)
                if n == first_piece[WOUT] - 2:
                    merged_transposed(0)
            for n in range(first_piece[WOUT], first_piece[WOUT + 1]):
                pe.wait_ge(mt_low_ready, 2 if n < first_piece[WOUT] + 2 else 4)
                split_piece(n, lambda t: bank[4 + 2 * t][:, :], x_high, x_low, done=out_proj_done)
                if n == first_piece[WOUT]:
                    merged_transposed(1)
            for t in range(NT):
                for n in range(first_piece[WOUT + 1], len(PIECES)):
                    split_piece(n, lambda t: bank[4 + 2 * t + 1][:, :], x_high, x_low, ts=[t], done=out_proj_done)

            def logits_by_tokens(t):
                pe.wait_ge(logits_copied, t + 1)
                nc.tensor.transpose(bank[6 + t][:, 0:NE], lgT[:, t, :], ident[0:NE, 0:NE]).then_inc(lt_done, 1)

            for t in range(NT):
                pe.wait_ge(h2_ready, t + 1)
                for q in range(2):
                    transposes(bank[2 * t + q], [h[:, t, (4 * q + n) * P:(4 * q + n + 1) * P] for n in range(4)]) \
                        .then_inc(h2t_done, 1)
                if t == 1:
                    logits_by_tokens(0)
                for k in range(KT):
                    if k % 4 == 0:
                        pe.wait_ge(h2t_copied, 2 * t + k // 4 + 1)
                    last = mm(bank[4 + t][0:NE, 0:P], w_rt[:, k, :], hT[:, k, t * P:(t + 1) * P],
                              start=(k == 0), stop=(k == KT - 1))
                last.then_inc(logits_done, 1)
            logits_by_tokens(1)
            pe.wait_ge(ones_ready, 4)
            pe.wait_ge(sel_ready, 1)
            mm(bank[5][:, 0:NE], upper_bf[:, :], sel_bf[:, 0, :], start=True, stop=True)
            mm(bank[5][:, NE:2 * NE], ones_bf[:, :], sel_bf[:, 0, :], start=True, stop=False)
            mm(bank[5][:, NE:2 * NE], upper_bf[:, :], sel_bf[:, 1, :], start=False, stop=True)
            for t in range(NT):
                last = mm(bank[4][0:NE, 0:CAP], sel_bf[:, t, :], ones_bf[:, 0:CAP], start=(t == 0), stop=(t == NT - 1))
            last.then_inc(rank_done, 1)

            def gather():
                for k in range(KT):
                    for t in range(NT):
                        last = mm(M[k // 4][:, (k % 4) * P:(k % 4 + 1) * P], h[:, t, k * P:(k + 1) * P],
                                  pick[:, t, :, :], start=(t == 0), stop=(t == NT - 1))
                    if k % 4 == 3:
                        last.then_inc(gathered, 1)

            def table_columns():
                for q in range(2):
                    for t in range(NT):
                        last = nc.tensor.transpose(bank[4][0:NE, (2 * q + t) * P:(2 * q + t + 1) * P],
                                                   (rank_tab, comb_tab)[q][:, t, 0:NE], ident)
                last.then_inc(cols_done, 1)

            def overflow_places():
                pe.wait_ge(cols_ready, 1)
                mm(bank[5][0:NE, 0:LEVELS], cst("upper32", NE), over_in, start=True, stop=False)
                mm(bank[5][0:NE, 0:LEVELS], ones_f[:, 0:NE], over_cum, start=False, stop=True)
                mm(bank[5][0:1, 32:33], ones_f[:, 0:1], over_n, start=True, stop=True).then_inc(pos_done, 1)

            def overflow_columns():
                pe.wait_ge(oh_ready, 1)
                for t in range(NT):
                    mm(bank[5][:, 64 + t * OVER:64 + (t + 1) * OVER], rank_cols[:, 0, t * P:(t + 1) * P], over_sel,
                       start=True, stop=False)
                    mm(bank[5][:, 64 + t * OVER:64 + (t + 1) * OVER], ones_f[:, :], over_shift,
                       start=False, stop=True)
                    mm(bank[5][:, 128 + t * OVER:128 + (t + 1) * OVER], rank_cols[:, 1, t * P:(t + 1) * P], over_sel,
                       start=True, stop=True)
                mm(bank[5][0:1, 192:192 + OVER], cst("expert_no", NE)[:, 0:1], over_sel, start=True, stop=True) \
                    .then_inc(over_done, 1)

            pe.wait_ge(pick_ready, 1)
            gather()
            pe.wait_ge(bias3_ready, 16 * BPARTS * 2 * NH)

            def expert_pair(i, first=False, second=False):
                def weights(j):
                    if first and RING <= j < RING + BONUS:
                        pe.wait_ge(bonus_loaded[j - RING], 16)
                        return bonus_places[j - RING]
                    n, src = chunk_place(j, early=first and j < RING)
                    loads = 1 if first and j < RING else (j - BONUS) // RING + 1
                    pe.wait_ge(chunk_loaded[n], i * 32 + 16 * loads)
                    return src

                def layer(which, dst, lhs, after=None):
                    for c in range(4):
                        if after is not None:
                            after(c)
                        wa = weights(8 * which + 2 * c)
                        steps = [(k, hh, side) for k in range(CH_KT) for hh in range(NH) for side in range(2)]
                        if which == 2 and c == 3:
                            steps.sort(key=lambda step: step[2])
                        else:
                            wb = weights(8 * which + 2 * c + 1)
                        for n, (k, hh, side) in enumerate(steps):
                            if which == 2 and c == 3 and n == len(steps) // 2:
                                wb = weights(8 * which + 2 * c + 1)
                            kt = c * CH_KT + k
                            w = wb if side else wa
                            last = mm(dst[hh][side * CAP:(side + 1) * CAP, :], lhs[:, kt, side * CAP:(side + 1) * CAP],
                                      w[:, k, hh * HALF:(hh + 1) * HALF], start=(which == 2 and kt == 0),
                                      stop=(kt == KT - 1), skip_group_check=True)
                        last.then_inc(chunks_used, 2)

                def biases(dst, at):
                    for hh in range(NH):
                        mm(dst[hh][:, :], bsel[:, :, :].rearrange("p x s -> p (x s)"),
                           bias3[:, at + hh * HALF:at + (hh + 1) * HALF], start=True, stop=False,
                           skip_group_check=True)

                pe.wait_ge(bsel_ready, i + 1)
                if second:
                    table_columns()
                biases(G, 0)
                layer(0, G, xgT, after=lambda c: pe.wait_ge(xgt_copied, i * 2 + 1 + c // 2) if c % 2 == 0 else None)
                if second:
                    overflow_places()
                if not first:
                    pe.wait_ge(comb_banks_free, i * 4)
                biases(U, D)
                layer(1, U, xgT)
                pe.wait_ge(pick_ready, i + 2)
                gather()
                if second:
                    overflow_columns()
                for hh in range(NH):
                    pe.wait_ge(a_ready, i * 2 + hh + 1)
                    transposes(G[hh], [act_a[:, (4 * hh + n) * P:(4 * hh + n + 1) * P] for n in range(4)]) \
                        .then_inc(at_done, 1)
                    if hh == 0:
                        pe.wait_ge(pickw_ready, i + 1)
                        for t in range(NT):
                            last = nc.tensor.transpose(
                                U[0][:, t * P:(t + 1) * P],
                                pickw[:, t, :, :].rearrange("p x s -> p (x s)"), ident)
                        last.then_inc(back_done, 1)
                if second:
                    pe.wait_ge(over_ready, 1)
                layer(2, Y, aT, after=lambda c: pe.wait_ge(at_copied, i * 2 + 1 + c // 2) if c % 2 == 0 else None)
                pe.wait_ge(back_copied, i + 1)
                pe.wait_ge(xgt_copied, i * 2 + 4)
                if second:
                    pe.wait_ge(bdn_loaded, 16)
                for t in range(NT):
                    for hh in range(NH):
                        sl = slice(hh * HALF, (hh + 1) * HALF)
                        if t == 0:
                            pe.wait_ge(y_copied[hh], i + 1)
                        last = mm((M, U)[t][hh][:, :], back[:, t * P:(t + 1) * P], y_sb[:, sl],
                                  start=True, stop=not second)
                        if second:
                            last = mm((M, U)[t][hh][:, :], rank_cols[:, 1, t * P:(t + 1) * P], b_dn[:, sl],
                                      start=False, stop=True)
                        last.then_inc(comb_done, 1)

            expert_pair(0, first=True)
            expert_pair(1, second=True)
            n_over = pe.value_load(over_i[0:1, OVER:OVER + 1], min_val=0, max_val=OVER)
            with pe.Fori(2, PAIRS) as i:
                expert_pair(i)
            with pe.If(n_over > 0):
                with pe.Fori(0, OVER // 2) as k:
                    with pe.If(k * 2 < n_over):
                        expert_pair(pe.snap(k + PAIRS))

        @block.scalar
        def _(act):
            def copy(dst, src):
                return nc.scalar.activation(dst, src, ACT.Copy)

            nc.scalar.preload_act_table(ACT.Sqrt)
            for t in range(NT):
                act.wait_ge(x_loaded[t], 16)
                nc.scalar.activation(h[:, t, :], resid[:, t, :], ACT.Square, accum_out=ssq[:, t:t + 1]) \
                    .then_inc(sq_done, 1)
                act.wait_ge(ms_ready, t + 1)
                nc.scalar.activation(rms[:, t:t + 1], ms[:, t:t + 1], ACT.Sqrt).then_inc(root_done, 1)
            def w_high(*pieces):
                for n in pieces:
                    _, raw, high, _ = piece_views(n)
                    if n == 0:
                        act.wait_ge(first_loaded, 16)
                    else:
                        act.wait_ge(*mixer_loaded(PIECES[n][0]))
                    if n >= SLOTS:
                        act.wait_ge(w_high_used, n - SLOTS + 1)
                    copy(high, raw).then_inc(w_high_ready, 1)

            for t in range(NT):
                for q in range(2):
                    act.wait_ge(ht_done, 2 * t + q + 1)
                    copy(x_high[:, 4 * q:4 * q + 4, t * P:(t + 1) * P],
                         bank[4 + 2 * t + q][:, :].rearrange("p (k s) -> p k s", k=4)).then_inc(ht_high_ready, 1)
                if t == 0:
                    w_high(0)
            w_high(1, 2, 3)
            act.wait_ge(ang_ready, 1)
            nc.scalar.activation(sin_t, ang, ACT.Sin).then_inc(sin_ready, 1)
            nc.scalar.activation(cos_t, rk, ACT.Sin).then_inc(sin_ready, 1)
            w_high(4, 5, 6, 7, 8, 9)
            for t in range(NT):
                act.wait_ge(kt_done, t + 1)
                copy(kT[:, :, :, t * P:(t + 1) * P],
                     bank[4 + t][:, :].rearrange("p (g r s) -> p g r s", g=NKV, r=2)).then_inc(kt_copied, 1)
            w_high(*range(10, 18))
            for q in range(2):
                act.wait_ge(pooled_done, 2 * q + 2)
                copy(pooledT[:, 2 * q:2 * q + 2, :],
                     bank[6 + q][:, :].rearrange("p (g s) -> p g s", g=2)).then_inc(pooled_copied, 1)
            w_high(*range(18, NP_A))
            for g in range(NG):
                act.wait_ge(mixed_done, g // 2 * 2 + 2)
                nc.scalar.activation(mixedT[:, g, :], bank[6 + g // 2][:, (g % 2) * S:(g % 2 + 1) * S],
                                     ACT.Copy, scale=pscale[:, g:g + 1]).then_inc(mixed_copied, 1)
            for q in range(4):
                t, half = q // 2, q % 2
                act.wait_ge(qt_done, q + 1)
                copy(qT[:, 4 * half:4 * half + 4, t * P:(t + 1) * P],
                     bank[4 + q][:, :].rearrange("p (k s) -> p k s", k=4)).then_inc(qt_copied, 1)

            def exps(s):
                n, hp = UNITS[s]
                act.wait_ge(max_ready, s + 1)
                keys = P * (n + 1)
                for par in range(2):
                    sl = probs[:, s % 3, par * keys:(par + 1) * keys]
                    nc.scalar.activation(sl, sl, ACT.Exp, bias=mneg[s % 2][:, par:par + 1],
                                         accum_out=sume[s % 2][:, par:par + 1])
                nc.scalar.activation(esink[s % 2], esink[s % 2], ACT.Exp).then_inc(exp_done, 1)

            def pt_copy(s):
                n, hp = UNITS[s]
                act.wait_ge(pt_done, s + 1)
                if s >= 2:
                    act.wait_ge(pv_done, s - 1)
                copy(pT[:, s % 2, 0:2 * P * (n + 1)], bank[6][:, 0:2 * P * (n + 1)]).then_inc(pt_copied, 1)

            def o_copy(s):
                n, hp = UNITS[s]
                act.wait_ge(pv_done, s + 1)
                copy(attnT[:, hp, n * P:(n + 1) * P], bank[7][:, (s % 4) * P:(s % 4 + 1) * P]).then_inc(o_copied, 1)

            def yp_copy(n):
                hh, t = n // 2, n % 2
                act.wait_ge(yp_done, n + 1)
                copy(y_pool[t][:, hh * HALF:(hh + 1) * HALF], bank[2 * hh + t][:, :]).then_inc(yp_copied, 1)

            YP_COPIES = [2, 4, 6, 8]
            for s in range(NU + 3):
                if s < NU:
                    exps(s)
                if 2 <= s < NU + 2:
                    pt_copy(s - 2)
                if s >= 3:
                    o_copy(s - 3)
                if s in YP_COPIES:
                    yp_copy(YP_COPIES.index(s))
                if s in (NU, NU + 1):
                    w_high(NP_B + 2 + s - NU)
                if s in W_STEPS:
                    w_high(NP_A + W_STEPS.index(s))
            act.wait_ge(o_copied, NU)
            for q in range(2):
                copy(a_high[:, 4 * q:4 * q + 4, :], attnT[:, 4 * q:4 * q + 4, :]).then_inc(at_high_ready, 1)
            w_high(NP_B + 4, NP_B + 5)
            for t in range(NT):
                nc.scalar.activation(zg[:, 1, t, :], zg[:, 1, t, :], ACT.Sigmoid).then_inc(gates_ready, 1)
            w_high(NP_B + 6, NP_B + 7)
            for t in range(NT):
                act.wait_ge(z_ready, NT * (NIN - 1) + t + 1)
                nc.scalar.activation(zg[:, 0, t, :], zg[:, 0, t, :], ACT.Sigmoid).then_inc(gates_ready, 1)

            def merged_high(hh):
                for t in range(NT):
                    act.wait_ge(mt_done, 2 * hh + t + 1)
                    copy(x_high[:, 4 * hh:4 * hh + 4, t * P:(t + 1) * P],
                         bank[2 * t + hh][:, :].rearrange("p (k s) -> p k s", k=4)).then_inc(mt_high_ready, 1)

            first = first_piece[WO]
            w_high(*range(first + 4, first + 11))
            merged_high(0)
            w_high(first + 11)
            merged_high(1)
            w_high(*range(first + 12, len(PIECES)))
            for t in range(NT):
                act.wait_ge(x1_ready, NT + t + 1)
                nc.scalar.activation(h[:, t, :], resid[:, t, :], ACT.Square, accum_out=ssq[:, t:t + 1]) \
                    .then_inc(sq_done, 1)
                act.wait_ge(ms_ready, NT + t + 1)
                nc.scalar.activation(rms[:, t:t + 1], ms[:, t:t + 1], ACT.Sqrt).then_inc(root_done, 1)
            for t in range(NT):
                for q in range(2):
                    act.wait_ge(h2t_done, 2 * t + q + 1)
                    copy(hT[:, 4 * q:4 * q + 4, t * P:(t + 1) * P],
                         bank[2 * t + q][:, :].rearrange("p (k s) -> p k s", k=4)).then_inc(h2t_copied, 1)
                act.wait_ge(logits_done, t + 1)
                copy(lgT[:, t, :], bank[4 + t][0:NE, 0:P]).then_inc(logits_copied, 1)
            for t in range(NT):
                act.wait_ge(top_ready, t + 1)
                nc.scalar.activation(ex[:, t, :], lg[:, t, :], ACT.Exp, bias=neg_top[:, t:t + 1]) \
                    .then_inc(rexp_done, 1)

            def copy_gathered(n):
                for q in range(2):
                    act.wait_ge(gathered, n + q)
                    copy(xgT[:, 4 * q:4 * q + 4, :],
                         M[q][:, :].rearrange("p (k s) -> p k s", k=4)).then_inc(xgt_copied, 1)

            copy_gathered(1)

            def expert_pair(i):
                for hh in range(NH):
                    act.wait_ge(gm_ready, i * 2 + hh + 1)
                    nc.scalar.activation(sg[:, hh * HALF:(hh + 1) * HALF], gm[:, hh * HALF:(hh + 1) * HALF],
                                         ACT.Sigmoid, scale=ALPHA).then_inc(sig_ready, 1)
                copy_gathered(i * 2 + 3)
                for hh in range(NH):
                    act.wait_ge(at_done, i * 2 + hh + 1)
                    copy(aT[:, 4 * hh:4 * hh + 4, :],
                         G[hh][:, :].rearrange("p (k s) -> p k s", k=4)).then_inc(at_copied, 1)
                    if hh == 0:
                        act.wait_ge(back_done, i + 1)
                        copy(back[:, :], U[0][:, 0:S]).then_inc(back_copied, 1)
                act.wait_ge(chunks_used, i * CHUNKS + CHUNKS)
                copy(y_sb[:, 0:HALF], Y[0][:, :]).then_inc(y_copied[0], 1)

            expert_pair(0)
            expert_pair(1)
            act.wait_ge(over_ready, 1)
            n_over = act.value_load(over_i[0:1, OVER:OVER + 1], min_val=0, max_val=OVER)
            with act.Fori(2, PAIRS) as i:
                expert_pair(i)
            with act.If(n_over > 0):
                with act.Fori(0, OVER // 2) as k:
                    with act.If(k * 2 < n_over):
                        expert_pair(act.snap(k + PAIRS))
            nc.scalar.preload_act_table(ACT.Sqrt)
            act.wait_ge(all_added, 1)
            nc.scalar.activation(sg[:, :], resid[:, 0, :], ACT.Square, accum_out=ssq[:, 0:1]).then_inc(fin_sq, 1)
            act.wait_ge(fin_ms, 1)
            nc.scalar.activation(rms, ms, ACT.Sqrt).then_inc(fin_root, 1)

        @block.vector
        def _(dve):
            v = nc.vector
            seq = [0]

            def link(ins):
                seq[0] += 1
                ins.then_inc(dve_seq, 1)
                dve.wait_ge(dve_seq, seq[0])

            def norm(t, n, ready):
                dve.wait_ge(sq_done, n)
                v.tensor_scalar(ms[:, t:t + 1], ssq[:, t:t + 1], 1.0 / D, EPS, ALU.mult, ALU.add) \
                    .then_inc(ms_ready, 1)
                dve.wait_ge(root_done, n)
                link(v.reciprocal(rstd[:, t:t + 1], rms[:, t:t + 1]))
                v.scalar_tensor_tensor(h[:, t, :], resid[:, t, :], rstd[:, t:t + 1], gvec[:, :],
                                       ALU.mult, ALU.mult).then_inc(ready, 1)

            def w_low(*pieces):
                for n in pieces:
                    _, raw, high, low = piece_views(n)
                    dve.wait_ge(w_high_ready, n + 1)
                    v.tensor_tensor(low, raw, high.bitcast(f32), ALU.subtract).then_inc(w_low_ready, 1)

            def low_of_bank(dst, src, high, ready):
                v.tensor_tensor(dst, src[:, :].rearrange("p (k s) -> p k s", k=4), high.bitcast(f32),
                                ALU.subtract).then_inc(ready, 1)

            dve.wait_ge(g_mix_loaded, 16)
            for t in range(NT):
                norm(t, t + 1, h_ready)
            for t in range(NT):
                for q in range(2):
                    at = (slice(None), slice(4 * q, 4 * q + 4), slice(t * P, (t + 1) * P))
                    dve.wait_ge(ht_high_ready, 2 * t + q + 1)
                    low_of_bank(x_low[at], bank[4 + 2 * t + q], x_high[at], ht_low_ready)
                if t == 0:
                    w_low(0)
            w_low(1, 2, 3)

            dve.wait_ge(small_loaded, 16 * 5)
            link(v.tensor_copy(posf, pos_i[:, :]))
            for t in range(NT):
                link(v.tensor_scalar(ang[:, t, :], cst("inv_freq"), posf[:, t:t + 1], None, ALU.mult))
            MAGIC = 12582912.0
            link(v.tensor_scalar(rk, ang, 0.15915494309189535, MAGIC, ALU.mult, ALU.add))
            link(v.tensor_scalar(rk, rk, MAGIC, None, ALU.subtract))
            for part in (6.28125, 0.0019350051879882812, 3.0199159819305583e-07):
                link(v.scalar_tensor_tensor(ang, rk, -part, ang, ALU.mult, ALU.add))
            link(v.tensor_scalar(ang, ang, 3.1415925, -3.1415925, ALU.min, ALU.max))
            link(v.tensor_scalar(rk, ang, -1.0, None, ALU.mult))
            link(v.tensor_tensor(rk, rk, ang, ALU.min))
            v.tensor_scalar(rk, rk, 1.5707963267948966, None, ALU.add).then_inc(ang_ready, 1)

            z_dst = {"kv": lambda t: zkv[:, t, :], "q0": lambda t: zq[:, t, 0:HALF], "q1": lambda t: zq[:, t, HALF:D],
                     "u": lambda t: zu[:, t, :]}
            for n, name in enumerate(("ga0", "ga1", "gb0", "gb1")):
                z_dst[name] = lambda t, n=n: zg[:, n // 2, t, (n % 2) * HALF:(n % 2 + 1) * HALF]

            def take_z(m, t):
                z = z_no(m)
                dve.wait_ge(z_done, NT * z + t + 1)
                v.tensor_tensor(z_dst[order[m]](t), bank[2 * (z % 2) + t][:, 0:width_of(m)],
                                bias_in[:, z % 3, 0:width_of(m)], ALU.add).then_inc(z_ready, 1)

            def rope(src, heads, dst, t):
                def wide(table):
                    return table[:, t, None, :].to_broadcast([P, 2 * heads, ROT])
                s4 = src.rearrange("p (a r) -> p a r", r=ROT)
                sn = tmp[:, 0:heads * DH]
                link(v.tensor_tensor(sn.rearrange("p (a r) -> p a r", r=ROT), s4, wide(sin_t), ALU.mult))
                link(v.tensor_tensor(s4, s4, wide(cos_t), ALU.mult))
                s_ = src.rearrange("p (a c r) -> p a c r", c=2, r=ROT)
                n_ = sn.rearrange("p (a c r) -> p a c r", c=2, r=ROT)
                link(v.tensor_tensor(dst[:, :, 0, :], s_[:, :, 0, :], n_[:, :, 1, :], ALU.subtract))
                return v.tensor_tensor(dst[:, :, 1, :], s_[:, :, 1, :], n_[:, :, 0, :], ALU.add)

            for t in range(NT):
                take_z(0, t)
            w_low(4, 5)
            dve.wait_ge(z_ready, NT)
            dve.wait_ge(sin_ready, 2)
            dve.wait_ge(kpad_zeroed, 1)
            for t in range(NT):
                k4 = kpad[:, t, :, :].rearrange("p (g r) (c d) -> p g r c d", g=NKV, c=2)
                link(rope(zkv[:, t, 0:KVW], NKV, k4[:, :, 0, 0, :].rearrange("p g (c r) -> p g c r", c=2), t))
                last = v.tensor_copy(k4[:, :, 1, 1, :], k4[:, :, 0, 0, :])
            last.then_inc(krot_ready, 1)
            w_low(6, 7)
            for t in range(NT):
                take_z(1, t)
            w_low(8, 9, 10, 11)
            for t in range(NT):
                take_z(2, t)
            w_low(12, 13)
            dve.wait_ge(z_ready, NT * 3)
            link(rope(zq[:, 0, :], NQ, zq[:, 0, :].rearrange("p (a c r) -> p a c r", c=2, r=ROT), 0))
            w_low(14, 15)
            for t in range(NT):
                take_z(3, t)
            w_low(16, 17)
            rope(zq[:, 1, :], NQ, zq[:, 1, :].rearrange("p (a c r) -> p a c r", c=2, r=ROT), 1) \
                .then_inc(qrot_ready, 1)
            w_low(18, 19)
            for t in range(NT):
                take_z(4, t)
            w_low(20, 21)
            for t in range(NT):
                take_z(5, t)

            def soft_a(s):
                n, hp = UNITS[s]
                keys = P * (n + 1)
                pr = probs[:, s % 3, 0:2 * keys].rearrange("p (a k) -> p a k", a=2)
                dve.wait_ge(score_done, s + 1)
                mask = cst("mask")[:, 2 * P - keys:2 * P]
                v.scalar_tensor_tensor(pr, bank[4 + s % 2][:, 0:2 * keys].rearrange("p (a k) -> p a k", a=2),
                                       DH ** -0.5, mask[:, None, :].to_broadcast([P, 2, keys]), ALU.mult, ALU.add) \
                    .then_inc(masked, 1)
                dve.wait_ge(masked, s + 1)
                link(v.tensor_reduce(mx, pr, AX.X, ALU.max))
                snk = sinks[:, 2 * hp:2 * hp + 2]
                link(v.tensor_tensor(mx, mx, snk, ALU.max))
                v.tensor_scalar(mneg[s % 2], mx, -1.0, None, ALU.mult)
                v.tensor_tensor(esink[s % 2], snk, mx, ALU.subtract).then_inc(max_ready, 1)

            def soft_b(s):
                n, hp = UNITS[s]
                keys = P * (n + 1)
                dve.wait_ge(exp_done, s + 1)
                link(v.tensor_tensor(dens, sume[s % 2], esink[s % 2], ALU.add))
                v.reciprocal(rden[s % 2], dens).then_inc(rden_ready, 1)
                dve.wait_ge(rden_ready, s + 1)
                for par in range(2):
                    sl = probs[:, s % 3, par * keys:(par + 1) * keys]
                    ins = v.tensor_scalar(sl, sl, rden[s % 2][:, par:par + 1], None, ALU.mult)
                ins.then_inc(probs_ready, 1)

            for s in range(NU):
                if s == 0:
                    soft_a(0)
                if s + 1 < NU:
                    if s >= 2:
                        dve.wait_ge(pt_done, s - 1)
                    soft_a(s + 1)
                soft_b(s)
                if s in W_STEPS:
                    w_low(NP_A + W_STEPS.index(s))
            for t in range(NT):
                take_z(POOL_UP + 1, t)
            w_low(NP_B + 2, NP_B + 3)
            for q in range(2):
                dve.wait_ge(at_high_ready, q + 1)
                v.tensor_tensor(a_low[:, 4 * q:4 * q + 4, :], attnT[:, 4 * q:4 * q + 4, :],
                                a_high[:, 4 * q:4 * q + 4, :].bitcast(f32), ALU.subtract).then_inc(at_low_ready, 1)
            w_low(NP_B + 4, NP_B + 5)

            def split_biases():
                dve.wait_ge(stage_loaded, 16 * 2 * NH)
                for q in range(BPARTS):
                    ins = v.tensor_copy(stage_part[q], stage)
                    if q < BPARTS - 1:
                        link(ins)
                        link(v.tensor_tensor(stage, stage, stage_part[q], ALU.subtract))
                ins.then_inc(parts_ready, 1)

            dve.wait_ge(yp_copied, NT * NH)
            for t in range(NT):
                dve.wait_ge(gates_ready, t + 1)
                v.tensor_tensor(pool_g[:, t, :], y_pool[t], zg[:, 1, t, :], ALU.mult).then_inc(dve_seq, 1)
                seq[0] += 1

            def add_output_bias(t):
                dve.wait_ge(gates_ready, NT + t + 1)
                link(v.tensor_tensor(zg[:, 1, t, :], zg[:, 0, t, :], b_oa, ALU.mult))
                link(v.tensor_tensor(pool_g[:, t, :], pool_g[:, t, :], zg[:, 1, t, :], ALU.add))

            def merge(hh):
                sl = slice(hh * HALF, (hh + 1) * HALF)
                for t in range(NT):
                    dve.wait_ge(ya_done, 2 * hh + t + 1)
                    link(v.tensor_tensor(zg[:, 0, t, sl], bank[4 + 2 * t + hh][:, :], zg[:, 0, t, sl], ALU.mult))
                    v.tensor_tensor(zg[:, 0, t, sl], zg[:, 0, t, sl], pool_g[:, t, sl], ALU.add) \
                        .then_inc(merged_ready, 1)

            def merged_low(hh):
                for t in range(NT):
                    at = (slice(None), slice(4 * hh, 4 * hh + 4), slice(t * P, (t + 1) * P))
                    dve.wait_ge(mt_high_ready, 2 * hh + t + 1)
                    low_of_bank(x_low[at], bank[2 * t + hh], x_high[at], mt_low_ready)

            for t in range(NT):
                take_z(POOL_UP + 2, t)
            w_low(NP_B + 6, NP_B + 7)
            first = first_piece[WO]
            w_low(first + 4, first + 5)
            dve.wait_ge(bo_loaded, 16)
            dve.wait_ge(dve_seq, seq[0])
            add_output_bias(0)
            w_low(first + 6)
            add_output_bias(1)
            merge(0)
            w_low(first + 7, first + 8, first + 9)
            merged_low(0)
            merge(1)
            w_low(first + 10, first + 11)
            merged_low(1)
            split_biases()
            w_low(first + 12, first + 13)
            w_low(first + 14, first + 15)
            dve.wait_ge(g_ffn_loaded, 16)

            def add_mixer(hh, t):
                sl = slice(hh * HALF, (hh + 1) * HALF)
                dve.wait_ge(out_proj_done, 2 * hh + t + 1)
                v.tensor_tensor(resid[:, t, sl], resid[:, t, sl], bank[4 + 2 * t + hh][:, :], ALU.add) \
                    .then_inc(x1_ready, 1)

            for t in range(NT):
                add_mixer(0, t)
            for t in range(NT):
                add_mixer(1, t)
                dve.wait_ge(x1_ready, NT + t + 1)
                norm(t, NT + t + 1, h2_ready)

            dve.wait_ge(ones_ready, 4)
            for t in range(NT):
                dve.wait_ge(lt_done, t + 1)
                link(v.tensor_tensor(lg[:, t, :], bank[6 + t][:, 0:NE], b_rt, ALU.add))
                link(v.max(v8[:, t, :], lg[:, t, :]))
                v.tensor_scalar(neg_top[:, t:t + 1], v8[:, t, 0:1], -1.0, None, ALU.mult).then_inc(top_ready, 1)
                kth = v8[:, t, TOPK - 1:TOPK]
                v.tensor_scalar(gt[:, t, :], lg[:, t, :], kth, None, ALU.is_gt)
                link(v.tensor_scalar(eq[:, t, :], lg[:, t, :], kth, None, ALU.is_equal))
                link(v.tensor_tensor_scan(pre[:, t, :], ones_row, eq[:, t, :], 0.0,
                                          ALU.mult, ALU.add))
            link(v.tensor_reduce(n_gt, gt, AX.X, ALU.add))
            link(v.tensor_scalar(need, n_gt, -1.0, float(TOPK), ALU.mult, ALU.add))
            for t in range(NT):
                link(v.scalar_tensor_tensor(pre[:, t, :], pre[:, t, :], need[:, t:t + 1], eq[:, t, :],
                                            ALU.is_le, ALU.mult))
            link(v.tensor_tensor(sel, pre, gt, ALU.add))
            v.tensor_copy(sel_bf[:, :, :], sel).then_inc(sel_ready, 1)
            dve.wait_ge(rexp_done, 2)
            link(v.tensor_tensor(ex, ex, sel, ALU.mult))
            link(v.tensor_reduce(wden, ex, AX.X, ALU.add))
            link(v.reciprocal(wrden, wden))
            v.memset(rank_tab[:, :, NE + OVER:ENTRIES], 0.0)
            v.memset(comb_tab[:, :, NE + OVER:ENTRIES], 0.0)
            v.memset(bsel_tab[:, NE + OVER:ENTRIES], 0.0)
            v.tensor_copy(bsel_tab[:, 0:NE], cst("bias_sel", BPARTS * NE))
            for t in range(NT):
                v.tensor_scalar(comb_tab[:, t, 0:NE], ex[:, t, :], wrden[:, t:t + 1], None, ALU.mult)
            dve.wait_ge(rank_done, 1)
            v.scalar_tensor_tensor(rank_tab[:, :, 0:NE], bank[5][:, 0:NT * NE].rearrange("p (t e) -> p t e", t=NT),
                                   1.0, sel, ALU.add, ALU.mult)
            v.memset(over_cum[:, 0:1], 0.0)
            for lv in range(LEVELS):
                ins = v.tensor_scalar(over_in[:, lv:lv + 1], bank[4][0:NE, 0:1], float(CAP * (lv + 1)), None,
                                      ALU.is_gt)
            ins.then_inc(tabs_ready, 1)

            slots = cst("slot_no")

            def make_pick(i):
                v.tensor_tensor(pick[:, :, :, :], slots[:, None, None, :].to_broadcast([P, NT, 2, CAP]),
                                rank_tab[:, :, bass.ds(i * 2, 2), None].to_broadcast([P, NT, 2, CAP]),
                                ALU.is_equal).then_inc(pick_ready, 1)

            def make_bsel(i):
                v.tensor_copy(bsel[:, :, :],
                              bsel_tab[:, bass.ds(i * 2, 2), None].to_broadcast([BPARTS * NE, 2, CAP])) \
                    .then_inc(bsel_ready, 1)

            dve.wait_ge(tabs_ready, 1)
            make_pick(0)
            make_bsel(0)
            v.tensor_copy(over_cum[:, 1:2], over_in[:, 0:1])
            link(v.tensor_tensor(over_cum[:, 2:3], over_in[:, 0:1], over_in[:, 1:2], ALU.add))
            link(v.tensor_reduce(over_n, over_in, AX.X, ALU.add))
            def overflow_one_hot():
                dve.wait_ge(pos_done, 1)
                link(v.tensor_copy(over_pos, bank[5][0:NE, 0:LEVELS]))
                for lv in range(LEVELS):
                    link(v.tensor_scalar(oh[:, lv, :], cst("entry_no", NE), over_pos[:, lv:lv + 1],
                                         over_in[:, lv:lv + 1], ALU.is_equal, ALU.mult))
                link(v.tensor_tensor(over_sel, oh[:, 0, :], oh[:, 1, :], ALU.add))
                link(v.tensor_tensor(over_sel, over_sel, oh[:, 2, :], ALU.add))
                link(v.tensor_scalar(over_shift, oh[:, 0, :], -float(CAP), None, ALU.mult))
                for lv in range(1, LEVELS):
                    link(v.scalar_tensor_tensor(over_shift, oh[:, lv, :], -float(CAP * (lv + 1)), over_shift,
                                                ALU.mult, ALU.add))
                for q in range(BPARTS):
                    v.tensor_copy(bsel_tab[q * NE:(q + 1) * NE, NE:NE + OVER], over_sel)
                v.tensor_copy(over_i[:, OVER:OVER + 1], bank[5][0:1, 32:33]).then_inc(oh_ready, 1)

            def overflow_tables():
                dve.wait_ge(over_done, 1)
                tab = bank[5][:, 64:64 + NT * OVER].rearrange("p (t o) -> p t o", t=NT)
                v.tensor_copy(rank_tab[:, :, NE:NE + OVER], tab)
                tab = bank[5][:, 128:128 + NT * OVER].rearrange("p (t o) -> p t o", t=NT)
                v.tensor_copy(comb_tab[:, :, NE:NE + OVER], tab)
                v.tensor_copy(over_i[:, 0:OVER], bank[5][0:1, 192:192 + OVER]).then_inc(over_ready, 1)

            def expert_pair(i, second=False):
                if second:
                    dve.wait_ge(cols_done, 1)
                    v.tensor_copy(rank_cols[:, :, :], bank[4][0:NE, :].rearrange("p (q s) -> p q s", q=2)) \
                        .then_inc(cols_ready, 1)
                dve.wait_ge(pick_ready, i + 1)
                v.tensor_tensor(pickw[:, :, :, :], pick[:, :, :, :],
                                comb_tab[:, :, bass.ds(i * 2, 2), None].to_broadcast([P, NT, 2, CAP]),
                                ALU.mult).then_inc(pickw_ready, 1)
                dve.wait_ge(pickw_ready, i + 1)
                dve.wait_ge(gathered, i * 2 + 2)
                make_pick(i + 1)
                dve.wait_ge(chunks_used, i * CHUNKS + 8)
                for hh in range(NH):
                    v.tensor_scalar(gm[:, hh * HALF:(hh + 1) * HALF], G[hh][:, :], LIMIT, None, ALU.min) \
                        .then_inc(gm_ready, 1)
                if second:
                    overflow_one_hot()
                dve.wait_ge(chunks_used, i * CHUNKS + 16)
                for hh in range(NH):
                    sl = slice(hh * HALF, (hh + 1) * HALF)
                    v.tensor_scalar(um[:, sl], U[hh][:, :], LIMIT, -LIMIT, ALU.min, ALU.max).then_inc(um_ready, 1)
                    dve.wait_ge(um_ready, i * 2 + hh + 1)
                    v.scalar_tensor_tensor(um[:, sl], um[:, sl], 1.0, gm[:, sl], ALU.add, ALU.mult) \
                        .then_inc(prod_ready, 1)
                    dve.wait_ge(prod_ready, i * 2 + hh + 1)
                    dve.wait_ge(sig_ready, i * 2 + hh + 1)
                    v.tensor_tensor(act_a[:, sl], um[:, sl], sg[:, sl], ALU.mult).then_inc(a_ready, 1)
                make_bsel(i + 1)
                if second:
                    overflow_tables()
                dve.wait_ge(chunks_used, i * CHUNKS + CHUNKS)
                v.tensor_copy(y_sb[:, HALF:D], Y[1][:, :]).then_inc(y_copied[1], 1)
                for n in range(4):
                    t, hh = n // 2, n % 2
                    sl = slice(hh * HALF, (hh + 1) * HALF)
                    dve.wait_ge(comb_done, i * 4 + n + 1)
                    v.tensor_tensor(resid[:, t, sl], resid[:, t, sl], (M, U)[t][hh][:, :], ALU.add) \
                        .then_inc(comb_banks_free, 1)

            expert_pair(0)
            expert_pair(1, second=True)
            dve.wait_ge(over_ready, 1)
            n_over = dve.value_load(over_i[0:1, OVER:OVER + 1], min_val=0, max_val=OVER)
            with dve.Fori(2, PAIRS) as i:
                expert_pair(i)
            with dve.If(n_over > 0):
                with dve.Fori(0, OVER // 2) as k:
                    with dve.If(k * 2 < n_over):
                        expert_pair(dve.snap(k + PAIRS))

            dve.wait_ge(g_final_loaded, 16)
            v.engine_nop().then_inc(all_added, 1)
            dve.wait_ge(all_added, 1)
            link(v.scalar_tensor_tensor(um[:, :], resid[:, 1, :], 1.0, resid[:, 1, :], ALU.mult, ALU.mult,
                                        accum_out=ssq[:, 1:2]))
            dve.wait_ge(fin_sq, 1)
            v.tensor_scalar(ms, ssq, 1.0 / D, EPS, ALU.mult, ALU.add).then_inc(fin_ms, 1)
            dve.wait_ge(fin_root, 1)
            link(v.reciprocal(rstd, rms))
            for t in range(NT):
                for hh in range(NH):
                    sl = slice(hh * HALF, (hh + 1) * HALF)
                    v.scalar_tensor_tensor(h[:, t, sl], resid[:, t, sl], rstd[:, t:t + 1], gvec[:, sl],
                                           ALU.mult, ALU.mult).then_inc(fin_ready, 1)

        @block.gpsimd
        def _(pool):
            g = nc.gpsimd
            g.memset(kpad[:, :, :, :], 0.0).then_inc(kpad_zeroed, 1)
            g.memset(ones_f[:, :], 1.0).then_inc(ones_ready, 1)
            g.memset(ones_bf[:, :], 1.0).then_inc(ones_ready, 1)
            g.memset(ones_row, 1.0).then_inc(ones_ready, 1)
            pool.wait_ge(small_loaded, 16 * 5)
            g.tensor_copy(upper_bf[:, :], cst("upper")).then_inc(ones_ready, 1)
            pool.wait_ge(h_ready, NT)
            pool.dma_start(gvec[:, :], norm_ffn_g.to_broadcast([P, D])).then_inc(g_ffn_loaded, 16)
            pool.wait_ge(qrot_ready, 1)
            pool.dma_start(b_oa, b_o_attn.to_broadcast([P, D])).then_inc(bo_loaded, 16)
            pool.wait_ge(o_copied, NU)
            pool.dma_start(b_dn, b_down[0]).then_inc(bdn_loaded, 16)
            for n, b in enumerate((b_gate, b_up)):
                for hh in range(NH):
                    j = n * NH + hh
                    pool.dma_start(stage[j * NE:(j + 1) * NE, :], b[0, :, hh * HALF:(hh + 1) * HALF]) \
                        .then_inc(stage_loaded, 16)
            pool.wait_ge(parts_ready, 1)
            for q in range(BPARTS):
                for j in range(2 * NH):
                    pool.dma_start(bias3[q * NE:(q + 1) * NE, j * HALF:(j + 1) * HALF],
                                   stage_part[q][j * NE:(j + 1) * NE, :]).then_inc(bias3_ready, 16)
            pool.wait_ge(h2_ready, NT)
            pool.dma_start(gvec[:, :], norm_final_g.rearrange("(a d) -> a d", a=1).to_broadcast([P, D])) \
                .then_inc(g_final_loaded, 16)


_INS = ["x", "positions", "norm_mix_g", "w_in", "b_in", "attn_sinks", "w_o_attn", "b_o_attn", "w_pool_mix",
        "pool_scale", "w_pool_up", "w_out", "norm_ffn_g", "w_router", "b_router", "w_gate", "b_gate", "w_up",
        "b_up", "w_down", "b_down", "norm_final_g"]
_OUTS = [((1, S, D), "float32")]


def shape_constants():
    import numpy as np

    def at(name):
        a, b = CONST_COLS[name]
        return slice(a, b)

    c = np.zeros((P, CONST_W), np.float32)
    r = np.arange(P)
    c[:, at("ident")] = np.eye(P)
    key = np.arange(2 * P)[None, :]
    dist = r[:, None] + P - key
    c[:, at("mask")] = np.where((dist >= 0) & (dist < P), 0.0, -1e30)
    band = np.zeros((P, NG, 3 * P))
    for g, w in enumerate(WINDOWS):
        for blk, (src, t0) in enumerate(((0, 0), (0, P), (P, P))):
            s_tok = src + r[:, None]
            tok = t0 + r[None, :]
            inside = (tok >= s_tok) & (tok - s_tok < w)
            band[:, g, blk * P:(blk + 1) * P] = inside / np.minimum(tok + 1, w) - (tok == s_tok)
    c[:, at("band")] = band.reshape(P, -1)
    c[:, at("upper")] = r[:, None] < r[None, :]
    c[:, at("slot_no")] = np.arange(1, CAP + 1)
    c[:BPARTS * NE, at("bias_sel")] = (np.arange(BPARTS * NE)[:, None] % NE) == np.arange(NE)
    c[:, at("entry_no")] = np.arange(OVER)
    c[:NE, at("upper32")] = np.arange(NE)[:, None] < np.arange(NE)[None, :]
    c[:NE, at("expert_no")] = np.arange(NE)[:, None]
    c[:, at("inv_freq")] = 10000.0 ** (-np.arange(0, DH, 2) / DH)
    return c


def kernel(**inputs):
    import numpy as _np
    import concourse.bacc as _bacc
    from concourse import mybir as _mybir
    from concourse.bass_utils import run_bass_kernel_spmd as _run

    nc = _bacc.Bacc("TRN2", target_bir_lowering=False, num_devices=1)
    arrays, args = {}, []
    given = {name: inputs[name] for name in _INS}
    given["consts"] = shape_constants()
    for name, a in given.items():
        a = _np.ascontiguousarray(a)
        arrays[f"in_{name}_dram"] = a
        args.append(nc.dram_tensor(f"in_{name}_dram", a.shape, _mybir.dt.from_np(a.dtype), kind="ExternalInput").ap())
    for i, (shape, dtype) in enumerate(_OUTS):
        dt = _mybir.dt.from_np(_np.dtype(dtype))
        args.append(nc.dram_tensor(f"out_{i}_dram", shape, dt, kind="ExternalOutput").ap())
    hybrid_block(nc, *args)
    r = _run(nc, [arrays], core_ids=[0])
    return _np.asarray(r.results[0]["out_0_dram"])
```
